# Optimizing a Trainium2 kernel written in Bass

```python
import math
import jax, jax.numpy as jnp
from jax import lax
import numpy as np
import jax
import jax.numpy as jnp

D_MODEL = 1024
BATCH = 1
SEQ = 512
DEPTH = 2

N_META = 16
Q_BLOCK = 128
GROUP_HEAD_DIM = 64
D_MIX = D_MODEL
ATTN_HEADS = 8
ATTN_HEAD_DIM = 64
D_ATTN = ATTN_HEADS * ATTN_HEAD_DIM
D_CONV = D_MIX // 4
D_SC = D_MIX - D_ATTN - D_CONV
CONV_KERNEL = 31
SC_KERNEL = 3
D_FF = 2816
FFN_KERNEL = 3
RMS_EPS = 1e-6
LN_EPS = 1e-5
IN_SPLITS = (D_ATTN, D_ATTN, D_ATTN, ATTN_HEADS,
             D_CONV, D_CONV,
             D_SC, D_SC, D_SC)
D_IN = sum(IN_SPLITS)
NEG_INF = -1e30


def rms_norm(x, g):
    xf = x.astype(jnp.float32)
    y = xf * lax.rsqrt(jnp.mean(xf * xf, axis=-1, keepdims=True) + RMS_EPS)
    return (y * g.astype(jnp.float32)).astype(x.dtype)

def head_rms_norm(y, g):
    b, l, d = y.shape
    yf = y.astype(jnp.float32).reshape(b, l, d // GROUP_HEAD_DIM, GROUP_HEAD_DIM)
    yf = yf * lax.rsqrt(jnp.mean(yf * yf, axis=-1, keepdims=True) + RMS_EPS)
    return (yf.reshape(b, l, d) * g.astype(jnp.float32)).astype(y.dtype)

def layer_norm(x, g, b):
    xf = x.astype(jnp.float32)
    mu = jnp.mean(xf, axis=-1, keepdims=True)
    var = jnp.mean(jnp.square(xf - mu), axis=-1, keepdims=True)
    y = (xf - mu) * lax.rsqrt(var + LN_EPS)
    return (y * g.astype(jnp.float32) + b.astype(jnp.float32)).astype(x.dtype)

def causal_depthwise_conv(x, w):
    k, c = w.shape
    return lax.conv_general_dilated(
        x, w[:, None, :].astype(x.dtype), window_strides=(1,),
        padding=[(k - 1, 0)], dimension_numbers=("NWC", "WIO", "NWC"),
        feature_group_count=c)

def forgetting_attention(q, k, v, log_f):
    L = q.shape[1]
    scale = ATTN_HEAD_DIM ** -0.5
    F = jnp.cumsum(log_f, axis=1).transpose(0, 2, 1)

    def attend(start, end):
        qb = q[:, start:end]
        s = jnp.einsum("bqhd,bkhd->bhqk", qb, k[:, :end],
                       preferred_element_type=jnp.float32) * scale
        s = s + F[:, :, start:end, None] - F[:, :, None, :end]
        mask = jnp.arange(start, end)[:, None] >= jnp.arange(end)[None, :]
        s = jnp.where(mask, s, NEG_INF)
        p = jax.nn.softmax(s, axis=-1)
        return jnp.einsum("bhqk,bkhd->bqhd", p.astype(v.dtype), v[:, :end])

    outs = [attend(0, N_META)]
    for i in range((L - N_META) // Q_BLOCK):
        start = N_META + i * Q_BLOCK
        outs.append(attend(start, start + Q_BLOCK))
    return jnp.concatenate(outs, axis=1)

def mixer_sublayer(h, pre_g, post_g, w_in, b_forget, a_dw_w, a_dw_b, a_ln_g,
                   a_ln_b, a_pw_w, sc_conv_w, head_g, w_out):
    bsz, L, _ = h.shape
    u = rms_norm(h, pre_g)
    z = jnp.einsum("bld,de->ble", u, w_in)
    idx = np.cumsum(IN_SPLITS)[:-1].tolist()
    q, k, v, f_logit, a_val, a_gate, sc_b, sc_c, sc_x = jnp.split(z, idx, axis=-1)

    log_f = jax.nn.log_sigmoid((f_logit + b_forget).astype(jnp.float32))
    hs = (bsz, L, ATTN_HEADS, ATTN_HEAD_DIM)
    y_attn = forgetting_attention(q.reshape(hs), k.reshape(hs), v.reshape(hs), log_f)
    y_attn = y_attn.reshape(bsz, L, D_ATTN)

    a = a_val * jax.nn.sigmoid(a_gate)
    a = causal_depthwise_conv(a, a_dw_w) + a_dw_b
    a = jax.nn.silu(layer_norm(a, a_ln_g, a_ln_b))
    y_conv = jnp.einsum("blc,ce->ble", a, a_pw_w)

    y_sc = sc_b * causal_depthwise_conv(sc_c * sc_x, sc_conv_w)

    y = jnp.concatenate([y_attn, y_conv, y_sc], axis=-1)
    y = jnp.einsum("ble,ed->bld", head_rms_norm(y, head_g), w_out)
    return h + rms_norm(y, post_g)

def ffn_sublayer(h, pre_g, post_g, w_up, conv_w, w_down):
    u = rms_norm(h, pre_g)
    z = jnp.einsum("bld,df->blf", u, w_up)
    z = causal_depthwise_conv(z, conv_w)
    g, up = jnp.split(z, 2, axis=-1)
    y = jnp.einsum("blf,fd->bld", jax.nn.silu(g) * up, w_down)
    return h + rms_norm(y, post_g)

def first_inputs(seed: int = 0) -> dict:
    key = jax.random.key(seed)
    ks = jax.random.split(key, 20)
    f32 = jnp.float32

    def nrm(k, shape, scale):
        return jax.random.normal(k, shape, f32) * scale

    def gain(k, shape):
        return 1.0 + 0.05 * jax.random.normal(k, shape, f32)

    x = jax.random.normal(ks[0], (BATCH, SEQ, D_MODEL), f32)
    meta_tokens = nrm(ks[1], (N_META, D_MODEL), 1.0)
    col_scale = np.ones((D_IN,), np.float32)
    f0 = 3 * D_ATTN
    col_scale[f0:f0 + ATTN_HEADS] = 0.1
    w_in = nrm(ks[2], (DEPTH, D_MODEL, D_IN), D_MODEL ** -0.5) * jnp.asarray(col_scale)
    b_forget = jax.random.uniform(ks[3], (DEPTH, ATTN_HEADS), f32, 3.0, 6.0)
    return {
        "x": x,
        "meta_tokens": meta_tokens,
        "mix_pre_g": gain(ks[4], (DEPTH, D_MODEL)),
        "mix_post_g": gain(ks[5], (DEPTH, D_MODEL)),
        "w_in": w_in,
        "b_forget": b_forget,
        "a_dw_w": nrm(ks[6], (DEPTH, CONV_KERNEL, D_CONV), CONV_KERNEL ** -0.5),
        "a_dw_b": nrm(ks[7], (DEPTH, D_CONV), 0.02),
        "a_ln_g": gain(ks[8], (DEPTH, D_CONV)),
        "a_ln_b": nrm(ks[9], (DEPTH, D_CONV), 0.02),
        "a_pw_w": nrm(ks[10], (DEPTH, D_CONV, D_CONV), D_CONV ** -0.5),
        "sc_conv_w": nrm(ks[11], (DEPTH, SC_KERNEL, D_SC), SC_KERNEL ** -0.5),
        "head_g": gain(ks[12], (DEPTH, D_MIX)),
        "w_out": nrm(ks[13], (DEPTH, D_MIX, D_MODEL), D_MIX ** -0.5),
        "ffn_pre_g": gain(ks[14], (DEPTH, D_MODEL)),
        "ffn_post_g": gain(ks[15], (DEPTH, D_MODEL)),
        "ffn_w_up": nrm(ks[16], (DEPTH, D_MODEL, 2 * D_FF), D_MODEL ** -0.5),
        "ffn_conv_w": nrm(ks[17], (DEPTH, FFN_KERNEL, 2 * D_FF), FFN_KERNEL ** -0.5),
        "ffn_w_down": nrm(ks[18], (DEPTH, D_FF, D_MODEL), D_FF ** -0.5),
    }

def first_block(x, meta_tokens, mix_pre_g, mix_post_g, w_in, b_forget, a_dw_w,
              a_dw_b, a_ln_g, a_ln_b, a_pw_w, sc_conv_w, head_g, w_out,
              ffn_pre_g, ffn_post_g, ffn_w_up, ffn_conv_w, ffn_w_down):
    bsz = x.shape[0]
    meta = jnp.broadcast_to(meta_tokens[None].astype(x.dtype), (bsz, N_META, x.shape[-1]))
    h = jnp.concatenate([meta, x], axis=1)
    for l in range(DEPTH):
        h = mixer_sublayer(h, mix_pre_g[l], mix_post_g[l], w_in[l], b_forget[l],
                           a_dw_w[l], a_dw_b[l], a_ln_g[l], a_ln_b[l], a_pw_w[l],
                           sc_conv_w[l], head_g[l], w_out[l])
        h = ffn_sublayer(h, ffn_pre_g[l], ffn_post_g[l], ffn_w_up[l],
                         ffn_conv_w[l], ffn_w_down[l])
    return h[:, N_META:]


HEAD_DIM = 64
N_HEADS = D_MODEL // HEAD_DIM
N_MIXERS = 4
GROUP_HEADS = N_HEADS // N_MIXERS
GROUP_WIDTH = GROUP_HEADS * HEAD_DIM
D_FF_2 = 4 * D_MODEL
NORM_EPS = 1e-6
NEG_INF_2 = -1e30
FORCE = 1e30
TINY = 1e-30
N_BUCKETS = 32
MAX_DISTANCE = 128
N_BIAS_HEADS = 3 * GROUP_HEADS
MOBA_BLOCK = 256
MOBA_TOPK = 3
MOBA_Q_CHUNK = 64
NSA_KV_DIM = HEAD_DIM
CMP_LEN = 32
CMP_STRIDE = 16
CMP_HIDDEN = 256
SLC_LEN = 64
SLC_TOPN = 4
WINDOW = 512
DIFF_HALF = HEAD_DIM // 2
SPLIT_SIZES = ((GROUP_WIDTH,) * 3
               + (GROUP_WIDTH,) * 3
               + (GROUP_WIDTH,)
               + (NSA_KV_DIM,) * 6
               + (3 * GROUP_HEADS,)
               + (GROUP_WIDTH,) * 3)
D_IN_2 = sum(SPLIT_SIZES)


def _rmsnorm(x, g):
    xf = x.astype(jnp.float32)
    y = xf * lax.rsqrt(jnp.mean(xf * xf, axis=-1, keepdims=True) + NORM_EPS)
    return (y * g.astype(jnp.float32)).astype(x.dtype)

def _masked_softmax(logits, mask):
    s = jnp.where(mask, logits, NEG_INF_2)
    m = jnp.max(s, axis=-1, keepdims=True)
    e = jnp.where(mask, jnp.exp(s - m), 0.0)
    return e / jnp.maximum(jnp.sum(e, axis=-1, keepdims=True), TINY)

def _t5_bucket(dist):
    n = jnp.maximum(dist, 0)
    max_exact = N_BUCKETS // 2
    nf = jnp.maximum(n, 1).astype(jnp.float32)
    large = max_exact + (jnp.log(nf / max_exact) / math.log(MAX_DISTANCE / max_exact)
                         * (N_BUCKETS - max_exact)).astype(jnp.int32)
    large = jnp.minimum(large, N_BUCKETS - 1)
    return jnp.where(n < max_exact, n, large)

def _rel_bias(dist, table):
    return jnp.moveaxis(table[_t5_bucket(dist)], -1, 0).astype(jnp.float32)

def _rel_bias_per_head(dist, table):
    h = table.shape[1]
    h_idx = jnp.arange(h).reshape((1, h) + (1,) * (dist.ndim - 2))
    return table.T[h_idx, _t5_bucket(dist)].astype(jnp.float32)

def _heads(t, n_heads):
    b, s, _ = t.shape
    return t.reshape(b, s, n_heads, -1).transpose(0, 2, 1, 3)

def _merge_heads(t):
    b, h, s, d = t.shape
    return t.transpose(0, 2, 1, 3).reshape(b, s, h * d)

def _q_blocks(t, block):
    b, h, s = t.shape[:3]
    t = t.reshape((b, h, s // block, block) + t.shape[3:])
    return jnp.moveaxis(t, 2, 0)

def _unblock(t):
    t = jnp.moveaxis(t, 0, 2)
    b, h, n, blk = t.shape[:4]
    return t.reshape((b, h, n * blk) + t.shape[4:])

def stick_breaking_attention(q, k, v):
    b, h, s, d = q.shape
    scale = d ** -0.5
    kpos = jnp.arange(s)

    def one_block(args):
        qb, i = args
        qpos = i * Q_BLOCK + jnp.arange(Q_BLOCK)
        z = jnp.einsum('bhqd,bhkd->bhqk', qb, k).astype(jnp.float32) * scale
        mask = kpos[None, :] < qpos[:, None]
        log_keep = jnp.where(mask, -jax.nn.softplus(z), 0.0)
        suffix = lax.cumsum(log_keep, axis=3, reverse=True) - log_keep
        a = jnp.where(mask, jnp.exp(jax.nn.log_sigmoid(z) + suffix), 0.0)
        return jnp.einsum('bhqk,bhkd->bhqd', a.astype(v.dtype), v)

    out = lax.map(one_block, (_q_blocks(q, Q_BLOCK), jnp.arange(s // Q_BLOCK)))
    return _unblock(out)

def moba_attention(q, k, v, table):
    b, h, s, d = q.shape
    scale = d ** -0.5
    n_blk = -(-s // MOBA_BLOCK)
    pad = n_blk * MOBA_BLOCK - s
    k_blk = jnp.pad(k, ((0, 0), (0, 0), (0, pad), (0, 0))).reshape(b, h, n_blk, MOBA_BLOCK, d)
    v_blk = jnp.pad(v, ((0, 0), (0, 0), (0, pad), (0, 0))).reshape(b, h, n_blk, MOBA_BLOCK, d)
    k_mean = jnp.mean(k_blk.astype(jnp.float32), axis=3)
    n_sel = min(MOBA_TOPK, n_blk - 1)
    blk_ids = jnp.arange(n_blk)
    in_blk = jnp.arange(MOBA_BLOCK)
    b_idx = jnp.arange(b)[:, None, None, None]
    h_idx = jnp.arange(h)[None, :, None, None]

    def one_chunk(args):
        qc, i = args
        qpos = i * MOBA_Q_CHUNK + jnp.arange(MOBA_Q_CHUNK)
        own = (i * MOBA_Q_CHUNK) // MOBA_BLOCK
        k_own = lax.dynamic_index_in_dim(k_blk, own, axis=2, keepdims=False)
        v_own = lax.dynamic_index_in_dim(v_blk, own, axis=2, keepdims=False)
        dist_own = qpos[:, None] - (own * MOBA_BLOCK + in_blk)[None, :]
        s_own = (jnp.einsum('bhqd,bhkd->bhqk', qc, k_own).astype(jnp.float32) * scale
                 + _rel_bias(dist_own, table)[None])
        m_own = jnp.broadcast_to(dist_own >= 0, s_own.shape)
        if n_sel == 0:
            p = _masked_softmax(s_own, m_own)
            return jnp.einsum('bhqk,bhkd->bhqd', p.astype(v.dtype), v_own)
        gate = jnp.einsum('bhqd,bhnd->bhqn', qc.astype(jnp.float32), k_mean)
        gate = jnp.where(blk_ids < own, gate, NEG_INF_2)
        _, sel = lax.top_k(gate, n_sel)
        k_sel = k_blk[b_idx, h_idx, sel]
        v_sel = v_blk[b_idx, h_idx, sel]
        sel_pos = sel[..., None] * MOBA_BLOCK + in_blk
        dist_sel = qpos[:, None, None] - sel_pos
        s_sel = (jnp.einsum('bhqd,bhqnkd->bhqnk', qc, k_sel).astype(jnp.float32) * scale
                 + _rel_bias_per_head(dist_sel, table))
        m_sel = jnp.broadcast_to((sel < own)[..., None], s_sel.shape)
        n_flat = n_sel * MOBA_BLOCK
        s_all = jnp.concatenate([s_sel.reshape(b, h, MOBA_Q_CHUNK, n_flat), s_own], axis=-1)
        m_all = jnp.concatenate([m_sel.reshape(b, h, MOBA_Q_CHUNK, n_flat), m_own], axis=-1)
        p = _masked_softmax(s_all, m_all)
        p_sel = p[..., :n_flat].reshape(s_sel.shape)
        p_own = p[..., n_flat:]
        return (jnp.einsum('bhqnk,bhqnkd->bhqd', p_sel.astype(v.dtype), v_sel)
                + jnp.einsum('bhqk,bhkd->bhqd', p_own.astype(v.dtype), v_own))

    out = lax.map(one_chunk, (_q_blocks(q, MOBA_Q_CHUNK), jnp.arange(s // MOBA_Q_CHUNK)))
    return _unblock(out)

def nsa_attention(q, k_c, v_c, k_s, v_s, k_w, v_w, gates, pos_k, pos_v, wk1, wk2, wv1, wv2, table):
    b, h, s, d = q.shape
    scale = d ** -0.5
    tpos = jnp.arange(s)
    n_cmp = (s - CMP_LEN) // CMP_STRIDE + 1
    cmp_idx = np.arange(n_cmp)[:, None] * CMP_STRIDE + np.arange(CMP_LEN)[None, :]
    cmp_end = jnp.asarray(cmp_idx[:, -1])

    def compress(t, pos, w1, w2):
        blocks = t[:, cmp_idx] + pos
        return jax.nn.gelu(blocks.reshape(b, n_cmp, CMP_LEN * d) @ w1) @ w2

    kc = compress(k_c, pos_k, wk1, wk2)
    vc = compress(v_c, pos_v, wv1, wv2)
    dist_c = tpos[:, None] - cmp_end[None, :]
    s_c = (jnp.einsum('bhtd,bcd->bhtc', q, kc).astype(jnp.float32) * scale
           + _rel_bias(dist_c, table)[None])
    p_c = _masked_softmax(s_c, dist_c >= 0)
    o_cmp = jnp.einsum('bhtc,bcd->bhtd', p_c.astype(vc.dtype), vc)
    n_slc = s // SLC_LEN
    n_top = min(SLC_TOPN, n_slc)
    s_start = np.arange(n_slc) * SLC_LEN
    cover = np.clip(np.minimum(cmp_idx[:, -1][:, None], (s_start + SLC_LEN - 1)[None, :])
                    - np.maximum(cmp_idx[:, 0][:, None], s_start[None, :]) + 1, 0, None) / CMP_LEN
    importance = jnp.einsum('btc,cj->btj', jnp.sum(p_c, axis=1), jnp.asarray(cover, jnp.float32))
    own = tpos // SLC_LEN
    blk = jnp.arange(n_slc)
    imp = jnp.where(blk[None, :] == own[:, None], FORCE,
                    jnp.where(blk[None, :] < own[:, None], importance, NEG_INF_2))
    _, sel = lax.top_k(imp, n_top)
    n_qb = s // Q_BLOCK
    sel_b = sel.reshape(b, n_qb, Q_BLOCK, n_top).transpose(1, 0, 2, 3)
    ks_blk = k_s.reshape(b, n_slc, SLC_LEN, d)
    vs_blk = v_s.reshape(b, n_slc, SLC_LEN, d)
    kw_pad = jnp.pad(k_w, ((0, 0), (WINDOW, 0), (0, 0)))
    vw_pad = jnp.pad(v_w, ((0, 0), (WINDOW, 0), (0, 0)))
    b_idx = jnp.arange(b)[:, None, None]
    in_slc = jnp.arange(SLC_LEN)
    in_win = jnp.arange(WINDOW + Q_BLOCK)

    def one_block(args):
        qb, selc, i = args
        qpos = i * Q_BLOCK + jnp.arange(Q_BLOCK)
        k_sel = ks_blk[b_idx, selc]
        v_sel = vs_blk[b_idx, selc]
        dist_s = qpos[:, None, None] - (selc[..., None] * SLC_LEN + in_slc)
        s_s = (jnp.einsum('bhqd,bqnkd->bhqnk', qb, k_sel).astype(jnp.float32) * scale
               + jnp.moveaxis(table[_t5_bucket(dist_s)], -1, 1).astype(jnp.float32))
        m_s = jnp.broadcast_to((dist_s >= 0)[:, None], s_s.shape)
        flat = (b, h, Q_BLOCK, n_top * SLC_LEN)
        p_s = _masked_softmax(s_s.reshape(flat), m_s.reshape(flat)).reshape(s_s.shape)
        o_s = jnp.einsum('bhqnk,bqnkd->bhqd', p_s.astype(v_sel.dtype), v_sel)
        kw = lax.dynamic_slice_in_dim(kw_pad, i * Q_BLOCK, WINDOW + Q_BLOCK, axis=1)
        vw = lax.dynamic_slice_in_dim(vw_pad, i * Q_BLOCK, WINDOW + Q_BLOCK, axis=1)
        kpos = i * Q_BLOCK - WINDOW + in_win
        dist_w = qpos[:, None] - kpos[None, :]
        m_w = (dist_w >= 0) & (dist_w < WINDOW) & (kpos[None, :] >= 0)
        s_w = (jnp.einsum('bhqd,bkd->bhqk', qb, kw).astype(jnp.float32) * scale
               + _rel_bias(dist_w, table)[None])
        p_w = _masked_softmax(s_w, m_w)
        o_w = jnp.einsum('bhqk,bkd->bhqd', p_w.astype(vw.dtype), vw)
        return o_s, o_w

    o_slc, o_win = lax.map(one_block, (_q_blocks(q, Q_BLOCK), sel_b, jnp.arange(n_qb)))
    o_slc, o_win = _unblock(o_slc), _unblock(o_win)
    g = jax.nn.sigmoid(gates.astype(jnp.float32)).reshape(b, s, 3, h).transpose(2, 0, 3, 1)[..., None]
    g = g.astype(q.dtype)
    return g[0] * o_cmp + g[1] * o_slc + g[2] * o_win

def diff_attention(q, k, v, lam, table):
    s = q.shape[2]
    scale = q.shape[-1] ** -0.5
    kpos = jnp.arange(s)

    def one_block(args):
        qb, i = args
        qpos = i * Q_BLOCK + jnp.arange(Q_BLOCK)
        dist = qpos[:, None] - kpos[None, :]
        sc = (jnp.einsum('bhqcd,bhkcd->bhcqk', qb, k).astype(jnp.float32) * scale
              + _rel_bias(dist, table)[None, :, None])
        p = _masked_softmax(sc, dist >= 0)
        w = p[:, :, 0] - lam * p[:, :, 1]
        return jnp.einsum('bhqk,bhkd->bhqd', w.astype(v.dtype), v)

    out = lax.map(one_block, (_q_blocks(q, Q_BLOCK), jnp.arange(s // Q_BLOCK)))
    return _unblock(out)

def second_inputs(seed: int = 0) -> dict:
    key = jax.random.key(seed)
    ks = jax.random.split(key, 17)
    f32 = jnp.float32

    def nrm(k, shape, scale):
        return jax.random.normal(k, shape, f32) * scale

    return {
        "x": nrm(ks[0], (BATCH, SEQ, D_MODEL), 1.0),
        "w_in": nrm(ks[1], (DEPTH, D_MODEL, D_IN_2), D_MODEL ** -0.5),
        "w_out": nrm(ks[2], (DEPTH, D_MODEL, D_MODEL), D_MODEL ** -0.5),
        "w_up": nrm(ks[3], (DEPTH, D_MODEL, D_FF_2), D_MODEL ** -0.5),
        "w_down": nrm(ks[4], (DEPTH, D_FF_2, D_MODEL), D_FF_2 ** -0.5),
        "norm_attn": 1.0 + nrm(ks[5], (DEPTH, D_MODEL), 0.05),
        "norm_mlp": 1.0 + nrm(ks[6], (DEPTH, D_MODEL), 0.05),
        "cmp_pos_k": nrm(ks[7], (DEPTH, CMP_LEN, HEAD_DIM), 0.1),
        "cmp_pos_v": nrm(ks[8], (DEPTH, CMP_LEN, HEAD_DIM), 0.1),
        "cmp_k_w1": nrm(ks[9], (DEPTH, CMP_LEN * HEAD_DIM, CMP_HIDDEN), (CMP_LEN * HEAD_DIM) ** -0.5),
        "cmp_k_w2": nrm(ks[10], (DEPTH, CMP_HIDDEN, HEAD_DIM), CMP_HIDDEN ** -0.5),
        "cmp_v_w1": nrm(ks[11], (DEPTH, CMP_LEN * HEAD_DIM, CMP_HIDDEN), (CMP_LEN * HEAD_DIM) ** -0.5),
        "cmp_v_w2": nrm(ks[12], (DEPTH, CMP_HIDDEN, HEAD_DIM), CMP_HIDDEN ** -0.5),
        "diff_lambda": nrm(ks[13], (DEPTH, 4, DIFF_HALF), 0.1),
        "diff_subln": 1.0 + nrm(ks[14], (DEPTH, HEAD_DIM), 0.05),
        "rel_bias": nrm(ks[15], (N_BUCKETS, N_BIAS_HEADS), 0.2),
        "final_norm": 1.0 + nrm(ks[16], (D_MODEL,), 0.05),
    }

def second_block(x, w_in, w_out, w_up, w_down, norm_attn, norm_mlp, cmp_pos_k, cmp_pos_v,
              cmp_k_w1, cmp_k_w2, cmp_v_w1, cmp_v_w2, diff_lambda, diff_subln, rel_bias, final_norm):
    bias_moba = rel_bias[:, :GROUP_HEADS]
    bias_nsa = rel_bias[:, GROUP_HEADS:2 * GROUP_HEADS]
    bias_diff = rel_bias[:, 2 * GROUP_HEADS:]
    split_at = np.cumsum(SPLIT_SIZES)[:-1].tolist()
    b, s, _ = x.shape
    for layer in range(DEPTH):
        h = _rmsnorm(x, norm_attn[layer])
        proj = h @ w_in[layer]
        (sb_q, sb_k, sb_v, mb_q, mb_k, mb_v, ns_q, ns_kc, ns_vc, ns_ks, ns_vs, ns_kw, ns_vw,
         ns_g, df_q, df_k, df_v) = jnp.split(proj, split_at, axis=-1)
        o_sb = stick_breaking_attention(_heads(sb_q, GROUP_HEADS), _heads(sb_k, GROUP_HEADS),
                                        _heads(sb_v, GROUP_HEADS))
        o_mb = moba_attention(_heads(mb_q, GROUP_HEADS), _heads(mb_k, GROUP_HEADS),
                              _heads(mb_v, GROUP_HEADS), bias_moba)
        o_ns = nsa_attention(_heads(ns_q, GROUP_HEADS), ns_kc, ns_vc, ns_ks, ns_vs, ns_kw, ns_vw, ns_g,
                             cmp_pos_k[layer], cmp_pos_v[layer], cmp_k_w1[layer], cmp_k_w2[layer],
                             cmp_v_w1[layer], cmp_v_w2[layer], bias_nsa)
        lambda_init = 0.8 - 0.6 * math.exp(-0.3 * layer)
        lv = diff_lambda[layer].astype(jnp.float32)
        lam = jnp.exp(jnp.sum(lv[0] * lv[1])) - jnp.exp(jnp.sum(lv[2] * lv[3])) + lambda_init
        dq = df_q.reshape(b, s, GROUP_HEADS, 2, DIFF_HALF).transpose(0, 2, 1, 3, 4)
        dk = df_k.reshape(b, s, GROUP_HEADS, 2, DIFF_HALF).transpose(0, 2, 1, 3, 4)
        o_df = diff_attention(dq, dk, _heads(df_v, GROUP_HEADS), lam, bias_diff)
        o_df = _rmsnorm(o_df, diff_subln[layer]) * (1.0 - lambda_init)
        mixed = jnp.concatenate([_merge_heads(o_sb), _merge_heads(o_mb),
                                 _merge_heads(o_ns), _merge_heads(o_df)], axis=-1)
        x = x + mixed @ w_out[layer]
        h2 = _rmsnorm(x, norm_mlp[layer])
        x = x + jnp.square(jax.nn.relu(h2 @ w_up[layer])) @ w_down[layer]
    return _rmsnorm(x, final_norm)


def setup_inputs(seed=0):
    out = dict(first_inputs(seed))
    for name, value in second_inputs(seed + 1).items():
        if name != "x":
            out[name + "_2"] = value
    return out


def reference(
    x, meta_tokens, mix_pre_g, mix_post_g, w_in, b_forget, a_dw_w, a_dw_b, a_ln_g, a_ln_b,
    a_pw_w, sc_conv_w, head_g, w_out, ffn_pre_g, ffn_post_g, ffn_w_up, ffn_conv_w, ffn_w_down,
    w_in_2, w_out_2, w_up_2, w_down_2, norm_attn_2, norm_mlp_2, cmp_pos_k_2, cmp_pos_v_2,
    cmp_k_w1_2, cmp_k_w2_2, cmp_v_w1_2, cmp_v_w2_2, diff_lambda_2, diff_subln_2, rel_bias_2,
    final_norm_2,
):
    x = first_block(
        x, meta_tokens, mix_pre_g, mix_post_g, w_in, b_forget, a_dw_w, a_dw_b, a_ln_g, a_ln_b,
        a_pw_w, sc_conv_w, head_g, w_out, ffn_pre_g, ffn_post_g, ffn_w_up, ffn_conv_w,
        ffn_w_down,
    )
    return second_block(
        x, w_in_2, w_out_2, w_up_2, w_down_2, norm_attn_2, norm_mlp_2, cmp_pos_k_2, cmp_pos_v_2,
        cmp_k_w1_2, cmp_k_w2_2, cmp_v_w1_2, cmp_v_w2_2, diff_lambda_2, diff_subln_2, rel_bias_2,
        final_norm_2,
    )


_drawn_inputs = setup_inputs


def setup_inputs(seed=0):
    import zlib

    import numpy as np

    out = dict(_drawn_inputs(seed))
    spreads = {}
    factors = {'a_ln_b': 3.727,
     'norm_attn_2': 2.803,
     'cmp_pos_k_2': 8.0,
     'cmp_pos_v_2': 6.96,
     'cmp_k_w1_2': 3.24,
     'cmp_k_w2_2': 3.237,
     'diff_lambda_2': 8.0,
     'diff_subln_2': 4.67}
    for name, (base, spread) in spreads.items():
        noise = np.random.default_rng([zlib.crc32(name.encode()), seed]).standard_normal(out[name].shape)
        drawn = base * np.exp(spread * noise) if base else spread * noise
        out[name] = jnp.asarray(drawn.astype(out[name].dtype))
    for name, factor in factors.items():
        out[name] = (out[name] * factor).astype(out[name].dtype)
    return out
```

```python
from contextlib import ExitStack

import numpy as np

import concourse.bass as bass
from concourse import mybir

F32 = mybir.dt.float32
ALU = mybir.AluOpType
ACT = mybir.ActivationFunctionType
AX_X = mybir.AxisListType.X

P = 128
D = 1024
KD = D // P
DEPTH = 2
SEQ, META = 512, 16
TA = SEQ + META
HALF_A = TA // 2
NEG = 1e30
DH = 64

HEADS_A = 8
TAPS_LONG, TAPS_SHORT = 31, 3
D_FF = 2816
FF_PAIRS = D_FF // P
Q_TILES_A = [(0, META)] + [(META + P * i, P) for i in range(SEQ // P)]
SLOTS_A = 54
TB = SEQ
HEADS_B = 4
Q_TILES_B = [(P * i, P) for i in range(TB // P)]
FF2 = 4096
N_CMP = 31
CMP_LEN, CMP_STRIDE, CMP_HID = 32, 16, 256
N_BUCKETS = 32
N_SLC, SLC_LEN, SLC_TOP = 8, 64, 4
TINY = 1e-30
SLOTS_B = 52
UNIT = P
SLOT = 16 * UNIT


class Signal:

    def __init__(self, sem, per_layer, step=1):
        self.sem, self.per_layer, self.step = sem, per_layer, step

    def at(self, layer, n):
        return layer * (self.per_layer * self.step) + n * self.step


def pass_waits(eng, S):
    eng.sem_inc(S["passed"], 1)


def chunks(t):
    return [(0, t)] if t <= 512 else [(0, t // 2), (t // 2, t - t // 2)]


def banks(ps, b, t):
    if t <= 512:
        return ps[:, b, 0:t]
    return ps[:, b:b + 2, 0:t // 2]


def split(ap, t):
    return ap if t <= 512 else ap.rearrange("p (c n) -> p c n", c=2)


def ring_feed(eng, ring, layer, base, done, source, then):
    tiles, full, mm_done = ring["tiles"], ring["full"], ring["mm_done"]
    count, src = source
    if count > 2:
        with eng.Fori(0, count // 2 - 1) as it:
            for s in range(2):
                eng.wait_ge(mm_done.sem, mm_done.at(layer, done(it * 2 + s)))
                w = src(it * 2 + (2 + s))
                eng.dma_start(tiles[:, s, 0:w.shape[-1]], w).then_inc(full[s], 16)
    if then is not None:
        for s in range(2):
            eng.wait_ge(mm_done.sem, mm_done.at(layer, done(count - 2 + s)))
            w = then(s)
            eng.dma_start(tiles[:, s, 0:w.shape[-1]], w).then_inc(full[s], 16)


def first_slots(eng, ring, source):
    for s in range(2):
        w = source(s)
        eng.dma_start(ring["tiles"][:, s, 0:w.shape[-1]], w).then_inc(ring["full"][s], 16)


def slot_full(ring, layer, base, j):
    return layer * (ring["per_layer"] // 2 * 16) + (j * 16 + (base // 2 + 1) * 16)


def norm_stage(nc, S, layer, use, T, x, gain, out, residual=None, first=None):
    ps, sq, rstd = S["psum"], S["scratch"], S["rstd"]
    with nc.Block() as block:
        if first is not None:
            @block.sync
            def _(sp):
                first(sp)

        @block.scalar
        def _(act):
            for k in range(KD):
                nc.scalar.activation(sq[:, k, 0:T], x[:, k, 0:T], ACT.Square).then_inc(S["squared"].sem, 1)
            act.wait_ge(S["summed"].sem, S["summed"].at(layer, use + 1))
            nc.scalar.activation(split(rstd[:, 0:T], T), banks(ps, 0, T), ACT.Sqrt,
                                 bias=S["eps6"][:, 0:1]).then_inc(S["rooted"].sem, 1)

        @block.tensor
        def _(pe):
            for k in range(KD):
                pe.wait_ge(S["squared"].sem, S["squared"].at(layer, KD * use + k + 1))
                for c, (c0, cn) in enumerate(chunks(T)):
                    last = nc.tensor.matmul(ps[:, c, 0:cn], S["mean_mat"][:, :], sq[:, k, c0:c0 + cn],
                                            start=(k == 0), stop=(k == KD - 1))
            last.then_inc(S["summed"].sem, 1)

        @block.vector
        def _(dve):
            dve.wait_ge(S["rooted"].sem, S["rooted"].at(layer, use + 1))
            nc.vector.reciprocal(rstd[:, 0:T], rstd[:, 0:T]).then_inc(S["rstd_ready"].sem, 1)
            dve.wait_ge(S["rstd_ready"].sem, S["rstd_ready"].at(layer, use + 1))
            for k in range(KD):
                nc.vector.scalar_tensor_tensor(out=out[:, k, 0:T], in0=x[:, k, 0:T], scalar=gain[:, k:k + 1],
                                               in1=rstd[:, 0:T], op0=ALU.mult,
                                               op1=ALU.mult).then_inc(S["scaled"].sem, 1)
            if residual is not None:
                for k in range(KD):
                    dve.wait_ge(S["scaled"].sem, S["scaled"].at(layer, KD * use + k + 1))
                    nc.vector.tensor_tensor(residual[:, k, 0:T], residual[:, k, 0:T], out[:, k, 0:T], ALU.add)


def linear_stage(nc, S, ring, layer, T, weights, slots, x, base, mm_base, free_base, then,
                 deep=0, evacuate="copy", out=None):
    ps, w, mm_done, free = S["psum"], ring["tiles"], ring["mm_done"], S["psum_free"]
    bufs = 2 if deep else 4
    rounds = slots // (4 if deep else 2)
    wide = 2 if T > 512 else 1
    groups = 2 if deep else 1
    slot_groups = 1 if deep else 2
    with nc.Block() as block:
        @block.sync
        def _(sp):
            ring_feed(sp, ring, layer, base, lambda j: j * slot_groups + (mm_base + slot_groups),
                      (slots, lambda j: weights[layer, j]), then)

        @block.tensor
        def _(pe):
            with pe.Fori(0, rounds) as it:
                for j in range(bufs):
                    pe.wait_ge(free.sem, free.at(layer, it * bufs + (free_base + j + 1)))
                    for s, kn in [(0, deep // 2), (1, deep // 2)] if deep else [(j // 2, KD)]:
                        if deep or j % 2 == 0:
                            pe.wait_ge(ring["full"][s],
                                       slot_full(ring, layer, base, it * 2 + j if deep else it))
                        for k in range(kn):
                            unit = k if deep else (j % 2) * KD + k
                            kx = s * kn + k if deep else k
                            for c, (c0, cn) in enumerate(chunks(T)):
                                mm = nc.tensor.matmul(ps[:, wide * j + c, 0:cn],
                                                      w[:, s, unit * UNIT:(unit + 1) * UNIT],
                                                      x[:, kx, c0:c0 + cn], start=(kx == 0),
                                                      stop=(kx == (deep or KD) - 1))
                        mm.then_inc(mm_done.sem, 1)

        def read_out(eng, op):
            eng.sem_inc(free.sem, bufs)
            with eng.Fori(0, rounds) as it:
                for j in range(bufs):
                    eng.wait_ge(mm_done.sem, mm_done.at(layer, it * (bufs * groups) + (mm_base + (j + 1) * groups)))
                    op(out[:, it * bufs + j, 0:T], banks(ps, wide * j, T)).then_inc(free.sem, 1)

        if evacuate == "add":
            @block.vector
            def _(dve):
                read_out(dve, lambda o, i: nc.vector.tensor_tensor(split(o, T), i, split(o, T), ALU.add))
        else:
            @block.scalar
            def _(act):
                func = ACT.Relu if evacuate == "relu2" else ACT.Copy
                read_out(act, lambda o, i: nc.scalar.activation(split(o, T), i, func))
        if evacuate == "relu2":
            @block.vector
            def _(dve):
                with dve.Fori(0, rounds) as it:
                    for j in range(bufs):
                        dve.wait_ge(free.sem, free.at(layer, it * bufs + (free_base + bufs + j + 1)))
                        o = out[:, it * bufs + j, 0:T]
                        nc.vector.tensor_tensor(o, o, o, ALU.mult)


def softmax_stage(nc, S, layer, C):
    ps, ident = S["psum"], S["ident"]
    N, Pb, PT, neg_max, total = S["N"], S["P"], S["PT"], S["neg_max"], S["total"]
    scores, shifted, probs = S["scores"], S["shifted"], S["probs"]
    inverted, factor = S["inverted"], S["factor"]
    turned, turned_out, mixed, stored, staged = (S[x] for x in ("turned", "turned_out", "mixed", "stored", "staged"))
    units, U, tiles = C["units"], len(C["units"]), C["q_tiles"]
    narrow = C["T"] <= 512

    def count(sig, it, u):
        return sig.at(layer, it * U + (C["base"] + u + 1))

    def score_view(u, qn, n):
        if n <= 512:
            return ps[0:qn, 2 * (u % 2), 0:n]
        return ps[0:qn, 2 * (u % 2):2 * (u % 2) + 2, 0:n // 2]

    def n_view(ap, n):
        return ap if n <= 512 else ap.rearrange("p (c n) -> p c n", c=2)

    def turned_at(u, j, sn, qn):
        if narrow:
            return ps[0:sn, 4 + u % 2, P * j:P * j + qn]
        return ps[0:sn, 5, 0:qn] if j == 0 else ps[0:sn, 4, P * (j - 1):P * (j - 1) + qn]

    def mixed_at(u, qn):
        return ps[0:qn, 6 + u % 2, 0:DH]

    with nc.Block() as block:
        @block.tensor
        def _(pe):
            def score(it, u):
                q0, qn = tiles[units[u]["i"]]
                n, _ = C["keys"](units[u]["i"])
                if u >= 2:
                    pe.wait_ge(shifted.sem, count(shifted, it, u - 2))
                if qn < P or u == 0:
                    pass_waits(pe, S)
                terms = [(C["q"](units[u], q0, qn), lambda a, b: C["k"](units[u], a, b))] + C["more"](it, units[u], q0, qn)
                for c, (c0, cn) in enumerate(chunks(n)):
                    for m, (lhs, rhs) in enumerate(terms):
                        mm = nc.tensor.matmul(ps[0:qn, 2 * (u % 2) + c, 0:cn], lhs, rhs(c0, c0 + cn),
                                              start=(m == 0), stop=(m == len(terms) - 1))
                mm.then_inc(scores.sem, 1)

            def turn(it, u):
                q0, qn = tiles[units[u]["i"]]
                _, keys = C["keys"](units[u]["i"])
                pe.wait_ge(probs.sem, count(probs, it, u))
                lag = 2 if narrow else 1
                if u >= lag:
                    pe.wait_ge(turned_out.sem, count(turned_out, it, u - lag))
                if qn < P:
                    pass_waits(pe, S)
                for j, (s0, sn) in enumerate(keys):
                    mm = nc.tensor.transpose(turned_at(u, j, sn, qn), Pb[0:qn, u % 3, s0:s0 + sn],
                                             ident[0:qn, 0:qn])
                mm.then_inc(turned.sem, 1)

            def mix(it, u):
                q0, qn = tiles[units[u]["i"]]
                _, keys = C["keys"](units[u]["i"])
                pe.wait_ge(turned_out.sem, count(turned_out, it, u))
                if u >= 2:
                    pe.wait_ge(stored.sem, count(stored, it, u - 2))
                if keys[0][1] < P:
                    pass_waits(pe, S)
                for j, (s0, sn) in enumerate(keys):
                    mm = nc.tensor.matmul(mixed_at(u, qn), PT[0:sn, u % 2, P * j:P * j + qn],
                                          C["v"](it, units[u], j, sn), start=(j == 0), stop=(j == len(keys) - 1))
                mm.then_inc(mixed.sem, 1)

            with pe.Fori(0, C["rounds"]) as it:
                pe.wait_ge(staged.sem, staged.at(layer, it + (C["stage_base"] + 1)))
                for u in range(U + 3):
                    if u < U:
                        score(it, u)
                    if 2 <= u < U + 2:
                        turn(it, u - 2)
                    if u >= 3:
                        mix(it, u - 3)
                pe.wait_ge(stored.sem, count(stored, it, U - 1))

        @block.vector
        def _(dve):
            def shift(it, u):
                q0, qn = tiles[units[u]["i"]]
                n, _ = C["keys"](units[u]["i"])
                if u >= 2:
                    dve.wait_ge(probs.sem, count(probs, it, u - 2))
                dve.wait_ge(scores.sem, count(scores, it, u))
                pass_waits(dve, S)
                nc.vector.tensor_tensor_reduce(n_view(N[0:qn, u % 2, 0:n], n), score_view(u, qn, n),
                                               n_view(C["bias"](units[u], qn, n), n), 1.0, 3e38, ALU.add,
                                               ALU.min, neg_max[0:qn, u % 4:u % 4 + 1]).then_inc(shifted.sem, 1)

            def invert(it, u):
                q0, qn = tiles[units[u]["i"]]
                dve.wait_ge(probs.sem, count(probs, it, u))
                C["invert"](dve, it, units[u], u, qn, factor[0:qn, u % 4:u % 4 + 1],
                            total[0:qn, u % 6:u % 6 + 1])

            with dve.Fori(0, C["rounds"]) as it:
                C["stage"](it).then_inc(staged.sem, 1)
                for u in range(U + 4):
                    if 3 <= u < U + 3:
                        invert(it, u - 3)
                    if u < U:
                        shift(it, u)
                    if u >= 4:
                        q0, qn = tiles[units[u - 4]["i"]]
                        dve.wait_ge(mixed.sem, count(mixed, it, u - 4))
                        dve.wait_ge(inverted.sem, count(inverted, it, u - 4))
                        C["finish"](dve, it, units[u - 4], u - 4, q0, qn, mixed_at(u - 4, qn),
                                    factor[0:qn, (u - 4) % 4:(u - 4) % 4 + 1]).then_inc(stored.sem, 1)

        @block.scalar
        def _(act):
            def exponent(it, u):
                q0, qn = tiles[units[u]["i"]]
                n, _ = C["keys"](units[u]["i"])
                if u >= 3:
                    act.wait_ge(turned.sem, count(turned, it, u - 3))
                if u >= 6:
                    act.wait_ge(stored.sem, count(stored, it, u - 6))
                act.wait_ge(shifted.sem, count(shifted, it, u))
                nc.scalar.activation(Pb[0:qn, u % 3, 0:n], N[0:qn, u % 2, 0:n], ACT.Exp,
                                     bias=neg_max[0:qn, u % 4:u % 4 + 1], scale=-1.0,
                                     accum_out=total[0:qn, u % 6:u % 6 + 1]).then_inc(probs.sem, 1)

            def copy_turned(it, u):
                q0, qn = tiles[units[u]["i"]]
                _, keys = C["keys"](units[u]["i"])
                act.wait_ge(turned.sem, count(turned, it, u))
                if u >= 2:
                    act.wait_ge(mixed.sem, count(mixed, it, u - 2))
                if narrow:
                    sn, nk = keys[0][1], len(keys)
                    last = nc.scalar.activation(PT[0:sn, u % 2, 0:P * nk], ps[0:sn, 4 + u % 2, 0:P * nk], ACT.Copy)
                else:
                    last = nc.scalar.activation(PT[0:META, u % 2, 0:qn], turned_at(u, 0, META, qn), ACT.Copy)
                    if len(keys) > 1:
                        last = nc.scalar.activation(PT[:, u % 2, P:P * len(keys)],
                                                    ps[:, 4, 0:P * (len(keys) - 1)], ACT.Copy)
                last.then_inc(turned_out.sem, 1)

            with act.Fori(0, C["rounds"]) as it:
                for u in range(U + 2):
                    if u < U:
                        exponent(it, u)
                    if u >= 2:
                        copy_turned(it, u - 2)


def turn_heads_stage(nc, S, layer, y_tm, y, pairs, q_tiles, base, col0=0):
    ps, ident = S["psum"], S["ident"]
    y_turned, y_out = S["y_turned"], S["y_out"]
    total = sum(n for _, n in q_tiles)
    wide = 2 if total > 512 else 1
    with nc.Block() as block:
        @block.tensor
        def _(pe):
            for f in range(pairs):
                if f >= 2:
                    pe.wait_ge(y_out.sem, y_out.at(layer, base + f - 1))
                    if wide == 2:
                        pass_waits(pe, S)
                for i, (q0, qn) in enumerate(q_tiles):
                    at = (ps[:, 2 * (f % 2) + 1, 0:qn] if i == 0 else ps[:, 2 * (f % 2), P * (i - 1):P * i]) \
                        if wide == 2 else ps[:, 2 * (f % 2), P * i:P * (i + 1)]
                    mm = nc.tensor.transpose(at, y_tm[0:qn, i, P * f:P * (f + 1)], ident[0:qn, 0:qn])
                mm.then_inc(y_turned.sem, 1)

        @block.scalar
        def _(act):
            for f in range(pairs):
                act.wait_ge(y_turned.sem, y_turned.at(layer, base + f + 1))
                if wide == 2:
                    nc.scalar.activation(y[:, f, 0:META], ps[:, 2 * (f % 2) + 1, 0:META], ACT.Copy)
                last = nc.scalar.activation(y[:, f, total - SEQ:total], ps[:, 2 * (f % 2), 0:SEQ], ACT.Copy)
                last.then_inc(y_out.sem, 1)


COLS_A = {}
_at = 0
for _name, _n in (("mix_pre", KD), ("mix_post", KD), ("ffn_pre", KD), ("ffn_post", KD), ("head_g", KD),
                  ("dw_b", 2), ("ln_g", 2), ("ln_b", 2), ("dw_w", 2 * TAPS_LONG), ("sc_w", 2 * TAPS_SHORT),
                  ("ff_w", 2 * FF_PAIRS * TAPS_SHORT), ("b_forget", 1), ("pw_w", 2 * 256)):
    COLS_A[_name] = (_at, _at + _n)
    _at += _n
N_COLS_A = _at
MM_A = 97


def in_stage_a(nc, S, ring, layer, A, M):
    ps, w, mm_done, u = S["psum"], ring["tiles"], ring["mm_done"], M["u"]
    act_out, dve_out, dve_step, f_step = S["act_out"], S["dve_out"], S["dve_step"], S["f_step"]
    ln_pe, ln_act, f_rows = S["ln_pe"], S["ln_act"], S["f_rows"]
    col = M["col"]
    a_pad, p_pad, acc, gate, scc, scb, y = (M[x] for x in ("a_pad", "p_pad", "acc", "gate", "scc", "scb", "y"))
    fx, fa = M["fx"], M["fa"]

    def buf(t):
        return banks(ps, 2 * (t % 2), TA)

    with nc.Block() as block:
        @block.sync
        def _(sp):
            full = ring["full"]
            groups = [2, 4, 6, 8, 10, 11, 13, 15, 17, 19, 24, 29]
            for j in range(12):
                sp.wait_ge(mm_done.sem, mm_done.at(layer, groups[j]))
                src = A["win"][layer, j + 2] if j < 10 else A["wout"][layer, j - 10]
                sp.dma_start(w[:, j % 2, :], src).then_inc(full[j % 2], 16)
                if j == 10:
                    sp.wait_ge(dve_step.sem, dve_step.at(layer, M["steps"]["F"]))
                    sp.dma_start(M["FR"][0:1, :, :], fx[:, :]).then_inc(f_rows.sem, 16)
                    sp.dma_start(M["FL"][1:2, :, :], fa[:, :]).then_inc(f_rows.sem, 16)
            sp.wait_ge(f_rows.sem, f_rows.at(layer, 2))
            pass_waits(sp, S)

        @block.tensor
        def _(pe):
            def tile(bufno, s, half, cols, j):
                for k in range(KD):
                    for c, (c0, cn) in enumerate(chunks(TA)):
                        unit = half * KD + k
                        mm = nc.tensor.matmul(ps[0:cols, 2 * bufno + c, 0:cn],
                                              w[:, s, unit * UNIT:unit * UNIT + cols],
                                              u[:, k, c0:c0 + cn], start=(k == 0), stop=(k == KD - 1))
                mm.then_inc(mm_done.sem, 1)

            reader = {2: (act_out, 1), 3: (act_out, 2), 4: (dve_out, 1), 5: (dve_out, 2), 6: (act_out, 3),
                      7: (act_out, 4), 8: (dve_out, 3), 9: (dve_out, 4), 10: (act_out, 5)}
            for t in range(11):
                if t in reader:
                    pe.wait_ge(reader[t][0].sem, reader[t][0].at(layer, reader[t][1]))
                if t % 2 == 0:
                    pe.wait_ge(ring["full"][(t // 2) % 2], slot_full(ring, layer, 0, t // 4))
                tile(t % 2, (t // 2) % 2, t % 2, P if t < 10 else HEADS_A, t)
            pe.wait_ge(act_out.sem, act_out.at(layer, 6))
            pe.wait_ge(dve_out.sem, dve_out.at(layer, 5))
            pass_waits(pe, S)
            with pe.Fori(0, 2) as it:
                for j in range(4):
                    pe.wait_ge(act_out.sem, act_out.at(layer, it * 4 + (5 + j)))
                    if j % 2 == 0:
                        pe.wait_ge(ring["full"][j // 2], slot_full(ring, layer, 6, it))
                    tile((11 + j) % 2, j // 2, j % 2, P, 11 + j)
            for s in range(2):
                pe.wait_ge(ring["full"][s], slot_full(ring, layer, 10, 0))
                for i, (q0, qn) in enumerate(Q_TILES_A):
                    n = 5 * s + i
                    if n >= 2:
                        pe.wait_ge(act_out.sem, act_out.at(layer, 14 + n - 1))
                    for k in range(KD):
                        mm = nc.tensor.matmul(ps[0:qn, 4 + n % 2, 0:256], u[:, k, q0:q0 + qn],
                                              w[:, s, k * 256:(k + 1) * 256], start=(k == 0), stop=(k == KD - 1))
                    mm.then_inc(mm_done.sem, 1)
            pe.wait_ge(dve_step.sem, dve_step.at(layer, M["steps"]["conv"]))
            for j in range(2):
                for c, (c0, cn) in enumerate(chunks(TA)):
                    mm = nc.tensor.matmul(ps[:, 6 + c, 0:cn], S["mean256"][:, :], acc[:, j, c0:c0 + cn],
                                          start=(j == 0), stop=(j == 1))
            mm.then_inc(ln_pe.sem, 1)
            pe.wait_ge(ln_act.sem, ln_act.at(layer, 2))
            for j in range(2):
                for c, (c0, cn) in enumerate(chunks(TA)):
                    mm = nc.tensor.matmul(ps[:, 6 + c, 0:cn], S["mean256"][:, :], gate[:, j, c0:c0 + cn],
                                          start=(j == 0), stop=(j == 1))
            mm.then_inc(ln_pe.sem, 1)
            pe.wait_ge(ln_act.sem, ln_act.at(layer, 5))
            for m in range(2):
                for k in range(2):
                    for c, (c0, cn) in enumerate(chunks(TA)):
                        pw = col("pw_w")
                        mm = nc.tensor.matmul(ps[:, 2 * m + c, 0:cn], pw[:, k * 256 + m * P:k * 256 + (m + 1) * P],
                                              acc[:, k, c0:c0 + cn], start=(k == 0), stop=(k == 1))
                mm.then_inc(ln_pe.sem, 1)

        @block.scalar
        def _(act):
            def take(t, group, out, func):
                act.wait_ge(mm_done.sem, mm_done.at(layer, group))
                return nc.scalar.activation(split(out, TA), buf(t), func).then_inc(act_out.sem, 1)

            for j in range(2):
                take(j, j + 1, gate[:, j, :], ACT.Sigmoid)
            for j in range(2):
                take(4 + j, 5 + j, scc[:, j, :], ACT.Copy)
            for j in range(2):
                take(8 + j, 9 + j, scb[:, j, :], ACT.Copy)
            act.wait_ge(dve_out.sem, dve_out.at(layer, 5))
            nc.scalar.activation(fa[:, :], fx[:, :], ACT.Abs).then_inc(f_step.sem, 1)
            act.wait_ge(f_step.sem, f_step.at(layer, 1))
            nc.scalar.activation(fa[:, :], fa[:, :], ACT.Exp, scale=-1.0).then_inc(f_step.sem, 1)
            act.wait_ge(f_step.sem, f_step.at(layer, 2))
            nc.scalar.activation(fa[:, :], fa[:, :], ACT.Ln, bias=1.0).then_inc(f_step.sem, 1)
            with act.Fori(0, 2) as it:
                for j in range(4):
                    act.wait_ge(mm_done.sem, mm_done.at(layer, it * 4 + (12 + j)))
                    nc.scalar.activation(split(M["qk"][:, it * 4 + j, :], TA), buf(11 + j),
                                         ACT.Copy).then_inc(act_out.sem, 1)
            for s in range(2):
                for i, (q0, qn) in enumerate(Q_TILES_A):
                    n = 5 * s + i
                    act.wait_ge(mm_done.sem, mm_done.at(layer, 20 + n))
                    nc.scalar.activation(M["v"][0:qn, i, 256 * s:256 * (s + 1)], ps[0:qn, 4 + n % 2, 0:256],
                                         ACT.Copy).then_inc(act_out.sem, 1)
            for j in range(2):
                act.wait_ge(dve_step.sem, dve_step.at(layer, M["steps"]["centred"] - 1 + j))
                nc.scalar.activation(gate[:, j, :], acc[:, j, :], ACT.Square).then_inc(ln_act.sem, 1)
            act.wait_ge(ln_pe.sem, ln_pe.at(layer, 2))
            nc.scalar.activation(split(scc[:, 0, :], TA), banks(ps, 6, TA), ACT.Sqrt,
                                 bias=S["eps5"][:, 0:1]).then_inc(ln_act.sem, 1)
            ln_b = col("ln_b")
            for j in range(2):
                act.wait_ge(dve_step.sem, dve_step.at(layer, M["steps"]["normed"] - 1 + j))
                nc.scalar.activation(acc[:, j, :], acc[:, j, :], ACT.Silu,
                                     bias=ln_b[:, j:j + 1]).then_inc(ln_act.sem, 1)
            for j in range(2):
                act.wait_ge(ln_pe.sem, ln_pe.at(layer, 3 + j))
                nc.scalar.activation(split(y[:, 4 + j, :], TA), banks(ps, 2 * j, TA), ACT.Copy)

        @block.vector
        def _(dve):
            step = [0]

            def then(ins):
                step[0] += 1
                return ins.then_inc(dve_step.sem, 1)

            def after(n):
                dve.wait_ge(dve_step.sem, dve_step.at(layer, n))

            def take(group, gates, t, other, out):
                dve.wait_ge(mm_done.sem, mm_done.at(layer, group))
                dve.wait_ge(act_out.sem, act_out.at(layer, gates))
                nc.vector.tensor_tensor(split(out, TA), buf(t), split(other, TA), ALU.mult).then_inc(dve_out.sem, 1)

            for j in range(2):
                take(3 + j, 1 + j, 2 + j, gate[:, j, :], a_pad[:, j, TAPS_LONG - 1:TAPS_LONG - 1 + TA])
            for j in range(2):
                take(7 + j, 3 + j, 6 + j, scc[:, j, :], p_pad[:, j, TAPS_SHORT - 1:TAPS_SHORT - 1 + TA])
            dve.wait_ge(mm_done.sem, mm_done.at(layer, 11))
            nc.vector.tensor_scalar(split(fx[:, :], TA), banks(ps, 0, TA)[0:HEADS_A], col("b_forget")[0:HEADS_A, 0:1],
                                    None, ALU.add).then_inc(dve_out.sem, 1)
            scw = col("sc_w")
            dve.wait_ge(dve_out.sem, dve_out.at(layer, 4))
            for j in range(2):
                then(nc.vector.tensor_scalar(scc[:, j, :], p_pad[:, j, 0:TA], scw[:, j * 3:j * 3 + 1], None, ALU.mult))
                for tap in range(1, TAPS_SHORT):
                    after(step[0])
                    then(nc.vector.scalar_tensor_tensor(
                        out=scc[:, j, :], in0=p_pad[:, j, tap:tap + TA], scalar=scw[:, j * 3 + tap:j * 3 + tap + 1],
                        in1=scc[:, j, :], op0=ALU.mult, op1=ALU.add))
                after(step[0])
                dve.wait_ge(act_out.sem, act_out.at(layer, 5 + j))
                then(nc.vector.tensor_tensor(y[:, 6 + j, :], scc[:, j, :], scb[:, j, :], ALU.mult))
            dve.wait_ge(f_step.sem, f_step.at(layer, 3))
            then(nc.vector.scalar_tensor_tensor(out=fa[:, :], in0=fx[:, :], scalar=0.0, in1=fa[:, :],
                                                op0=ALU.min, op1=ALU.subtract))
            after(step[0])
            then(nc.vector.tensor_tensor_scan(fx[:, :], S["ones"][0:HEADS_A, 0:TA], fa[:, :], 0.0, ALU.mult, ALU.add))
            after(step[0])
            then(nc.vector.tensor_scalar(fa[:, :], fx[:, :], -1.0, None, ALU.mult))
            assert step[0] == M["steps"]["F"]
            dww, dwb = col("dw_w"), col("dw_b")
            for j in range(2):
                dve.wait_ge(dve_out.sem, dve_out.at(layer, 1 + j))
                then(nc.vector.tensor_scalar(acc[:, j, :], a_pad[:, j, 0:TA], dww[:, j * TAPS_LONG:j * TAPS_LONG + 1],
                                             dwb[:, j:j + 1], ALU.mult, ALU.add))
            with dve.Fori(0, TAPS_LONG - 1) as it:
                for j in range(2):
                    dve.wait_ge(dve_step.sem, dve_step.at(layer, it * 2 + (step[0] - 1 + j)))
                    nc.vector.scalar_tensor_tensor(
                        out=acc[:, j, :], in0=a_pad[:, j, bass.ds(it + 1, TA)],
                        scalar=dww[:, bass.ds(it + (j * TAPS_LONG + 1), 1)], in1=acc[:, j, :],
                        op0=ALU.mult, op1=ALU.add).then_inc(dve_step.sem, 1)
            step[0] += 2 * (TAPS_LONG - 1)
            assert step[0] == M["steps"]["conv"]
            dve.wait_ge(ln_pe.sem, ln_pe.at(layer, 1))
            for j in range(2):
                then(nc.vector.tensor_tensor(split(acc[:, j, :], TA), split(acc[:, j, :], TA), banks(ps, 6, TA),
                                             ALU.subtract))
            assert step[0] == M["steps"]["centred"]
            dve.wait_ge(ln_act.sem, ln_act.at(layer, 3))
            then(nc.vector.reciprocal(scc[:, 0, :], scc[:, 0, :]))
            after(step[0])
            ln_g = col("ln_g")
            for j in range(2):
                then(nc.vector.scalar_tensor_tensor(out=acc[:, j, :], in0=acc[:, j, :], scalar=ln_g[:, j:j + 1],
                                                    in1=scc[:, 0, :], op0=ALU.mult, op1=ALU.mult))
            assert step[0] == M["steps"]["normed"] == dve_step.per_layer


STEPS_A = {"F": 8 + 3, "conv": 11 + 2 * TAPS_LONG, "centred": 13 + 2 * TAPS_LONG, "normed": 16 + 2 * TAPS_LONG}


def head_norm_stage(nc, S, layer, M):
    ps, y, sq = S["psum"], M["y"], S["scratch"]
    g = M["col"]("head_g")
    hn_sq, hn_pe, hn_root, hn_dve = S["hn_sq"], S["hn_pe"], S["hn_root"], S["hn_dve"]
    with nc.Block() as block:
        @block.tensor
        def _(pe):
            for k in range(KD):
                pe.wait_ge(hn_sq.sem, hn_sq.at(layer, k + 1))
                if k >= 4:
                    pe.wait_ge(hn_root.sem, hn_root.at(layer, k - 3))
                for c, (c0, cn) in enumerate(chunks(TA)):
                    mm = nc.tensor.matmul(ps[:, 2 * (k % 4) + c, 0:cn], S["mean64"][:, :], sq[:, k, c0:c0 + cn],
                                          start=True, stop=True)
                mm.then_inc(hn_pe.sem, 1)

        @block.scalar
        def _(act):
            for k in range(KD):
                nc.scalar.activation(sq[:, k, :], y[:, k, :], ACT.Square).then_inc(hn_sq.sem, 1)
            for k in range(KD):
                act.wait_ge(hn_pe.sem, hn_pe.at(layer, k + 1))
                nc.scalar.activation(split(sq[:, k, :], TA), banks(ps, 2 * (k % 4), TA), ACT.Sqrt,
                                     bias=S["eps6"][:, 0:1]).then_inc(hn_root.sem, 1)

        @block.vector
        def _(dve):
            for k in range(KD):
                dve.wait_ge(hn_root.sem, hn_root.at(layer, k + 1))
                nc.vector.reciprocal(sq[:, k, :], sq[:, k, :]).then_inc(hn_dve.sem, 1)
                dve.wait_ge(hn_dve.sem, hn_dve.at(layer, k + 1))
                nc.vector.scalar_tensor_tensor(out=y[:, k, :], in0=y[:, k, :], scalar=g[:, k:k + 1],
                                               in1=sq[:, k, :], op0=ALU.mult, op1=ALU.mult)


def up_stage_a(nc, S, ring, layer, A, M):
    ps, w, mm_done, u, hid = S["psum"], ring["tiles"], ring["mm_done"], M["u"], M["hid"]
    free, convolved, activated, gated = S["psum_free"], S["ff_conv"], S["ff_act"], S["ff_gated"]
    z_pad, cv = M["z_pad"], M["cv"]
    ffw = M["col"]("ff_w")
    base, mm_base, free_base = 16, 37, 8 + 4
    with nc.Block() as block:
        @block.sync
        def _(sp):
            ring_feed(sp, ring, layer, base, lambda j: j * 2 + (mm_base + 2),
                      (FF_PAIRS, lambda j: A["wup"][layer, j]), lambda j: A["wdown"][layer, j])

        @block.tensor
        def _(pe):
            with pe.Fori(0, FF_PAIRS // 2) as it:
                for j in range(4):
                    pe.wait_ge(free.sem, free.at(layer, it * 4 + (free_base + j + 1)))
                    if j % 2 == 0:
                        pe.wait_ge(ring["full"][j // 2], slot_full(ring, layer, base, it))
                    for k in range(KD):
                        for c, (c0, cn) in enumerate(chunks(TA)):
                            unit = (j % 2) * KD + k
                            mm = nc.tensor.matmul(ps[:, 2 * j + c, 0:cn], w[:, j // 2, unit * UNIT:(unit + 1) * UNIT],
                                                  u[:, k, c0:c0 + cn], start=(k == 0), stop=(k == KD - 1))
                    mm.then_inc(mm_done.sem, 1)

        @block.scalar
        def _(act):
            act.sem_inc(free.sem, 4)
            act.sem_inc(convolved.sem, 4)
            with act.Fori(0, FF_PAIRS // 2) as it:
                for j in range(4):
                    act.wait_ge(mm_done.sem, mm_done.at(layer, it * 4 + (mm_base + j + 1)))
                    act.wait_ge(convolved.sem, convolved.at(layer, it * 4 + (j + 1)))
                    nc.scalar.activation(split(z_pad[:, j, TAPS_SHORT - 1:TAPS_SHORT - 1 + TA], TA),
                                         banks(ps, 2 * j, TA), ACT.Copy).then_inc(free.sem, 1)
                    if j % 2 == 1:
                        act.wait_ge(convolved.sem, convolved.at(layer, it * 4 + (4 + j)))
                        nc.scalar.activation(cv[:, j - 1, :], cv[:, j - 1, :], ACT.Silu).then_inc(activated.sem, 1)

        @block.vector
        def _(dve):
            dve.sem_inc(gated.sem, 2)
            with dve.Fori(0, FF_PAIRS // 2) as it:
                for j in range(4):
                    dve.wait_ge(free.sem, free.at(layer, it * 4 + (free_base + 4 + j + 1)))
                    if j % 2 == 0:
                        dve.wait_ge(gated.sem, gated.at(layer, it * 2 + (j // 2 + 1)))
                    m = it * 2 + j // 2
                    wcol = [ffw[:, bass.ds(m * 6 + (3 * (j % 2) + tap), 1)] for tap in range(TAPS_SHORT)]
                    nc.vector.tensor_scalar(cv[:, j, :], z_pad[:, j, 0:TA], wcol[0], None,
                                            ALU.mult).then_inc(S["ff_tap"].sem, 1)
                    for tap in (1, 2):
                        dve.wait_ge(S["ff_tap"].sem, S["ff_tap"].at(layer, it * 8 + (2 * j + tap)))
                        last = nc.vector.scalar_tensor_tensor(out=cv[:, j, :], in0=z_pad[:, j, tap:tap + TA],
                                                              scalar=wcol[tap], in1=cv[:, j, :],
                                                              op0=ALU.mult, op1=ALU.add)
                        last.then_inc(S["ff_tap"].sem if tap == 1 else convolved.sem, 1)
                    if j % 2 == 1:
                        dve.wait_ge(activated.sem, activated.at(layer, it * 2 + (j // 2 + 1)))
                        dve.wait_ge(convolved.sem, convolved.at(layer, it * 4 + (4 + j + 1)))
                        nc.vector.tensor_tensor(hid[:, it * 2 + j // 2, 0:TA], cv[:, j - 1, :], cv[:, j, :],
                                                ALU.mult).then_inc(gated.sem, 1)


def first_stack(nc, G, A, h):
    with ExitStack() as ctx:
        def sb(name, shape):
            return ctx.enter_context(nc.sbuf_tensor(name, shape, F32))

        def sem(name):
            return ctx.enter_context(nc.semaphore(name))

        def signal(name, per_layer, step=1):
            return Signal(sem(name), per_layer, step)

        u, y = sb("u_a", [P, KD, TA]), sb("y_a", [P, KD, TA])
        arena = sb("arena_a", [P, 15744])
        stage = sb("stage_a", [P, 7744])
        cols = sb("cols_a", [P, N_COLS_A])
        FL, FR = sb("f_left", [2, HEADS_A, TA]), sb("f_right", [2, HEADS_A, TA])
        strip = sb("mask_strip_a", [P, TA + META])
        rstd = sb("rstd_a", [P, TA])

        def part(where, at, *shape):
            n = int(np.prod(shape))
            ap = where[:, at:at + n]
            return ap if len(shape) == 1 else ap.rearrange("p (a b) -> p a b", a=shape[0])

        def col(name):
            return cols[:, COLS_A[name][0]:COLS_A[name][1]]

        M = {"u": u, "y": y, "col": col, "FL": FL, "FR": FR, "steps": STEPS_A,
             "qk": part(arena, 0, 8, TA), "v": part(arena, 8 * TA, 5, 512), "y_tm": part(arena, 8 * TA + 2560, 5, 512),
             "hid": part(arena, 0, FF_PAIRS, TA)}
        at = 8 * TA + 5120
        M["a_pad"] = part(arena, at, 2, TA + TAPS_LONG - 1)
        M["p_pad"] = part(arena, at + 1116, 2, TA + TAPS_SHORT - 1)
        for n, name in enumerate(("acc", "gate", "scc", "scb")):
            M[name] = part(arena, at + 1116 + 1060 + n * 2 * TA, 2, TA)
        qs, ks, fls = part(stage, 0, TA), part(stage, TA, TA), part(stage, 2 * TA, 2, TA)
        frs, vp = part(stage, 9 * TA + 1280, 2, TA), part(stage, 11 * TA + 1280, 5, P)
        M["fx"], M["fa"] = stage[0:HEADS_A, 0:TA], stage[0:HEADS_A, TA:2 * TA]
        M["z_pad"] = part(stage, 0, 4, TA + 2)
        M["cv"] = part(stage, 4 * (TA + 2), 4, TA)

        ring = {"tiles": G["ring"], "full": [sem(f"slot{s}_full_a") for s in range(2)],
                "mm_done": signal("mm_done_a", MM_A), "per_layer": SLOTS_A}
        U = 2 * len(Q_TILES_A)
        per = HEADS_A // 2 * U
        S = dict(G["consts"])
        S.update(
            psum=G["psum"], scratch=part(arena, 0, KD, TA), rstd=rstd,
            N=part(stage, 4 * TA, 2, TA), P=part(stage, 6 * TA, 3, TA), PT=part(stage, 9 * TA, 2, 640),
            squared=signal("squared_a", 4 * KD), summed=signal("summed_a", 4), rooted=signal("rooted_a", 4),
            rstd_ready=signal("rstd_ready_a", 4), scaled=signal("scaled_a", 4 * KD),
            act_out=signal("act_out", 24), dve_out=signal("dve_out", 5),
            dve_step=signal("dve_step", STEPS_A["normed"]), f_step=signal("f_step", 3),
            ln_pe=signal("ln_pe", 4), ln_act=signal("ln_act", 5), f_rows=signal("f_rows", 2, 16),
            cols_in=signal("cols_in_a", 1, 16),
            scores=signal("scores_a", per), shifted=signal("shifted_a", per), inverted=signal("inverted_a", per), probs=signal("probs_a", per),
            turned=signal("turned_a", per), turned_out=signal("turned_out_a", per), mixed=signal("mixed_a", per),
            stored=signal("stored_a", per), staged=signal("staged_a", HEADS_A // 2),
            y_turned=signal("y_turned_a", 4), y_out=signal("y_out_a", 4),
            hn_sq=signal("hn_sq", KD), hn_pe=signal("hn_pe", KD), hn_root=signal("hn_root", KD),
            hn_dve=signal("hn_dve", KD),
            psum_free=signal("psum_free_a", (8 + 4) + (44 + 4) + (8 + 2)),
            ff_conv=signal("ff_conv", 4 + 2 * FF_PAIRS), ff_act=signal("ff_act", FF_PAIRS),
            ff_gated=signal("ff_gated", 2 + FF_PAIRS), ff_tap=signal("ff_tap", 4 * FF_PAIRS))
        consts_in = sem("consts_in_a")

        with nc.Block() as block:
            @block.sync
            def _(sp):
                sp.dma_start(strip[:, :], A["mask_a"]).then_inc(consts_in, 16)
                sp.wait_ge(consts_in, 16)

            @block.vector
            def _(dve):
                nc.vector.memset(FL[:, :, :], 1.0)
                nc.vector.memset(FR[:, :, :], 1.0)

        def last_key(i):
            q0, qn = Q_TILES_A[i]
            return q0 + qn, Q_TILES_A[:i + 1]

        units = [{"hh": hh, "i": i} for hh in range(2) for i in range(len(Q_TILES_A))]

        with nc.Fori(0, DEPTH) as layer:
            with nc.Block() as block:
                @block.sync
                def _(sp):
                    sp.dma_start(cols[:, :], A["cols_a"][layer]).then_inc(S["cols_in"].sem, 16)
                    first_slots(sp, ring, lambda j: A["win"][layer, j])
                    sp.wait_ge(S["cols_in"].sem, S["cols_in"].at(layer, 1))
                    pass_waits(sp, S)

                @block.vector
                def _(dve):
                    nc.vector.memset(M["a_pad"][:, :, 0:TAPS_LONG - 1], 0.0)
                    nc.vector.memset(M["p_pad"][:, :, 0:TAPS_SHORT - 1], 0.0)

            norm_stage(nc, S, layer, 0, TA, h, col("mix_pre"), u)
            in_stage_a(nc, S, ring, layer, A, M)

            def stage_pair(it):
                nc.vector.tensor_scalar(qs, M["qk"][:, it * 2, :], -DH ** -0.5, None, ALU.mult)
                nc.vector.tensor_copy(ks, M["qk"][:, it * 2 + 1, :])
                nc.vector.tensor_copy(vp[0:META, 0, :], M["v"][0:META, 0, bass.ds(it * P, P)])
                nc.vector.tensor_copy(vp[:, 1:5, :], M["v"][:, 1:5, bass.ds(it * P, P)])
                nc.vector.tensor_copy(frs[0:2, :, :], FR[:, bass.ds(it * 2, 2), :])
                return nc.vector.tensor_copy(fls[0:2, :, :], FL[:, bass.ds(it * 2, 2), :])

            def invert(dve, it, unit, u_, qn, factor, total):
                nc.vector.reciprocal(factor, total).then_inc(S["inverted"].sem, 1)

            def finish(dve, it, unit, u_, q0, qn, product, factor):
                dst = M["y_tm"][0:qn, unit["i"], bass.ds(it * P + unit["hh"] * DH, DH)]
                return nc.vector.tensor_scalar(dst, product, factor, None, ALU.mult)

            softmax_stage(nc, S, layer, {
                "base": 0, "stage_base": 0, "rounds": HEADS_A // 2, "units": units, "T": TA,
                "q_tiles": Q_TILES_A, "keys": last_key, "stage": stage_pair, "finish": finish, "invert": invert,
                "q": lambda un, q0, qn: qs[DH * un["hh"]:DH * (un["hh"] + 1), q0:q0 + qn],
                "k": lambda un, a, b: ks[DH * un["hh"]:DH * (un["hh"] + 1), a:b],
                "v": lambda it, un, j, sn: vp[0:sn, j, DH * un["hh"]:DH * (un["hh"] + 1)],
                "more": lambda it, un, q0, qn: [(fls[0:2, un["hh"], q0:q0 + qn],
                                                 lambda a, b: frs[0:2, un["hh"], a:b])],
                "bias": lambda un, qn, n: strip[0:qn, TA:TA + n] if un["i"] == 0 else strip[0:qn, TA - n:TA],
            })
            turn_heads_stage(nc, S, layer, M["y_tm"], y, 4, Q_TILES_A, 0)
            head_norm_stage(nc, S, layer, M)
            linear_stage(nc, S, ring, layer, TA, A["wout"], 4, y, 12, 29, 0, lambda j: A["wup"][layer, j], out=u)
            norm_stage(nc, S, layer, 1, TA, u, col("mix_post"), y, residual=h)
            with nc.Block() as block:
                @block.vector
                def _(dve):
                    nc.vector.memset(M["z_pad"][:, :, 0:TAPS_SHORT - 1], 0.0)
            norm_stage(nc, S, layer, 2, TA, h, col("ffn_pre"), u)
            up_stage_a(nc, S, ring, layer, A, M)
            linear_stage(nc, S, ring, layer, TA, A["wdown"], 16, M["hid"], 38, 81, 12 + 48, None,
                         deep=FF_PAIRS, out=u)
            norm_stage(nc, S, layer, 3, TA, u, col("ffn_post"), y, residual=h)


MM_B = 92
OUT_TOKENS = TB
LAST_DIST = TB - 1
ROW_LEN = 640
T_SB, T_MB, T_DF, T_NSQ, T_CMP, T_KSW = 0, 4, 8, 12, 14, 15
V_SB, V_MB, V_DF, V_SLC, V_WIN, V_G = 0, 256, 512, 768, 832, 896
Y_SB, Y_MB, Y_NS, Y_DF = 0, 256, 512, 768
COLS_B = {}
_at = 0
for _name, _n in (("attn_g", KD), ("mlp_g", KD), ("pos", 2 * 16), ("w2k", 2 * P), ("w2v", 2 * DH),
                  ("lambda", 4 * 32), ("neg_lambda_init", 1), ("one_less_init", 1), ("subln", DH)):
    COLS_B[_name] = (_at, _at + _n)
    _at += _n
N_COLS_B = _at
UNITS_B = 96


def bias_setup(nc, S, A, M):
    ps = S["psum"]
    loaded, multiplied, copied, row_out, strips_in = (M[x] for x in ("loaded", "multiplied", "copied", "row_out", "strips_in"))
    table, rev, fwd, rows = M["table"], M["rev"], M["fwd"], M["rows"]
    scratch = M["bias_rows"]
    with nc.Block() as block:
        @block.sync
        def _(sp):
            sp.dma_start(table[0:N_BUCKETS, :], A["rel_bias"]).then_inc(loaded, 16)
            sp.dma_start(rev[:, :], A["onehot_rev"]).then_inc(loaded, 16)
            sp.dma_start(fwd[:, :], A["onehot_fwd"]).then_inc(loaded, 16)
            for name in ("tri", "neg_ones", "mask01", "mask_add", "cover", "blocks", "imp_scale", "imp_add",
                         "tri8", "valid", "reverse"):
                sp.dma_start(M[name][:, :], A[name]).then_inc(loaded, 16)
            sp.wait_ge(copied, 1)
            sp.dma_start(scratch, rows[:, :]).then_inc(row_out, 16)
            sp.wait_ge(row_out, 16)
            for hd in range(3 * HEADS_B):
                src = bass.AP(scratch.tensor, hd * ROW_LEN, [[1, P], [1, TB]])
                sp.dma_start(M["strips"][:, hd, :], src).then_inc(strips_in, 16)
            sp.wait_ge(strips_in, 16 * 3 * HEADS_B)
            sp.wait_ge(loaded, 16 * 14)

        @block.vector
        def _(dve):
            nc.vector.memset(table[N_BUCKETS:N_BUCKETS + 1, :], 1.0).then_inc(M["one_row"], 1)

        @block.tensor
        def _(pe):
            pe.wait_ge(loaded, 16 * 14)
            pe.wait_ge(M["one_row"], 1)
            for c in range(2):
                mm = nc.tensor.matmul(ps[0:3 * HEADS_B, c, 0:ROW_LEN // 2], table[:, :],
                                      rev[:, c * (ROW_LEN // 2):(c + 1) * (ROW_LEN // 2)], start=True, stop=True)
            mm.then_inc(multiplied, 1)
            for i in range(4):
                for c in range(N_CMP):
                    f0 = LAST_DIST + P * i - CMP_STRIDE * c - (CMP_LEN - 1)
                    at = (i * N_CMP + c) * HEADS_B
                    mm = nc.tensor.matmul(ps[:, 2, at:at + HEADS_B], fwd[:, f0:f0 + P],
                                          table[:, HEADS_B:2 * HEADS_B], start=True, stop=True)
            mm.then_inc(multiplied, 1)

        @block.scalar
        def _(act):
            act.wait_ge(multiplied, 1)
            nc.scalar.activation(rows[:, :].rearrange("p (c n) -> p c n", c=2),
                                 ps[0:3 * HEADS_B, 0:2, 0:ROW_LEN // 2], ACT.Copy).then_inc(copied, 1)
            act.wait_ge(multiplied, 2)
            for hd in range(HEADS_B):
                src = ps[:, 2, 0:4 * N_CMP * HEADS_B].rearrange("p (i c h) -> p i c h", i=4, h=HEADS_B)[:, :, :, hd]
                nc.scalar.activation(M["cbias"][:, hd, :, :], src, ACT.Copy)

    turned, placed = M["strip_turned"], M["strip_placed"]
    with nc.Block() as block:
        @block.tensor
        def _(pe):
            for hd in range(3 * HEADS_B):
                if hd >= 8:
                    pe.wait_ge(placed, hd - 7)
                nc.tensor.matmul(ps[:, hd % 8, 0:TB], M["reverse"][:, :], M["strips"][:, hd, :],
                                 start=True, stop=True).then_inc(turned, 1)

        @block.scalar
        def _(act):
            for hd in range(3 * HEADS_B):
                act.wait_ge(turned, hd + 1)
                nc.scalar.activation(M["strips"][:, hd, :], ps[:, hd % 8, 0:TB], ACT.Copy).then_inc(placed, 1)


def token_major_stage(nc, S, ring, layer, A, M):
    ps, w, mm_done, free, u = S["psum"], ring["tiles"], ring["mm_done"], S["tm_free"], M["u"]
    base, mm_base = 8, 16
    with nc.Block() as block:
        @block.sync
        def _(sp):
            ring_feed(sp, ring, layer, base, lambda j: j * 4 + (mm_base + 4),
                      (4, lambda j: A["wv_b"][layer, j]), lambda j: A["wcmp"][layer, j])

        @block.tensor
        def _(pe):
            with pe.Fori(0, 2) as it:
                for s in range(2):
                    pe.wait_ge(ring["full"][s], slot_full(ring, layer, base, it))
                    for i in range(4):
                        pe.wait_ge(free.sem, free.at(layer, it * 8 + (4 * s + i + 1)))
                        for k in range(KD):
                            mm = nc.tensor.matmul(ps[:, 4 + i, 0:256], u[:, k, P * i:P * (i + 1)],
                                                  w[:, s, k * 256:(k + 1) * 256], start=(k == 0), stop=(k == KD - 1))
                        mm.then_inc(mm_done.sem, 1)

        @block.scalar
        def _(act):
            act.sem_inc(free.sem, 4)
            with act.Fori(0, 2) as it:
                for s in range(2):
                    for i in range(4):
                        act.wait_ge(mm_done.sem, mm_done.at(layer, it * 8 + (mm_base + 4 * s + i + 1)))
                        nc.scalar.activation(M["v_tm"][:, i, bass.ds(it * 512 + 256 * s, 256)], ps[:, 4 + i, 0:256],
                                             ACT.Copy).then_inc(free.sem, 1)


def prepare_stage(nc, S, ring, layer, A, M):
    ps, w, mm_done, fm, col = S["psum"], ring["tiles"], ring["mm_done"], M["fm"], M["col"]
    blocks_in, hidden, projected, lam_step = S["blocks_in"], S["hidden"], S["projected"], S["lam_step"]
    base, mm_base = 12, 32
    xb, hg = M["xb"], M["hg"]
    with nc.Block() as block:
        @block.sync
        def _(sp):
            ring_feed(sp, ring, layer, base, lambda j: j + (mm_base + 1),
                      (4, lambda j: A["wcmp"][layer, j]), lambda j: A["wout_b"][layer, j])

        @block.vector
        def _(dve):
            pos = col("pos").rearrange("p (t r) -> p t r", t=2)
            tokens = fm[:, T_CMP, :].rearrange("p (c r t) -> p t r c", r=8, t=2)
            for kv in range(2):
                rows = slice(64 * kv, 64 * kv + 64)
                for t in range(2):
                    for half in range(2):
                        last = nc.vector.tensor_tensor(
                            xb[64 * t:64 * t + 64, kv, 8 * half:8 * half + 8, :],
                            tokens[rows, t, :, half:half + N_CMP],
                            pos[rows, t, 8 * half:8 * half + 8].unsqueeze(2).to_broadcast([64, 8, N_CMP]), ALU.add)
                last.then_inc(blocks_in.sem, 1)
            for n, dst in enumerate((M["k_slc"], M["k_win"])):
                for half in range(2):
                    nc.vector.tensor_copy(dst[64 * half:64 * half + 64, :], fm[64 * n:64 * n + 64, T_KSW, :])
            nc.vector.memset(M["pc_sum"][:, :, :], 0.0)
            lam, pr = M["lam"], M["lam_products"]
            lv = col("lambda")
            for n in range(2):
                last = nc.vector.tensor_tensor_reduce(pr[:, 32 * n:32 * n + 32], lv[:, 64 * n:64 * n + 32], lv[:, 64 * n + 32:64 * n + 64],
                                                      1.0, 0.0, ALU.mult, ALU.add, lam[:, n:n + 1])
            last.then_inc(lam_step.sem, 1)
            nc.vector.tensor_scalar(M["subln"][:, :], col("subln"), col("one_less_init"), None, ALU.mult)
            dve.wait_ge(lam_step.sem, lam_step.at(layer, 2))
            nc.vector.scalar_tensor_tensor(out=M["neg_lam"][:, :], in0=lam[:, 1:2], scalar=lam[:, 0:1],
                                           in1=col("neg_lambda_init"), op0=ALU.subtract, op1=ALU.add)
            dve.wait_ge(lam_step.sem, lam_step.at(layer, 3))
            nc.vector.tensor_scalar(M["gates"][:, 0, 0:HEADS_B], M["gates"][:, 0, 0:HEADS_B], M["valid"][:, 0:1],
                                    None, ALU.mult)

        @block.tensor
        def _(pe):
            for kv in range(2):
                pe.wait_ge(blocks_in.sem, blocks_in.at(layer, kv + 1))
                for s in range(2):
                    pe.wait_ge(ring["full"][s], slot_full(ring, layer, base, kv))
                    for l8 in range(8):
                        for m in range(2):
                            unit = 2 * l8 + m
                            mm = nc.tensor.matmul(ps[:, 2 * kv + m, 0:N_CMP], w[:, s, unit * UNIT:(unit + 1) * UNIT],
                                                  xb[:, kv, 8 * s + l8, :], start=(s == 0 and l8 == 0),
                                                  stop=(s == 1 and l8 == 7))
                    mm.then_inc(mm_done.sem, 1)
            w2k, w2v = col("w2k"), col("w2v")
            pe.wait_ge(hidden.sem, hidden.at(layer, 4))
            for m in range(2):
                nc.tensor.matmul(ps[:, 4, 0:N_CMP], w2k[:, P * m:P * (m + 1)], hg[:, m, :], start=(m == 0), stop=(m == 1))
            for m in range(2):
                mm = nc.tensor.matmul(ps[0:N_CMP, 5, 0:DH], hg[:, 2 + m, :], w2v[:, DH * m:DH * (m + 1)],
                                      start=(m == 0), stop=(m == 1))
            mm.then_inc(projected.sem, 1)

        @block.scalar
        def _(act):
            act.wait_ge(lam_step.sem, lam_step.at(layer, 1))
            nc.scalar.activation(M["lam"][:, 0:2], M["lam"][:, 0:2], ACT.Exp).then_inc(lam_step.sem, 1)
            nc.scalar.activation(M["gates"][:, :, :], M["v_tm"][:, :, V_G:V_G + 12], ACT.Sigmoid).then_inc(lam_step.sem, 1)
            for n in range(4):
                act.wait_ge(mm_done.sem, mm_done.at(layer, mm_base + 2 * (n // 2) + 2))
                nc.scalar.activation(hg[:, n, :], ps[:, n, 0:N_CMP], ACT.Gelu_apprx_tanh).then_inc(hidden.sem, 1)
            act.wait_ge(projected.sem, projected.at(layer, 1))
            nc.scalar.activation(M["k_cmp"][:, :], ps[:, 4, 0:N_CMP], ACT.Copy)
            nc.scalar.activation(M["v_cmp"][0:N_CMP, :], ps[0:N_CMP, 5, 0:DH], ACT.Copy)


def stick_stage(nc, S, layer, M):
    ps, fm, qs, ks = S["psum"], M["fm"], M["qs"], M["ks"]
    z_in, softplus, logit, fenced, weight, mixed, stored, staged = (
        S[x] for x in ("sb_z", "sb_softplus", "sb_logit", "sb_fenced", "sb_weight", "sb_mixed", "sb_stored", "sb_staged"))
    ln, sb_ln = M["sb_log"], S["sb_ln"]
    sp_, aw = M["sb_sp"], M["sb_w"]
    units = [(hh, st) for hh in range(2) for st in (3, 2, 1, 0)]
    U = len(units)

    def at(sig, it, n, per=1):
        return sig.at(layer, it * (U * per) + n)

    with nc.Block() as block:
        @block.tensor
        def _(pe):
            def z_term(out, u, start, stop):
                hh, st = units[u]
                rows = slice(64 * hh, 64 * hh + 64)
                return nc.tensor.matmul(out, ks[rows, P * st:P * (st + 1)], qs[rows, P * st:TB], start=start, stop=stop)

            def logits(it, u):
                hh, st = units[u]
                n = TB - P * st
                pe.wait_ge(softplus.sem, at(softplus, it, 2 * (u + 1), 2))
                if u >= 2:
                    pe.wait_ge(weight.sem, at(weight, it, u - 1))
                b = 2 + u % 2
                z_term(ps[:, b, 0:n], u, True, False)
                for jt in range(st + 1, 4):
                    nc.tensor.matmul(ps[:, b, P * (jt - st):n], M["neg_ones"][:, :], sp_[:, hh, jt, 0:TB - P * jt],
                                     start=False, stop=False, skip_group_check=True)
                mm = nc.tensor.matmul(ps[:, b, 0:n], M["tri"][:, :], sp_[:, hh, st, 0:n], start=False, stop=True)
                mm.then_inc(logit.sem, 1)

            def mix(it, hh):
                pe.wait_ge(weight.sem, at(weight, it, 4 * (hh + 1)))
                for tt in range(4):
                    for st in range(tt + 1):
                        mm = nc.tensor.matmul(ps[:, 4 + hh, DH * tt:DH * (tt + 1)],
                                              aw[:, hh, st, P * (tt - st):P * (tt - st + 1)],
                                              M["v_tm"][:, st, bass.ds(it * P + (V_SB + DH * hh), DH)],
                                              start=(st == 0), stop=(st == tt))
                mm.then_inc(mixed.sem, 1)

            with pe.Fori(0, 2) as it:
                pe.wait_ge(staged.sem, staged.at(layer, it + 1))
                for u in range(U + 2):
                    if u < U:
                        hh, st = units[u]
                        z_term(ps[:, u % 2, 0:TB - P * st], u, True, True).then_inc(z_in.sem, 1)
                    if 1 <= u <= U:
                        logits(it, u - 1)
                    if u >= 2 and (u - 2) % 4 == 3:
                        mix(it, (u - 2) // 4)
                pe.wait_ge(stored.sem, stored.at(layer, it * 2 + 2))

        @block.scalar
        def _(act):
            def log_term(it, u):
                n = TB - P * units[u][1]
                buf = ln[:, u % 2, 0:n]
                act.wait_ge(z_in.sem, at(z_in, it, u + 1))
                if u >= 2:
                    act.wait_ge(softplus.sem, at(softplus, it, 2 * (u - 1), 2))
                nc.scalar.activation(buf, ps[:, u % 2, 0:n], ACT.Abs).then_inc(sb_ln.sem, 1)
                act.wait_ge(sb_ln.sem, at(sb_ln, it, 3 * u + 1, 3))
                nc.scalar.activation(buf, buf, ACT.Exp, scale=-1.0).then_inc(sb_ln.sem, 1)
                act.wait_ge(sb_ln.sem, at(sb_ln, it, 3 * u + 2, 3))
                nc.scalar.activation(buf, buf, ACT.Ln, bias=1.0).then_inc(sb_ln.sem, 1)

            def weights(it, u):
                hh, st = units[u]
                n = TB - P * st
                act.wait_ge(fenced.sem, at(fenced, it, u + 1))
                nc.scalar.activation(aw[:, hh, st, 0:n], ps[:, 2 + u % 2, 0:n], ACT.Exp).then_inc(weight.sem, 1)

            with act.Fori(0, 2) as it:
                for u in range(U + 1):
                    if u < U:
                        log_term(it, u)
                    if u >= 1:
                        weights(it, u - 1)

        @block.vector
        def _(dve):
            with dve.Fori(0, 2) as it:
                nc.vector.tensor_scalar(qs, fm[:, it * 2 + T_SB, :], DH ** -0.5, None, ALU.mult)
                nc.vector.tensor_copy(ks, fm[:, it * 2 + (T_SB + 1), :]).then_inc(staged.sem, 1)
                for u in range(U + 1):
                    if u < U:
                        hh, st = units[u]
                        n = TB - P * st
                        dve.wait_ge(sb_ln.sem, at(sb_ln, it, 3 * (u + 1), 3))
                        nc.vector.scalar_tensor_tensor(out=sp_[:, hh, st, 0:n], in0=ps[:, u % 2, 0:n], scalar=0.0,
                                                       in1=ln[:, u % 2, 0:n], op0=ALU.max,
                                                       op1=ALU.add).then_inc(softplus.sem, 1)
                        dve.wait_ge(softplus.sem, at(softplus, it, 2 * u + 1, 2))
                        nc.vector.tensor_tensor(sp_[:, hh, st, 0:P], sp_[:, hh, st, 0:P], M["mask01"][:, :],
                                                ALU.mult).then_inc(softplus.sem, 1)
                    if u >= 1:
                        dve.wait_ge(logit.sem, at(logit, it, u))
                        diag = ps[:, 2 + (u - 1) % 2, 0:P]
                        nc.vector.tensor_tensor(diag, diag, M["mask_add"][:, :], ALU.add).then_inc(fenced.sem, 1)
                for hh in range(2):
                    dve.wait_ge(mixed.sem, mixed.at(layer, it * 2 + (hh + 1)))
                    dst = M["y_tm"][:, :, bass.ds(it * P + (Y_SB + DH * hh), DH)]
                    nc.vector.tensor_copy(dst, ps[:, 4 + hh, 0:4 * DH].rearrange("p (t d) -> p t d", t=4)) \
                        .then_inc(stored.sem, 1)


def select_stage(nc, S, layer, M):
    ps, ident = S["psum"], S["ident"]
    pe_s, act_s, dve_s = S["sel_pe"], S["sel_act"], S["sel_dve"]
    pc, pcT, imp = M["pc_sum"], M["pc_turned"], M["imp"]
    gt, eq, rank = M["gt"], M["eq"], M["rank"]
    with nc.Block() as block:
        @block.tensor
        def _(pe):
            for i in range(4):
                mm = nc.tensor.transpose(ps[0:N_CMP, 0, P * i:P * (i + 1)], pc[:, i, :], ident[:, :])
            mm.then_inc(pe_s.sem, 1)
            pe.wait_ge(act_s.sem, act_s.at(layer, 1))
            for i in range(4):
                mm = nc.tensor.matmul(ps[:, 1, N_SLC * i:N_SLC * (i + 1)], pcT[0:N_CMP, P * i:P * (i + 1)],
                                      M["cover"][:, :], start=True, stop=True)
            mm.then_inc(pe_s.sem, 1)
            pe.wait_ge(dve_s.sem, dve_s.at(layer, 7))
            for i in range(4):
                mm = nc.tensor.transpose(ps[0:N_SLC, 2, P * i:P * (i + 1)], rank[:, i, :], ident[:, :])
            mm.then_inc(pe_s.sem, 1)

        @block.scalar
        def _(act):
            act.wait_ge(pe_s.sem, pe_s.at(layer, 1))
            nc.scalar.activation(pcT[0:N_CMP, :], ps[0:N_CMP, 0, :], ACT.Copy).then_inc(act_s.sem, 1)
            act.wait_ge(pe_s.sem, pe_s.at(layer, 3))
            nc.scalar.activation(M["not_sel"][:, :], ps[0:N_SLC, 2, :], ACT.Copy)

        @block.vector
        def _(dve):
            done = [0]

            def then(ins):
                ins.then_inc(dve_s.sem, 1)
                done[0] += 1
                dve.wait_ge(dve_s.sem, dve_s.at(layer, done[0]))

            flat = imp[:, :, :].rearrange("p i j -> p (i j)")
            wide = [P, 4, N_SLC, N_SLC]
            other = imp[:, :, :].unsqueeze(2).to_broadcast(wide)
            own = imp[:, :, :].unsqueeze(3).to_broadcast(wide)
            dve.wait_ge(pe_s.sem, pe_s.at(layer, 2))
            then(nc.vector.tensor_tensor(flat, ps[:, 1, 0:4 * N_SLC], M["imp_scale"][:, :], ALU.mult))
            then(nc.vector.tensor_tensor(flat, flat, M["imp_add"][:, :], ALU.add))
            nc.vector.tensor_tensor(gt[:, :, :, :], other, own, ALU.is_gt)
            then(nc.vector.tensor_tensor(eq[:, :, :, :], other, own, ALU.is_equal))
            tri8 = M["tri8"][:, :].rearrange("p (j k) -> p j k", j=N_SLC).unsqueeze(1).to_broadcast(wide)
            then(nc.vector.tensor_tensor(eq[:, :, :, :], eq[:, :, :, :], tri8, ALU.mult))
            then(nc.vector.tensor_tensor(gt[:, :, :, :], gt[:, :, :, :], eq[:, :, :, :], ALU.add))
            then(nc.vector.tensor_reduce(rank[:, :, :], gt[:, :, :, :], AX_X, ALU.add))
            then(nc.vector.tensor_scalar(rank[:, :, :], rank[:, :, :], float(SLC_TOP), None, ALU.is_ge))
            pass_waits(dve, S)


def diff_norm_stage(nc, S, layer, M):
    dn_dve, dn_act = S["dn_dve"], S["dn_act"]
    sq, ms = M["dn_sq"], M["dn_ms"]
    yv = M["y_tm"][:, :, Y_DF:Y_DF + 256].rearrange("p i (h d) -> p i h d", h=HEADS_B)
    shape = [P, 4, HEADS_B, DH]
    with nc.Block() as block:
        @block.vector
        def _(dve):
            nc.vector.tensor_tensor(sq[:, :, :, :], yv, yv, ALU.mult).then_inc(dn_dve.sem, 1)
            dve.wait_ge(dn_dve.sem, dn_dve.at(layer, 1))
            nc.vector.tensor_reduce(ms[:, :, :], sq[:, :, :, :], AX_X, ALU.add).then_inc(dn_dve.sem, 1)
            dve.wait_ge(dn_act.sem, dn_act.at(layer, 1))
            nc.vector.reciprocal(ms[:, :, :], ms[:, :, :]).then_inc(dn_dve.sem, 1)
            dve.wait_ge(dn_dve.sem, dn_dve.at(layer, 3))
            nc.vector.tensor_tensor(sq[:, :, :, :], yv, ms[:, :, :].unsqueeze(3).to_broadcast(shape),
                                    ALU.mult).then_inc(dn_dve.sem, 1)
            dve.wait_ge(dn_dve.sem, dn_dve.at(layer, 4))
            gain = M["subln"][:, :].unsqueeze(1).to_broadcast([P, 16, DH])
            nc.vector.tensor_tensor(sq[:, :, :, :].rearrange("p i h d -> p (i h) d"),
                                    sq[:, :, :, :].rearrange("p i h d -> p (i h) d"), gain,
                                    ALU.mult).then_inc(dn_dve.sem, 1)
            dve.wait_ge(dn_dve.sem, dn_dve.at(layer, 5))
            nc.vector.tensor_copy(M["y_tm"][:, :, Y_DF:Y_DF + 256],
                                  sq[:, :, :, :].rearrange("p i h d -> p i (h d)"))

        @block.scalar
        def _(act):
            act.wait_ge(dn_dve.sem, dn_dve.at(layer, 2))
            nc.scalar.activation(ms[:, :, :], ms[:, :, :], ACT.Sqrt, scale=1.0 / DH,
                                 bias=S["eps6"][:, 0:1]).then_inc(dn_act.sem, 1)


def second_stack(nc, G, A, h_all, out):
    h = h_all[:, :, META:TA]
    with ExitStack() as ctx:
        def sb(name, shape):
            return ctx.enter_context(nc.sbuf_tensor(name, shape, F32))

        def sem(name):
            return ctx.enter_context(nc.semaphore(name))

        def signal(name, per_layer, step=1):
            return Signal(sem(name), per_layer, step)

        u, y = sb("u_b", [P, KD, TB]), sb("y_b", [P, KD, TB])
        arena = sb("arena_b", [P, 32 * TB])
        stage = sb("stage_b", [P, 15 * TB])
        cols = sb("cols_b", [P, N_COLS_B])
        strips = sb("strips", [P, 3 * HEADS_B, TB])

        def part(where, at, *shape):
            ap = where[:, at:at + int(np.prod(shape))]
            return ap if len(shape) == 1 else ap.rearrange("p (a b) -> p a b", a=shape[0])

        def col(name):
            return cols[:, COLS_B[name][0]:COLS_B[name][1]]

        M = {"u": u, "y": y, "col": col, "strips": strips,
             "fm": part(arena, 0, 16, TB), "v_tm": part(arena, 16 * TB, 4, 1024),
             "y_tm": part(arena, 24 * TB, 4, 1024), "hid": part(arena, 0, 32, TB),
             "qs": part(stage, 0, TB), "ks": part(stage, TB, TB),
             "sb_log": part(stage, 2 * TB, 2, TB),
             "sb_sp": stage[:, 4 * TB:12 * TB].rearrange("p (a b c) -> p a b c", a=2, b=4),
             "sb_w": y[:, :, :].rearrange("p (a b) c -> p a b c", a=2),
             "bias_pair": part(stage, 9 * TB, 2, TB),
             "k_slc": part(stage, 11 * TB, TB), "k_win": part(stage, 12 * TB, TB),
             "dn_sq": stage[:, 13 * TB:15 * TB].rearrange("p (a b c) -> p a b c", a=4, b=HEADS_B)}
        for name, shape in (("xb", [P, 2, 16, N_CMP]), ("hg", [P, 4, N_CMP]), ("k_cmp", [P, N_CMP]),
                            ("v_cmp", [N_CMP, DH]), ("gates", [P, 4, 12]), ("pc_sum", [P, 4, N_CMP]),
                            ("lam", [P, 2]), ("lam_products", [P, 64]), ("neg_lam", [P, 1]), ("subln", [P, DH]),
                            ("imp", [P, 4, N_SLC]), ("gt", [P, 4, N_SLC, N_SLC]),
                            ("eq", [P, 4, N_SLC, N_SLC]), ("rank", [P, 4, N_SLC]), ("not_sel", [N_SLC, TB]),
                            ("dn_ms", [P, 4, HEADS_B]), ("cbias", [P, HEADS_B, 4, N_CMP]),
                            ("tri", [P, P]), ("neg_ones", [P, P]), ("mask01", [P, P]), ("mask_add", [P, P]),
                            ("cover", [N_CMP, N_SLC]), ("blocks", [N_SLC, TB]), ("imp_scale", [P, 4 * N_SLC]),
                            ("imp_add", [P, 4 * N_SLC]), ("tri8", [P, N_SLC * N_SLC]), ("valid", [P, 4])):
            M[name] = sb(name, shape)
        M["pc_turned"] = stage[0:N_CMP, 0:TB]
        M["table"] = arena[0:N_BUCKETS + 1, 0:3 * HEADS_B]
        M["rev"] = arena[0:N_BUCKETS + 1, 512:512 + ROW_LEN]
        M["fwd"] = arena[0:N_BUCKETS + 1, 2048:2048 + 1024]
        M["reverse"] = arena[:, 5120:5120 + P]
        M["rows"] = arena[0:3 * HEADS_B, 4096:4096 + ROW_LEN]
        M["bias_rows"] = nc.dram_tensor("bias_rows", (3 * HEADS_B, ROW_LEN), F32, kind="Internal").ap()
        for name in ("loaded", "multiplied", "copied", "row_out", "strips_in", "one_row", "strip_turned", "strip_placed"):
            M[name] = sem(name + "_b")

        ring = {"tiles": G["ring"], "full": [sem(f"slot{s}_full_b") for s in range(2)],
                "mm_done": signal("mm_done_b", MM_B), "per_layer": SLOTS_B}
        S = dict(G["consts"])
        S.update(
            psum=G["psum"], scratch=part(arena, 0, KD, TB), rstd=part(stage, 0, TB),
            N=part(stage, 2 * TB, 2, TB), P=part(stage, 4 * TB, 3, TB), PT=part(stage, 7 * TB, 2, TB),
            squared=signal("squared_b", 2 * KD), summed=signal("summed_b", 2), rooted=signal("rooted_b", 2),
            rstd_ready=signal("rstd_ready_b", 2), scaled=signal("scaled_b", 2 * KD), cols_in=signal("cols_in_b", 1, 16),
            psum_free=signal("psum_free_b", (16 + 4) + (8 + 4) + (32 + 4) + (8 + 2)), tm_free=signal("tm_free", 16 + 4),
            blocks_in=signal("blocks_in", 2), hidden=signal("hidden", 4), projected=signal("projected", 1),
            lam_step=signal("lam_step", 3), inv_step=signal("inv_step", 2 * UNITS_B),
            staged=signal("staged_b", 10), y_turned=signal("y_turned_b", 8), y_out=signal("y_out_b", 8),
            sb_z=signal("sb_z", 16), sb_ln=signal("sb_ln", 48), sb_softplus=signal("sb_softplus", 32),
            sb_logit=signal("sb_logit", 16), sb_fenced=signal("sb_fenced", 16), sb_weight=signal("sb_weight", 16),
            sb_mixed=signal("sb_mixed", 4), sb_stored=signal("sb_stored", 4), sb_staged=signal("sb_staged", 2),
            sel_pe=signal("sel_pe", 3), sel_act=signal("sel_act", 1), sel_dve=signal("sel_dve", 7),
            dn_dve=signal("dn_dve", 5), dn_act=signal("dn_act", 1))
        for name in ("scores", "shifted", "probs", "turned", "turned_out", "mixed", "stored", "inverted"):
            S[name] = signal(name + "_b", UNITS_B)

        bias_setup(nc, S, A, M)

        qs, ks, pair = M["qs"], M["ks"], M["bias_pair"]
        v_tm, y_tm, ones = M["v_tm"], M["y_tm"], S["ones"]
        inv_step, inverted = S["inv_step"], S["inverted"]
        by_head = [{"hh": hh, "i": i, "row": DH * hh, "k": DH} for hh in range(2) for i in range(4)]
        by_half = [{"hh": hh, "i": i, "comp": c, "row": DH * hh + 32 * c, "k": 32}
                   for hh in range(2) for i in range(4) for c in range(2)]

        def causal_keys(i):
            return P * (i + 1), Q_TILES_B[:i + 1]

        with nc.Fori(0, DEPTH) as layer:
            def softmax_pass(base, stage_base, units, q_tile, scale, strip0, numerator, finish, v, k=None,
                             k_tile=None, keys=causal_keys, more=None, compressed=False):
                U = len(units)

                def stage_pair(it):
                    last = nc.vector.tensor_scalar(qs, M["fm"][:, q_tile(it), :], scale, None, ALU.mult)
                    if k_tile is not None:
                        last = nc.vector.tensor_copy(ks, M["fm"][:, k_tile(it), :])
                    if compressed:
                        return nc.vector.tensor_copy(
                            pair[:, 0, 0:2 * 4 * N_CMP].rearrange("p (h i c) -> p h i c", h=2, i=4),
                            M["cbias"][:, bass.ds(it * 2, 2), :, :])
                    return nc.vector.tensor_copy(pair, strips[:, bass.ds(it * 2 + strip0, 2), :])

                def bias(un, qn, n):
                    if compressed:
                        at = (un["hh"] * 4 + un["i"]) * N_CMP
                        return pair[:, 0, at:at + N_CMP]
                    return pair[:, un["hh"], TB - n:TB]

                def invert(dve, it, un, u_, qn, factor, total):
                    def after(n):
                        dve.wait_ge(inv_step.sem, inv_step.at(layer, it * (2 * U) + (2 * base + 2 * u_ + n)))

                    nc.vector.tensor_scalar(factor, total, TINY, None, ALU.max).then_inc(inv_step.sem, 1)
                    after(1)
                    nc.vector.reciprocal(factor, factor).then_inc(inv_step.sem, 1)
                    after(2)
                    nc.vector.tensor_tensor(factor, factor, numerator(it, un), ALU.mult).then_inc(inverted.sem, 1)
                    if compressed:
                        dve.wait_ge(inverted.sem, inverted.at(layer, it * U + (base + u_ + 1)))
                        acc = M["pc_sum"][:, un["i"], :]
                        nc.vector.scalar_tensor_tensor(out=acc, in0=S["P"][:, u_ % 3, 0:N_CMP], scalar=factor,
                                                       in1=acc, op0=ALU.mult, op1=ALU.add)

                row = lambda un: slice(un["row"], un["row"] + un["k"])
                kk = ks if k is None else k
                softmax_stage(nc, S, layer, {
                    "base": base, "stage_base": stage_base, "rounds": 2, "units": units, "T": TB,
                    "q_tiles": Q_TILES_B, "keys": keys, "stage": stage_pair, "finish": finish, "invert": invert,
                    "q": lambda un, q0, qn: qs[row(un), q0:q0 + qn], "k": lambda un, a, b: kk[row(un), a:b],
                    "v": v, "more": more or (lambda it, un, q0, qn: []), "bias": bias})

            def put(y0, onto=None):
                def finish(dve, it, un, u_, q0, qn, product, factor):
                    dst = y_tm[:, un["i"], bass.ds(it * P + (y0 + DH * un["hh"]), DH)]
                    if onto is not None and onto(un):
                        if "comp" in un:
                            dve.wait_ge(S["stored"].sem, S["stored"].at(layer, it * 16 + (64 + u_)))
                        return nc.vector.scalar_tensor_tensor(out=dst, in0=product, scalar=factor, in1=dst,
                                                              op0=ALU.mult, op1=ALU.add)
                    return nc.vector.tensor_scalar(dst, product, factor, None, ALU.mult)
                return finish

            def gate(branch):
                return lambda it, un: M["gates"][:, un["i"], bass.ds(it * 2 + (4 * branch + un["hh"]), 1)]

            def put_compressed(dve, it, un, u_, q0, qn, product, factor):
                dst = y_tm[:, un["i"], bass.ds(it * P + (Y_NS + DH * un["hh"]), DH)]
                return nc.vector.tensor_scalar(dst, product, factor, gate(0)(it, un), ALU.mult, ALU.mult)

            with nc.Block() as block:
                @block.sync
                def _(sp):
                    sp.dma_start(cols[:, :], A["cols_b"][layer]).then_inc(S["cols_in"].sem, 16)
                    first_slots(sp, ring, lambda j: A["win_b"][layer, j])
                    sp.wait_ge(S["cols_in"].sem, S["cols_in"].at(layer, 1))
                    pass_waits(sp, S)

            norm_stage(nc, S, layer, 0, TB, h, col("attn_g"), u)
            linear_stage(nc, S, ring, layer, TB, A["win_b"], 8, u, 0, 0, 0, lambda j: A["wv_b"][layer, j], out=M["fm"])
            token_major_stage(nc, S, ring, layer, A, M)
            stick_stage(nc, S, layer, M)
            prepare_stage(nc, S, ring, layer, A, M)
            at_v = lambda v0: (lambda it, un, j, sn: v_tm[:, j, bass.ds(it * P + (v0 + DH * un["hh"]), DH)])
            softmax_pass(0, 0, by_head, lambda it: it * 2 + T_MB, -DH ** -0.5, 0, lambda it, un: ones[:, 0:1],
                         put(Y_MB), at_v(V_MB), k_tile=lambda it: it * 2 + (T_MB + 1))
            softmax_pass(16, 2, by_head, lambda it: it + T_NSQ, -DH ** -0.5, None,
                         lambda it, un: M["valid"][:, un["i"]:un["i"] + 1], put_compressed,
                         lambda it, un, j, sn: M["v_cmp"][:, :], k=M["k_cmp"],
                         keys=lambda i: (N_CMP, [(0, N_CMP)]), compressed=True)
            select_stage(nc, S, layer, M)
            softmax_pass(32, 4, by_head, lambda it: it + T_NSQ, -DH ** -0.5, HEADS_B, gate(1),
                         put(Y_NS, lambda un: True), lambda it, un, j, sn: v_tm[:, j, V_SLC:V_SLC + DH], k=M["k_slc"],
                         more=lambda it, un, q0, qn: [(M["not_sel"][:, q0:q0 + qn], lambda a, b: M["blocks"][:, a:b])])
            softmax_pass(48, 6, by_head, lambda it: it + T_NSQ, -DH ** -0.5, HEADS_B, gate(2),
                         put(Y_NS, lambda un: True), lambda it, un, j, sn: v_tm[:, j, V_WIN:V_WIN + DH], k=M["k_win"])
            softmax_pass(64, 8, by_half, lambda it: it * 2 + T_DF, -32 ** -0.5, 2 * HEADS_B,
                         lambda it, un: M["neg_lam"][:, 0:1] if un["comp"] else ones[:, 0:1],
                         put(Y_DF, lambda un: un["comp"] == 1), at_v(V_DF), k_tile=lambda it: it * 2 + (T_DF + 1))
            diff_norm_stage(nc, S, layer, M)
            turn_heads_stage(nc, S, layer, y_tm, y, 8, Q_TILES_B, 0)
            linear_stage(nc, S, ring, layer, TB, A["wout_b"], 4, y, 16, 36, 20, lambda j: A["wup_b"][layer, j],
                         evacuate="add", out=h)
            norm_stage(nc, S, layer, 1, TB, h, col("mlp_g"), u)
            linear_stage(nc, S, ring, layer, TB, A["wup_b"], 16, u, 20, 44, 32, lambda j: A["wdown_b"][layer, j],
                         evacuate="relu2", out=M["hid"])
            linear_stage(nc, S, ring, layer, TB, A["wdown_b"], 16, M["hid"], 36, 76, 68, None, deep=32,
                         evacuate="add", out=h)

        final_in, out_done = sem("final_in"), sem("out_done")
        with nc.Block() as block:
            @block.sync
            def _(sp):
                sp.dma_start(cols[:, 0:KD], A["final_g"]).then_inc(final_in, 16)
                sp.wait_ge(final_in, 16)
        norm_stage(nc, S, DEPTH, 0, TB, h, cols[:, 0:KD], u)
        with nc.Block() as block:
            @block.sync
            def _(sp):
                sp.dma_start(out, u[:, :, :]).then_inc(out_done, 16)
                sp.wait_ge(out_done, 16)


def constants_b():
    dist = np.arange(-LAST_DIST, TB)
    n = np.maximum(dist, 0)
    exact = N_BUCKETS // 2
    nf = np.maximum(n, 1).astype(np.float32)
    large = exact + (np.log(nf / np.float32(exact)) / np.float32(np.log(128 / exact))
                     * np.float32(N_BUCKETS - exact)).astype(np.int32)
    bucket = np.where(n < exact, n, np.minimum(large, N_BUCKETS - 1))
    fwd = np.zeros((N_BUCKETS + 1, 1024), np.float32)
    for x, (d, b) in enumerate(zip(dist, bucket)):
        fwd[b if d >= 0 else N_BUCKETS, x] = -1.0 if d >= 0 else NEG
    rev = np.zeros((N_BUCKETS + 1, ROW_LEN), np.float32)
    rev[:, 0:639] = fwd[:, 2 * LAST_DIST - np.arange(639)]
    p, c = np.arange(P)[:, None], np.arange(P)[None, :]
    out = {"onehot_fwd": fwd, "reverse": np.eye(P)[::-1], "onehot_rev": rev, "tri": np.where(p >= c, -1, 0), "neg_ones": np.full((P, P), -1),
           "mask01": np.where(c > p, 1, 0), "mask_add": np.where(c > p, 0, -NEG)}
    start, s0 = np.arange(N_CMP) * CMP_STRIDE, np.arange(N_SLC) * SLC_LEN
    lo = np.maximum(start[:, None], s0[None])
    hi = np.minimum(start[:, None] + CMP_LEN - 1, s0[None] + SLC_LEN - 1)
    out["cover"] = np.clip(hi - lo + 1, 0, None) / CMP_LEN
    out["blocks"] = np.kron(np.eye(N_SLC), np.full((1, SLC_LEN), NEG))
    own = (np.arange(TB) // SLC_LEN).reshape(4, P).T[:, :, None]
    j = np.arange(N_SLC)[None, None]
    out["imp_scale"] = (j < own).astype(np.float32).reshape(P, -1)
    out["imp_add"] = np.where(j == own, NEG, np.where(j < own, 0, -NEG)).reshape(P, -1)
    out["tri8"] = np.tile((np.arange(8)[None, :] < np.arange(8)[:, None]).reshape(1, -1), (P, 1))
    valid = np.ones((P, 4))
    valid[:CMP_LEN - 1, 0] = 0
    out["valid"] = valid
    return {k: np.ascontiguousarray(v.astype(np.float32)) for k, v in out.items()}


def pack_b(i):
    w = i["w_in_2"]
    sizes = [256] * 7 + [64] * 6 + [12] + [256] * 3
    at = np.cumsum([0] + sizes)
    (sbq, sbk, sbv, mbq, mbk, mbv, nsq, kc, vc, ks, vs, kw, vw, g, dfq, dfk, dfv) = (
        w[..., a:b] for a, b in zip(at[:-1], at[1:]))
    fm = np.concatenate([interleave(sbq, sbk), interleave(mbq, mbk), interleave(dfq, dfk), nsq, kc, vc, ks, kw], -1)
    pad = np.zeros(g.shape[:2] + (1024 - V_G - 12,), np.float32)
    tm = np.concatenate([sbv, mbv, dfv, vs, vw, g, pad], -1)

    def first_layer(w1):
        return w1.reshape(DEPTH, 2, 8, P, CMP_HID).transpose(0, 1, 3, 2, 4).reshape(DEPTH, 2, P, 8 * CMP_HID)

    def by_tile(v):
        n, k, m = v.shape
        return v.reshape(n, k // P, P, m).transpose(0, 2, 1, 3).reshape(n, P, -1)

    pos = np.concatenate([i[n].reshape(DEPTH, 16, 2, DH).transpose(0, 3, 2, 1) for n in ("cmp_pos_k_2", "cmp_pos_v_2")], 1)
    rep = lambda v: np.broadcast_to(v.reshape(DEPTH, 1, -1), (DEPTH, P, v.reshape(DEPTH, -1).shape[1]))
    init = np.array([0.8 - 0.6 * np.exp(-0.3 * l) for l in range(DEPTH)], np.float64)
    w2k = i["cmp_k_w2_2"]
    cols = {"attn_g": feature_columns(i["norm_attn_2"]), "mlp_g": feature_columns(i["norm_mlp_2"]),
            "pos": pos.reshape(DEPTH, P, 32), "w2k": by_tile(np.concatenate([w2k, w2k], -1)),
            "w2v": by_tile(i["cmp_v_w2_2"]), "lambda": rep(i["diff_lambda_2"]),
            "neg_lambda_init": rep((-init).astype(np.float32)), "one_less_init": rep((1 - init).astype(np.float32)),
            "subln": rep(i["diff_subln_2"])}
    return {**constants_b(), "win_b": by_pairs(fm), "wv_b": by_columns(tm),
            "wcmp": np.concatenate([first_layer(i["cmp_k_w1_2"]), first_layer(i["cmp_v_w1_2"])], 1),
            "wout_b": by_pairs(i["w_out_2"]), "wup_b": by_pairs(i["w_up_2"]), "wdown_b": by_halves(i["w_down_2"]),
            "rel_bias": i["rel_bias_2"], "final_g": np.ascontiguousarray(feature_columns(i["final_norm_2"][None])[0]),
            "cols_b": np.concatenate([cols[n] for n in COLS_B], -1)}


def constants():
    c = {"ident": np.eye(P), "mean_mat": np.full((P, P), 1 / D), "mean256": np.full((P, P), 1 / 256)}
    c["mean64"] = np.kron(np.eye(2), np.full((64, 64), 1 / 64))
    p, col = np.arange(P)[:, None], np.arange(P)[None, :]
    mask = np.zeros((P, TA + META))
    mask[:, TA - P:TA] = np.where(col > p, NEG, 0)
    mask[:, TA:] = np.where(np.arange(META)[None, :] > p, NEG, 0)
    c["mask_a"] = mask
    return {k: np.ascontiguousarray(v.astype(np.float32)) for k, v in c.items()}


def by_pairs(w):
    n, k, m = w.shape
    w = w.reshape(n, k // P, P, m // (2 * P), 2, P).transpose(0, 3, 2, 4, 1, 5)
    return np.ascontiguousarray(w).reshape(n, m // (2 * P), P, 2 * (k // P) * P)


def by_halves(w):
    n, k, m = w.shape
    w = w.reshape(n, 2, k // (2 * P), P, m // P, P).transpose(0, 4, 1, 3, 2, 5)
    return np.ascontiguousarray(w).reshape(n, 2 * m // P, P, (k // (2 * P)) * P)


def by_columns(w):
    n, k, m = w.shape
    w = w.reshape(n, k // P, P, m // 256, 256).transpose(0, 3, 2, 1, 4)
    return np.ascontiguousarray(w).reshape(n, m // 256, P, (k // P) * 256)


def feature_columns(v):
    return np.ascontiguousarray(v.reshape(v.shape[0], -1, P).transpose(0, 2, 1))


def tap_columns(w):
    n, taps, c = w.shape
    return np.ascontiguousarray(w.reshape(n, taps, c // P, P).transpose(0, 3, 2, 1)).reshape(n, P, -1)


def interleave(a, b):
    n, k, m = a.shape
    return np.stack([a.reshape(n, k, -1, P), b.reshape(n, k, -1, P)], 3).reshape(n, k, 2 * m)


def pack_a(i):
    w = i["w_in"]
    q, k, v = w[..., :512], w[..., 512:1024], w[..., 1024:1536]
    f, rest = w[..., 1536:1544], w[..., 1544:]
    val, gate, sb_, sc_, sx = (rest[..., 256 * n:256 * (n + 1)] for n in range(5))
    fpad = np.concatenate([f, np.zeros(f.shape[:2] + (248,), np.float32)], -1)
    branches = by_pairs(np.concatenate([gate, val, sc_, sx, sb_, fpad], -1))
    out = {"win": np.concatenate([branches, by_pairs(interleave(q, k)), by_columns(v)], 1),
           "wout": by_pairs(i["w_out"]),
           "wup": by_pairs(interleave(i["ffn_w_up"][..., :D_FF], i["ffn_w_up"][..., D_FF:])),
           "wdown": by_halves(i["ffn_w_down"])}
    bf = np.zeros((DEPTH, P, 1), np.float32)
    bf[:, :HEADS_A, 0] = i["b_forget"]
    pw = i["a_pw_w"].reshape(DEPTH, 2, P, 256).transpose(0, 2, 1, 3).reshape(DEPTH, P, 512)
    cols = {"mix_pre": feature_columns(i["mix_pre_g"]), "mix_post": feature_columns(i["mix_post_g"]),
            "ffn_pre": feature_columns(i["ffn_pre_g"]), "ffn_post": feature_columns(i["ffn_post_g"]),
            "head_g": feature_columns(i["head_g"]), "dw_b": feature_columns(i["a_dw_b"]),
            "ln_g": feature_columns(i["a_ln_g"]), "ln_b": feature_columns(i["a_ln_b"]),
            "dw_w": tap_columns(i["a_dw_w"]), "sc_w": tap_columns(i["sc_conv_w"]),
            "ff_w": tap_columns(interleave(i["ffn_conv_w"][..., :D_FF], i["ffn_conv_w"][..., D_FF:])),
            "b_forget": bf, "pw_w": pw}
    out["cols_a"] = np.concatenate([cols[n] for n in COLS_A], -1)
    x = np.concatenate([i["meta_tokens"][None], i["x"]], 1)[0]
    out["x"] = x.T.reshape(KD, P, TA).transpose(1, 0, 2)
    return out


def build(nc, A, out):
    with ExitStack() as ctx:
        def sb(name, shape):
            return ctx.enter_context(nc.sbuf_tensor(name, shape, F32))

        h = sb("h", [P, KD, TA])
        ring = sb("ring", [P, 2, SLOT])
        psum = ctx.enter_context(nc.psum_tensor("psum", [P, 8, 512], F32))
        consts = {n: sb(n, [P, P]) for n in ("ident", "mean_mat", "mean256", "mean64")}
        consts["ones"] = sb("ones", [P, TA])
        consts["eps5"], consts["eps6"] = sb("eps5", [P, 1]), sb("eps6", [P, 1])
        consts["neg_max"], consts["total"] = sb("neg_max", [P, 4]), sb("total", [P, 6])
        consts["factor"] = sb("factor", [P, 4])
        loaded = ctx.enter_context(nc.semaphore("loaded"))
        consts["passed"] = ctx.enter_context(nc.semaphore("passed"))
        G = {"ring": ring, "psum": psum, "consts": consts}
        names = ("ident", "mean_mat", "mean256", "mean64")
        with nc.Block() as block:
            @block.sync
            def _(sp):
                sp.dma_start(h[:, :, :], A["x"]).then_inc(loaded, 16)
                for n in names:
                    sp.dma_start(consts[n][:, :], A[n]).then_inc(loaded, 16)
                sp.wait_ge(loaded, 16 * (1 + len(names)))

            @block.vector
            def _(dve):
                nc.vector.memset(consts["ones"][:, :], 1.0)
                nc.vector.memset(consts["eps5"][:, :], 1e-5)
                nc.vector.memset(consts["eps6"][:, :], 1e-6)
        first_stack(nc, G, A, h)
        second_stack(nc, G, A, h, out)


def kernel(**inputs):
    import concourse.bacc as bacc
    from concourse.bass_utils import run_bass_kernel_spmd

    nc = bacc.Bacc("TRN2", target_bir_lowering=False, num_devices=1)
    inputs = {k: np.ascontiguousarray(v) for k, v in inputs.items()}
    arrays = {**constants(), **pack_a(inputs), **pack_b(inputs)}
    arrays = {f"in_{k}": np.ascontiguousarray(v) for k, v in arrays.items()}
    A = {k[3:]: nc.dram_tensor(k, v.shape, mybir.dt.from_np(v.dtype), kind="ExternalInput").ap()
         for k, v in arrays.items()}
    out = nc.dram_tensor("out", (P, KD, OUT_TOKENS), F32, kind="ExternalOutput").ap()
    build(nc, A, out)
    r = run_bass_kernel_spmd(nc, [arrays], core_ids=[0])
    got = r.results[0]["out"]
    return np.ascontiguousarray(got.transpose(2, 1, 0)).reshape(1, OUT_TOKENS, D)
```

```python
from contextlib import ExitStack, nullcontext

import numpy as np

import concourse.bass as bass
from concourse import mybir

F32 = mybir.dt.float32
F32R = mybir.dt.float32r
ALU = mybir.AluOpType
ACT = mybir.ActivationFunctionType
AX_X = mybir.AxisListType.X

P = 128
D = 1024
KD = D // P
DEPTH = 2
SEQ, META = 512, 16
TA = SEQ + META
HALF_A = TA // 2
NEG = 1e30
DH = 64

HEADS_A = 8
TAPS_LONG, TAPS_SHORT = 31, 3
D_FF = 2816
FF_PAIRS = D_FF // P
Q_TILES_A = [(0, META)] + [(META + P * i, P) for i in range(SEQ // P)]
SLOTS_A = 54
TB = SEQ
HEADS_B = 4
Q_TILES_B = [(P * i, P) for i in range(TB // P)]
FF2 = 4096
N_CMP = 31
CMP_LEN, CMP_STRIDE, CMP_HID = 32, 16, 256
N_BUCKETS = 32
N_SLC, SLC_LEN, SLC_TOP = 8, 64, 4
TINY = 1e-30
SLOTS_B = 52
LN_EXP_TABLES = 6
UNIT = P
SLOT = 16 * UNIT


class Signal:

    def __init__(self, sem, per_layer, step=1):
        self.sem, self.per_layer, self.step = sem, per_layer, step

    def at(self, layer, n):
        return layer * (self.per_layer * self.step) + n * self.step


def pass_waits(eng, S):
    eng.sem_inc(S["passed"], 1)


def chunks(t):
    return [(0, t)] if t <= 512 else [(0, t // 2), (t // 2, t - t // 2)]


def banks(ps, b, t):
    if t <= 512:
        return ps[:, b, 0:t]
    return ps[:, b:b + 2, 0:t // 2]


def split(ap, t):
    return ap if t <= 512 else ap.rearrange("p (c n) -> p c n", c=2)


class Scope:

    def __init__(self, nc, ctx):
        self.nc, self.ctx = nc, ctx

    def sb(self, name, shape, dtype=F32):
        return self.ctx.enter_context(self.nc.sbuf_tensor(name, shape, dtype))

    def parts(self, name, *shape):
        return self.sb(name + "_hi", [P, *shape], F32R), self.sb(name + "_lo", [P, *shape], F32R)


def ring_feed(eng, ring, layer, base, freed, release, source, then):
    tiles, full = ring["tiles"], ring["full"]
    count, src = source
    if count > 2:
        with eng.Fori(0, count // 2 - 1) as it:
            for s in range(2):
                eng.wait_ge(freed.sem, freed.at(layer, release(it * 2 + s)))
                w = src(it * 2 + (2 + s))
                eng.dma_start(tiles[:, s, 0:w.shape[-1]], w).then_inc(full[s], 16)
    if then is not None:
        for s in range(2):
            eng.wait_ge(freed.sem, freed.at(layer, release(count - 2 + s)))
            w = then(s)
            eng.dma_start(tiles[:, s, 0:w.shape[-1]], w).then_inc(full[s], 16)


def first_slots(eng, ring, source):
    for s in range(2):
        w = source(s)
        eng.dma_start(ring["tiles"][:, s, 0:w.shape[-1]], w).then_inc(ring["full"][s], 16)


def slot_full(ring, layer, base, j):
    return layer * (ring["per_layer"] // 2 * 16) + (j * 16 + (base // 2 + 1) * 16)


def weight_high(nc, act, W, layer, buf, slot, at, n, full_at, used):
    act.wait_ge(W["full"][slot], full_at)
    act.wait_ge(W["mm_done"].sem, W["mm_done"].at(layer, used))
    nc.scalar.activation(W["hi"][:, buf, 0:n], W["tiles"][:, slot, at:at + n], ACT.Copy).then_inc(W["w_hi"].sem, 1)


def weight_low(nc, dve, W, layer, buf, slot, at, n, part):
    dve.wait_ge(W["w_hi"].sem, W["w_hi"].at(layer, part))
    nc.vector.tensor_tensor(W["lo"][:, buf, 0:n], W["tiles"][:, slot, at:at + n], W["hi"][:, buf, 0:n].bitcast(F32),
                            ALU.subtract).then_inc(W["w_lo"].sem, 1)


def product(nc, out, a, b, start, stop):
    (a_hi, a_lo), n = a, len(b)
    for c, (b_hi, b_lo) in enumerate(b):
        nc.tensor.matmul(out[c], a_hi, b_hi, start=start, stop=False)
        nc.tensor.matmul(out[c], a_hi, b_lo, start=False, stop=False)
    for c, (b_hi, _) in enumerate(b):
        mm = nc.tensor.matmul(out[c], a_lo, b_hi, start=False, stop=stop)
    return mm


def load_ln_and_exp(nc, act):
    act.add_instruction(mybir.InstLoadActFuncSet(act_func_set_id=LN_EXP_TABLES, name=nc.get_next_instruction_name()))


def in_loop(eng, n):
    return eng.Fori(0, n) if n > 1 else nullcontext(0)


def in_rounds(eng, n, body):
    if n > 1:
        with eng.Fori(0, n - 1) as it:
            body(it, False)
    body(n - 1, True)


def norm_stage(nc, S, layer, use, T, x, gain, out, residual=None, plain=False):
    ps, sq, rstd = S["psum"], S["scratch"], S["rstd"]
    in_parts = residual is None and not plain
    value = sq if in_parts else out
    with nc.Block() as block:
        @block.scalar
        def _(act):
            for k in range(KD):
                nc.scalar.activation(sq[:, k, 0:T], x[:, k, 0:T], ACT.Square).then_inc(S["squared"].sem, 1)
            act.wait_ge(S["summed"].sem, S["summed"].at(layer, use + 1))
            nc.scalar.activation(split(rstd[:, 0:T], T), banks(ps, 0, T), ACT.Ln,
                                 bias=S["eps6"][:, 0:1]).then_inc(S["rooted"].sem, 1)
            act.wait_ge(S["rooted"].sem, S["rooted"].at(layer, use + 1))
            nc.scalar.activation(rstd[:, 0:T], rstd[:, 0:T], ACT.Exp, scale=-0.5).then_inc(S["rstd_ready"].sem, 1)
            if in_parts:
                for k in range(KD):
                    act.wait_ge(S["scaled"].sem, S["scaled"].at(layer, KD * use + k + 1))
                    nc.scalar.activation(out[0][:, k, 0:T], sq[:, k, 0:T], ACT.Copy).then_inc(S["rounded"].sem, 1)

        @block.tensor
        def _(pe):
            for k in range(KD):
                pe.wait_ge(S["squared"].sem, S["squared"].at(layer, KD * use + k + 1))
                for c, (c0, cn) in enumerate(chunks(T)):
                    last = nc.tensor.matmul(ps[:, c, 0:cn], S["mean_mat"][:, :], sq[:, k, c0:c0 + cn],
                                            start=(k == 0), stop=(k == KD - 1))
            last.then_inc(S["summed"].sem, 1)

        @block.vector
        def _(dve):
            dve.wait_ge(S["rstd_ready"].sem, S["rstd_ready"].at(layer, use + 1))
            for k in range(KD + 2):
                if k < KD:
                    nc.vector.scalar_tensor_tensor(out=value[:, k, 0:T], in0=x[:, k, 0:T], scalar=gain[:, k:k + 1],
                                                   in1=rstd[:, 0:T], op0=ALU.mult,
                                                   op1=ALU.mult).then_inc(S["scaled"].sem, 1)
                if k >= 2 and residual is not None:
                    dve.wait_ge(S["scaled"].sem, S["scaled"].at(layer, KD * use + k - 1))
                    nc.vector.tensor_tensor(residual[:, k - 2, 0:T], residual[:, k - 2, 0:T], out[:, k - 2, 0:T], ALU.add)
                elif k >= 2 and in_parts:
                    dve.wait_ge(S["rounded"].sem, S["rounded"].at(layer, KD * S["split_norm"][use] + k - 1))
                    nc.vector.tensor_tensor(out[1][:, k - 2, 0:T], sq[:, k - 2, 0:T],
                                            out[0][:, k - 2, 0:T].bitcast(F32), ALU.subtract)


def linear_stage(nc, S, W, layer, T, weights, slots, x, base, mm_base, part_base, free_base, then,
                 units=KD, tile_parts=1, evacuate="copy", out=None, out_parts=None):
    ps, mm_done, free, w_lo = S["psum"], W["mm_done"], S["psum_free"], W["w_lo"]
    per_slot = 2 if units == KD else 1
    lots, bufs = slots * per_slot, 4 // tile_parts
    rounds, wide, n = lots // 4, 2 if T > 512 else 1, units * UNIT
    x_hi, x_lo = x

    def lot(j, it):
        q = j // per_slot
        return (j % 2, q % 2, (j % per_slot) * n), slot_full(W, layer, base, it * (2 // per_slot) + q // 2)

    with nc.Block() as block:
        @block.sync
        def _(sp):
            ring_feed(sp, W, layer, base, w_lo, lambda j: j * per_slot + (part_base + per_slot),
                      (slots, weights), then)

        @block.tensor
        def _(pe):
            with pe.Fori(0, rounds) as it:
                for j in range(4):
                    b, first, last = j // tile_parts, j % tile_parts == 0, (j + 1) % tile_parts == 0
                    if first:
                        pe.wait_ge(free.sem, free.at(layer, it * bufs + (free_base + b + 1)))
                    pe.wait_ge(w_lo.sem, w_lo.at(layer, it * 4 + (part_base + j + 1)))
                    for k in range(units):
                        kx, cols = (j % tile_parts) * units + k, slice(k * UNIT, (k + 1) * UNIT)
                        mm = product(nc, [ps[:, wide * b + c, 0:cn] for c, (_, cn) in enumerate(chunks(T))],
                                     (W["hi"][:, j % 2, cols], W["lo"][:, j % 2, cols]),
                                     [(x_hi[:, kx, c0:c0 + cn], x_lo[:, kx, c0:c0 + cn]) for c0, cn in chunks(T)],
                                     first and k == 0, last and k == units - 1)
                    mm.then_inc(mm_done.sem, 1)

        @block.scalar
        def _(act):
            def high(it, j):
                (buf, slot, at), full_at = lot(j, it)
                weight_high(nc, act, W, layer, buf, slot, at, n, full_at, it * 4 + (mm_base + j - 1))

            def step(it, last):
                for j in range(4):
                    if not last or j < 2:
                        high(it, j + 2)
                    if evacuate == "add" or (j + 1) % tile_parts:
                        continue
                    b = j // tile_parts
                    act.wait_ge(mm_done.sem, mm_done.at(layer, it * 4 + (mm_base + j + 1)))
                    if evacuate == "copy":
                        nc.scalar.activation(split(out[:, it * bufs + b, 0:T], T), banks(ps, wide * b, T),
                                             ACT.Copy).then_inc(free.sem, 1)
                    else:
                        act.wait_ge(S["sq_out"].sem, S["sq_out"].at(layer, it * 4 + (S["sq_base"] + b + 1)))
                        nc.scalar.activation(out[:, b, 0:T], banks(ps, wide * b, T), ACT.Relu).then_inc(free.sem, 1)
                        act.wait_ge(S["sq_done"].sem, S["sq_done"].at(layer, it * 4 + (S["sq_base2"] + b + 1)))
                        nc.scalar.activation(out_parts[0][:, it * 4 + b, 0:T], out[:, b, 0:T],
                                             ACT.Copy).then_inc(S["sq_high"].sem, 1)

            if evacuate != "add":
                act.sem_inc(free.sem, bufs)
            high(0, 0)
            high(0, 1)
            in_rounds(act, rounds, step)

        @block.vector
        def _(dve):
            def low(it, j):
                (buf, slot, at), _ = lot(j, it)
                weight_low(nc, dve, W, layer, buf, slot, at, n, it * 4 + (part_base + j + 1))

            def step(it, last):
                for j in range(4):
                    if not last or j < 2:
                        low(it, j + 2)
                    if evacuate == "copy" or (j + 1) % tile_parts:
                        continue
                    b = j // tile_parts
                    if evacuate == "add":
                        dve.wait_ge(mm_done.sem, mm_done.at(layer, it * 4 + (mm_base + j + 1)))
                        o = split(out[:, it * bufs + b, 0:T], T)
                        nc.vector.tensor_tensor(o, banks(ps, wide * b, T), o, ALU.add).then_inc(free.sem, 1)
                    else:
                        dve.wait_ge(free.sem, free.at(layer, it * 4 + (free_base + 4 + b + 1)))
                        nc.vector.tensor_tensor(out[:, b, 0:T], out[:, b, 0:T], out[:, b, 0:T],
                                                ALU.mult).then_inc(S["sq_done"].sem, 1)
                        dve.wait_ge(S["sq_high"].sem, S["sq_high"].at(layer, it * 4 + (S["sq_base2"] + b + 1)))
                        nc.vector.tensor_tensor(out_parts[1][:, it * 4 + b, 0:T], out[:, b, 0:T],
                                                out_parts[0][:, it * 4 + b, 0:T].bitcast(F32),
                                                ALU.subtract).then_inc(S["sq_out"].sem, 1)

            if evacuate == "add":
                dve.sem_inc(free.sem, bufs)
            if evacuate == "relu2":
                dve.sem_inc(S["sq_out"].sem, 4)
            low(0, 0)
            low(0, 1)
            in_rounds(dve, rounds, step)


def softmax_stage(nc, S, layer, C):
    ps, ident = S["psum"], S["ident"]
    N, Pb, PT, neg_max, total = S["N"], S["P"], S["PT"], S["neg_max"], S["total"]
    scores, shifted, probs = S["scores"], S["shifted"], S["probs"]
    inverted, factor = S["inverted"], S["factor"]
    turned, turned_out, mixed, stored, staged = (
        S.get(x) for x in ("turned", "turned_out", "mixed", "stored", "staged"))
    units, U, tiles, stages = C["units"], len(C["units"]), C["q_tiles"], C["stages"]
    narrow = C["T"] <= 512
    banks_n, n_bufs, p_bufs, lag = (4, 4, 4, 3) if narrow else (2, 2, 3, 2)

    def count(sig, it, u):
        return sig.at(layer, it * U + (C["base"] + u + 1))

    def score_view(u, qn, n):
        if n <= 512:
            return ps[0:qn, u % 4 if narrow else 2 * (u % 2), 0:n]
        return ps[0:qn, 2 * (u % 2):2 * (u % 2) + 2, 0:n // 2]

    def n_view(ap, n):
        return ap if n <= 512 else ap.rearrange("p (c n) -> p c n", c=2)

    def turned_at(u, j, sn, qn):
        if narrow:
            return ps[0:sn, 4 + u % 2, P * j:P * j + qn]
        return ps[0:sn, 5, 0:qn] if j == 0 else ps[0:sn, 4, P * (j - 1):P * (j - 1) + qn]

    def mixed_at(u, qn):
        return ps[0:qn, 6 + u % 2, 0:DH]

    with nc.Block() as block:
        @block.tensor
        def _(pe):
            def score(it, u):
                q0, qn = tiles[units[u]["i"]]
                n, _ = C["keys"](units[u])
                if u >= banks_n:
                    pe.wait_ge(shifted.sem, count(shifted, it, u - banks_n))
                if qn < P or u == 0:
                    pass_waits(pe, S)
                terms = [(C["q"](units[u], q0, qn), lambda a, b: C["k"](units[u], a, b))] + C["more"](it, units[u], q0, qn)
                for c, (c0, cn) in enumerate(chunks(n)):
                    for m, (lhs, rhs) in enumerate(terms):
                        mm = nc.tensor.matmul(ps[0:qn, u % 4 if narrow else 2 * (u % 2) + c, 0:cn], lhs, rhs(c0, c0 + cn),
                                              start=(m == 0), stop=(m == len(terms) - 1))
                mm.then_inc(scores.sem, 1)

            def turn(it, u):
                q0, qn = tiles[units[u]["i"]]
                _, keys = C["keys"](units[u])
                pe.wait_ge(probs.sem, count(probs, it, u))
                back = 2 if narrow else 1
                if u >= back:
                    pe.wait_ge(turned_out.sem, count(turned_out, it, u - back))
                if qn < P:
                    pass_waits(pe, S)
                for j, (s0, sn) in enumerate(keys):
                    mm = nc.tensor.transpose(turned_at(u, j, sn, qn), Pb[0:qn, u % p_bufs, s0:s0 + sn],
                                             ident[0:qn, 0:qn])
                mm.then_inc(turned.sem, 1)

            def mix(it, u):
                q0, qn = tiles[units[u]["i"]]
                _, keys = C["keys"](units[u])
                pe.wait_ge(turned_out.sem, count(turned_out, it, u))
                if u >= 2:
                    pe.wait_ge(stored.sem, count(stored, it, u - 2))
                if keys[0][1] < P:
                    pass_waits(pe, S)
                for j, (s0, sn) in enumerate(keys):
                    mm = nc.tensor.matmul(mixed_at(u, qn), PT[0:sn, u % 2, P * j:P * j + qn],
                                          C["v"](it, units[u], j, sn), start=(j == 0), stop=(j == len(keys) - 1))
                mm.then_inc(mixed.sem, 1)

            with in_loop(pe, C["rounds"]) as it:
                for u in range(U + lag + 1):
                    if u in stages:
                        pe.wait_ge(staged.sem, staged.at(layer, it * len(stages) + stages.index(u) + 1))
                    if u < U:
                        score(it, u)
                    if lag <= u < U + lag:
                        turn(it, u - lag)
                    if u > lag:
                        mix(it, u - lag - 1)
                pe.wait_ge(stored.sem, count(stored, it, U - 1))

        @block.vector
        def _(dve):
            def shift(it, u):
                q0, qn = tiles[units[u]["i"]]
                n, _ = C["keys"](units[u])
                if u >= n_bufs:
                    dve.wait_ge(probs.sem, count(probs, it, u - n_bufs))
                dve.wait_ge(scores.sem, count(scores, it, u))
                pass_waits(dve, S)
                nc.vector.tensor_tensor_reduce(n_view(N[0:qn, u % n_bufs, 0:n], n), score_view(u, qn, n),
                                               n_view(C["bias"](units[u], qn, n), n), 1.0, 3e38, ALU.add,
                                               ALU.min, neg_max[0:qn, u % 4:u % 4 + 1]).then_inc(shifted.sem, 1)

            def invert(it, u):
                q0, qn = tiles[units[u]["i"]]
                dve.wait_ge(probs.sem, count(probs, it, u))
                C["invert"](dve, it, units[u], u, qn, factor[0:qn, u % 4:u % 4 + 1],
                            total[0:qn, u % 6:u % 6 + 1])

            with in_loop(dve, C["rounds"]) as it:
                for u in range(U + lag + 2):
                    if 3 <= u < U + 3:
                        invert(it, u - 3)
                    for n, at in enumerate(stages):
                        if u == max(at - 6, 0):
                            C["stage"](it, n).then_inc(staged.sem, 1)
                    if u < U:
                        shift(it, u)
                    if u >= lag + 2:
                        done = u - lag - 2
                        q0, qn = tiles[units[done]["i"]]
                        dve.wait_ge(mixed.sem, count(mixed, it, done))
                        dve.wait_ge(inverted.sem, count(inverted, it, done))
                        C["finish"](dve, it, units[done], done, q0, qn, mixed_at(done, qn),
                                    factor[0:qn, done % 4:done % 4 + 1]).then_inc(stored.sem, 1)

        @block.scalar
        def _(act):
            def exponent(it, u):
                q0, qn = tiles[units[u]["i"]]
                n, _ = C["keys"](units[u])
                if u >= p_bufs:
                    act.wait_ge(turned.sem, count(turned, it, u - p_bufs))
                if u >= 6:
                    act.wait_ge(stored.sem, count(stored, it, u - 6))
                act.wait_ge(shifted.sem, count(shifted, it, u))
                nc.scalar.activation(Pb[0:qn, u % p_bufs, 0:n], N[0:qn, u % n_bufs, 0:n], ACT.Exp,
                                     bias=neg_max[0:qn, u % 4:u % 4 + 1], scale=-1.0,
                                     accum_out=total[0:qn, u % 6:u % 6 + 1]).then_inc(probs.sem, 1)

            def copy_turned(it, u):
                q0, qn = tiles[units[u]["i"]]
                _, keys = C["keys"](units[u])
                act.wait_ge(turned.sem, count(turned, it, u))
                if u >= 2:
                    act.wait_ge(mixed.sem, count(mixed, it, u - 2))
                if narrow:
                    sn, nk = keys[0][1], len(keys)
                    last = nc.scalar.activation(PT[0:sn, u % 2, 0:P * nk], ps[0:sn, 4 + u % 2, 0:P * nk], ACT.Copy)
                else:
                    last = nc.scalar.activation(PT[0:META, u % 2, 0:qn], turned_at(u, 0, META, qn), ACT.Copy)
                    if len(keys) > 1:
                        last = nc.scalar.activation(PT[:, u % 2, P:P * len(keys)],
                                                    ps[:, 4, 0:P * (len(keys) - 1)], ACT.Copy)
                last.then_inc(turned_out.sem, 1)

            with in_loop(act, C["rounds"]) as it:
                for u in range(U + lag):
                    if u < U:
                        exponent(it, u)
                    if u >= lag:
                        copy_turned(it, u - lag)


def turn_heads_stage(nc, S, layer, y_tm, y, pairs, q_tiles, y_low=None):
    ps, ident = S["psum"], S["ident"]
    y_turned, y_out, y_high = S["y_turned"], S["y_out"], S.get("y_high")
    total = sum(n for _, n in q_tiles)
    wide = 2 if total > 512 else 1
    with nc.Block() as block:
        @block.tensor
        def _(pe):
            for f in range(pairs):
                if f >= 2:
                    pe.wait_ge(y_out.sem, y_out.at(layer, f - 1))
                    if wide == 2:
                        pass_waits(pe, S)
                for i, (q0, qn) in enumerate(q_tiles):
                    at = (ps[:, 2 * (f % 2) + 1, 0:qn] if i == 0 else ps[:, 2 * (f % 2), P * (i - 1):P * i]) \
                        if wide == 2 else ps[:, 2 * (f % 2), P * i:P * (i + 1)]
                    mm = nc.tensor.transpose(at, y_tm[0:qn, i, P * f:P * (f + 1)], ident[0:qn, 0:qn])
                mm.then_inc(y_turned.sem, 1)

        @block.scalar
        def _(act):
            for f in range(pairs):
                act.wait_ge(y_turned.sem, y_turned.at(layer, f + 1))
                if wide == 2:
                    nc.scalar.activation(y[:, f, 0:META], ps[:, 2 * (f % 2) + 1, 0:META], ACT.Copy)
                last = nc.scalar.activation(y[:, f, total - SEQ:total], ps[:, 2 * (f % 2), 0:SEQ], ACT.Copy)
                last.then_inc((y_out if y_low is None else y_high).sem, 1)

        if y_low is not None:
            @block.vector
            def _(dve):
                for f in range(pairs):
                    dve.wait_ge(y_high.sem, y_high.at(layer, f + 1))
                    nc.vector.tensor_tensor(y_low[:, f, 0:SEQ], ps[:, 2 * (f % 2), 0:SEQ],
                                            y[:, f, 0:SEQ].bitcast(F32), ALU.subtract).then_inc(y_out.sem, 1)


COLS_A = {}
_at = 0
for _name, _n in (("mix_pre", KD), ("mix_post", KD), ("ffn_pre", KD), ("ffn_post", KD), ("head_g", KD),
                  ("dw_b", 2), ("ln_g", 2), ("ln_b", 2), ("dw_w", 2 * TAPS_LONG), ("sc_w", 2 * TAPS_SHORT),
                  ("ff_w", 2 * FF_PAIRS * TAPS_SHORT), ("b_forget", 1), ("pw_w", 2 * 256)):
    COLS_A[_name] = (_at, _at + _n)
    _at += _n
N_COLS_A = _at
MM_A = 2 + 39 + 8 + 44 + 16
LOTS_A = 23 + 8 + 44 + 16


STEPS_A = {"conv": 2 * TAPS_LONG}
STEPS_A["centred"] = STEPS_A["conv"] + 2
STEPS_A["F"] = STEPS_A["centred"] + 3
STEPS_A["short"] = STEPS_A["F"] + 2 * (TAPS_SHORT + 1)
STEPS_A["normed"] = STEPS_A["short"] + 2


def in_stage_a(nc, S, W, layer, A, M):
    ps, mm_done, w_lo = S["psum"], W["mm_done"], W["w_lo"]
    u_hi, u_lo = M["u"]
    act_out, dve_out, dve_step, f_step = S["act_out"], S["dve_out"], S["dve_step"], S["f_step"]
    ln_pe, ln_act, f_rows = S["ln_pe"], S["ln_act"], S["f_rows"]
    col = M["col"]
    a_pad, p_pad, acc, gate, scc, scb, y = (M[x] for x in ("a_pad", "p_pad", "acc", "gate", "scc", "scb", "y"))
    fx, fa = M["f_sum"], M["fa"]
    mm0, QK, V, N_LOTS = 2, 11, 19, 23
    LOT = KD * UNIT
    V_BANKS = (4, 5, 2, 3, 0)
    TAPS_STATIC = 14

    def buf(t):
        return banks(ps, 2 * (t % 2), TA)

    def slot_of(p):
        return p // 2 if p < QK else 6 + (p - QK) // 2

    def half_of(p):
        return p % 2 if p < QK else (p - QK) % 2

    def used(p):
        return mm0 + p - 1 if p < V + 2 else mm0 + V + 5 * (p - V - 1)

    with nc.Block() as block:
        @block.sync
        def _(sp):
            full = W["full"]
            for j in range(12):
                sp.wait_ge(w_lo.sem, w_lo.at(layer, 2 * j + 2 if j < 5 else QK + 2 * (j - 5)))
                src = A["win"][layer, j + 2] if j < 10 else A["wout"][layer, j - 10]
                sp.dma_start(W["tiles"][:, j % 2, :], src).then_inc(full[j % 2], 16)
                if j == 10:
                    sp.wait_ge(dve_step.sem, dve_step.at(layer, M["steps"]["F"]))
                    sp.dma_start(M["f_left"][HEADS_A:2 * HEADS_A, :], fa[:, :]).then_inc(f_rows.sem, 16)
            sp.wait_ge(f_rows.sem, f_rows.at(layer, 1))
            pass_waits(sp, S)

        @block.tensor
        def _(pe):
            def lot(p, b):
                pe.wait_ge(w_lo.sem, w_lo.at(layer, p + 1))
                for k in range(KD):
                    cols = slice(k * UNIT, (k + 1) * UNIT)
                    mm = product(nc, [ps[:, 2 * b + c, 0:cn] for c, (_, cn) in enumerate(chunks(TA))],
                                 (W["hi"][:, b, cols], W["lo"][:, b, cols]),
                                 [(u_hi[:, k, c0:c0 + cn], u_lo[:, k, c0:c0 + cn]) for c0, cn in chunks(TA)],
                                 k == 0, k == KD - 1)
                mm.then_inc(mm_done.sem, 1)

            reader = {2: (act_out, 1), 3: (act_out, 2), 4: (dve_out, 1), 5: (dve_out, 2), 6: (act_out, 3),
                      7: (act_out, 4), 8: (dve_out, 3), 9: (dve_out, 4), 10: (act_out, 5)}
            for t in range(QK):
                if t in reader:
                    pe.wait_ge(reader[t][0].sem, reader[t][0].at(layer, reader[t][1]))
                lot(t, t % 2)
            pe.wait_ge(act_out.sem, act_out.at(layer, 6))
            pe.wait_ge(dve_out.sem, dve_out.at(layer, 5))
            pass_waits(pe, S)
            with pe.Fori(0, 2) as it:
                for j in range(4):
                    pe.wait_ge(act_out.sem, act_out.at(layer, it * 4 + (5 + j)))
                    lot(it * 4 + (QK + j), (QK + j) % 2)

            def channel_sums(x):
                for j in range(2):
                    for c, (c0, cn) in enumerate(chunks(TA)):
                        mm = nc.tensor.matmul(ps[:, 6 + c, 0:cn], S["mean256"][:, :], x[:, j, c0:c0 + cn],
                                              start=(j == 0), stop=(j == 1))
                mm.then_inc(ln_pe.sem, 1)

            pe.wait_ge(dve_step.sem, dve_step.at(layer, M["steps"]["conv"]))
            channel_sums(acc)
            for s in range(2):
                for half in range(2):
                    p = V + 2 * s + half
                    pe.wait_ge(w_lo.sem, w_lo.at(layer, p + 1))
                    for i, (q0, _) in enumerate(Q_TILES_A):
                        if half == 0 and (s == 1 or i >= 2):
                            pe.wait_ge(act_out.sem, act_out.at(layer, 15 + i if s else 13 + (i >= 4)))
                        for k in range(4):
                            kk, cols = 4 * half + k, slice(k * 256, (k + 1) * 256)
                            mm = product(nc, [ps[:, V_BANKS[i], 0:256]],
                                         (u_hi[:, kk, q0:q0 + P], u_lo[:, kk, q0:q0 + P]),
                                         [(W["hi"][:, p % 2, cols], W["lo"][:, p % 2, cols])],
                                         kk == 0, kk == KD - 1)
                        mm.then_inc(mm_done.sem, 1)
                if s == 0:
                    pe.wait_ge(ln_act.sem, ln_act.at(layer, 2))
                    channel_sums(gate)
            pe.wait_ge(ln_act.sem, ln_act.at(layer, 6))
            pe.wait_ge(act_out.sem, act_out.at(layer, 24))
            for m in range(2):
                for k in range(2):
                    for c, (c0, cn) in enumerate(chunks(TA)):
                        pw = col("pw_w")
                        mm = nc.tensor.matmul(ps[:, 2 * m + c, 0:cn], pw[:, k * 256 + m * P:k * 256 + (m + 1) * P],
                                              acc[:, k, c0:c0 + cn], start=(k == 0), stop=(k == 1))
                mm.then_inc(ln_pe.sem, 1)

        @block.scalar
        def _(act):
            def high(p, it=0):
                s = slot_of(p)
                full_at = slot_full(W, layer, 0, s // 2) if p < QK else slot_full(W, layer, 6, it + (s - 6) // 2)
                weight_high(nc, act, W, layer, p % 2, s % 2, half_of(p) * LOT, LOT, full_at, it * 4 + used(p))

            def take(t, out, func):
                act.wait_ge(mm_done.sem, mm_done.at(layer, mm0 + t + 1))
                nc.scalar.activation(split(out, TA), buf(t), func).then_inc(act_out.sem, 1)

            def take_v(s, i):
                qn = Q_TILES_A[i][1]
                act.wait_ge(mm_done.sem, mm_done.at(layer, mm0 + V + (2 * s + 1) * 5 + i + 1))
                nc.scalar.activation(M["v"][0:qn, i, 256 * s:256 * (s + 1)], ps[0:qn, V_BANKS[i], 0:256],
                                     ACT.Copy).then_inc(act_out.sem, 1)

            high(0)
            high(1)
            takes = {0: (gate, 0, ACT.Sigmoid), 1: (gate, 1, ACT.Sigmoid), 4: (scc, 0, ACT.Copy), 5: (scc, 1, ACT.Copy),
                     8: (scb, 0, ACT.Copy), 9: (scb, 1, ACT.Copy)}
            for t in range(QK):
                high(t + 2)
                if t in takes:
                    out, j, func = takes[t]
                    take(t, out[:, j, :], func)
            act.wait_ge(dve_out.sem, dve_out.at(layer, 5))
            nc.scalar.activation(fa[:, :], fx[:, :], ACT.Abs).then_inc(f_step.sem, 1)
            act.wait_ge(f_step.sem, f_step.at(layer, 1))
            nc.scalar.activation(fa[:, :], fa[:, :], ACT.Exp, scale=-1.0).then_inc(f_step.sem, 1)
            act.wait_ge(f_step.sem, f_step.at(layer, 2))
            nc.scalar.activation(fa[:, :], fa[:, :], ACT.Ln, bias=1.0).then_inc(f_step.sem, 1)
            with act.Fori(0, 2) as it:
                for j in range(4):
                    high(QK + 2 + j, it)
                    act.wait_ge(mm_done.sem, mm_done.at(layer, it * 4 + (mm0 + QK + j + 1)))
                    nc.scalar.activation(split(M["qk"][:, it * 4 + j, :], TA), buf(QK + j),
                                         ACT.Copy).then_inc(act_out.sem, 1)
            for j in range(2):
                act.wait_ge(dve_step.sem, dve_step.at(layer, M["steps"]["centred"] - 1 + j))
                nc.scalar.activation(gate[:, j, :], acc[:, j, :], ACT.Square).then_inc(ln_act.sem, 1)
            high(V + 2)
            for i in range(5):
                take_v(0, i)
            high(V + 3)
            act.wait_ge(ln_pe.sem, ln_pe.at(layer, 2))
            nc.scalar.activation(split(gate[:, 0, :], TA), banks(ps, 6, TA), ACT.Ln,
                                 bias=S["eps5"][:, 0:1]).then_inc(ln_act.sem, 1)
            act.wait_ge(ln_act.sem, ln_act.at(layer, 3))
            nc.scalar.activation(gate[:, 0, :], gate[:, 0, :], ACT.Exp, scale=-0.5).then_inc(ln_act.sem, 1)
            ln_b = col("ln_b")
            for j in range(2):
                act.wait_ge(dve_step.sem, dve_step.at(layer, M["steps"]["normed"] - 1 + j))
                nc.scalar.activation(acc[:, j, :], acc[:, j, :], ACT.Silu,
                                     bias=ln_b[:, j:j + 1]).then_inc(ln_act.sem, 1)
            for i in range(5):
                take_v(1, i)
            for j in range(2):
                act.wait_ge(ln_pe.sem, ln_pe.at(layer, 3 + j))
                nc.scalar.activation(split(y[:, 4 + j, :], TA), banks(ps, 2 * j, TA), ACT.Copy)

        @block.vector
        def _(dve):
            step = [0]

            def then(ins):
                step[0] += 1
                return ins.then_inc(dve_step.sem, 1)

            def after(n):
                dve.wait_ge(dve_step.sem, dve_step.at(layer, n))

            def low(p, it=0):
                weight_low(nc, dve, W, layer, p % 2, slot_of(p) % 2, half_of(p) * LOT, LOT, it * 4 + (p + 1))

            def take(t, gates, other, out):
                dve.wait_ge(mm_done.sem, mm_done.at(layer, mm0 + t + 1))
                dve.wait_ge(act_out.sem, act_out.at(layer, gates))
                nc.vector.tensor_tensor(split(out, TA), buf(t), split(other, TA), ALU.mult).then_inc(dve_out.sem, 1)

            dww, dwb = col("dw_w"), col("dw_b")

            def long_tap(tap, before):
                for j in range(2):
                    dve.wait_ge(dve_step.sem, dve_step.at(layer, before + j))
                    nc.vector.scalar_tensor_tensor(
                        out=acc[:, j, :], in0=a_pad[:, j, bass.ds(tap, TA)],
                        scalar=dww[:, bass.ds(tap + j * TAPS_LONG, 1)], in1=acc[:, j, :],
                        op0=ALU.mult, op1=ALU.add).then_inc(dve_step.sem, 1)

            low(0)
            low(1)
            for t in range(QK):
                low(t + 2)
                if t in (2, 3):
                    take(t, t - 1, gate[:, t - 2, :], a_pad[:, t - 2, TAPS_LONG - 1:TAPS_LONG - 1 + TA])
                if t in (6, 7):
                    take(t, t - 3, scc[:, t - 6, :], p_pad[:, t - 6, TAPS_SHORT - 1:TAPS_SHORT - 1 + TA])
                if t == 10:
                    dve.wait_ge(mm_done.sem, mm_done.at(layer, mm0 + 11))
                    nc.vector.tensor_scalar(split(fx[:, :], TA), banks(ps, 0, TA)[0:HEADS_A],
                                            col("b_forget")[0:HEADS_A, 0:1], None, ALU.add).then_inc(dve_out.sem, 1)
                if t == 4:
                    dve.wait_ge(dve_out.sem, dve_out.at(layer, 2))
                    for j in range(2):
                        then(nc.vector.tensor_scalar(acc[:, j, :], a_pad[:, j, 0:TA],
                                                     dww[:, j * TAPS_LONG:j * TAPS_LONG + 1], dwb[:, j:j + 1],
                                                     ALU.mult, ALU.add))
                if t >= 4:
                    for tap in range(2 * (t - 4) + 1, 2 * (t - 4) + 3):
                        long_tap(tap, step[0] - 1)
                        step[0] += 2
            assert step[0] == 2 * (TAPS_STATIC + 1)
            with dve.Fori(0, 2) as it:
                for j in range(4):
                    low(QK + 2 + j, it)
                    for r in range(2):
                        done = TAPS_STATIC + 1 + 2 * j + r
                        long_tap(it * 8 + done, it * 16 + (2 * done - 1))
            step[0] += 2 * 16
            assert step[0] == M["steps"]["conv"]
            dve.wait_ge(ln_pe.sem, ln_pe.at(layer, 1))
            for j in range(2):
                then(nc.vector.tensor_tensor(split(acc[:, j, :], TA), split(acc[:, j, :], TA), banks(ps, 6, TA),
                                             ALU.subtract))
            assert step[0] == M["steps"]["centred"]
            dve.wait_ge(f_step.sem, f_step.at(layer, 3))
            then(nc.vector.scalar_tensor_tensor(out=fa[:, :], in0=fx[:, :], scalar=0.0, in1=fa[:, :],
                                                op0=ALU.min, op1=ALU.subtract))
            after(step[0])
            then(nc.vector.tensor_tensor_scan(fx[:, :], S["ones"][0:HEADS_A, 0:TA], fa[:, :], 0.0, ALU.mult, ALU.add))
            after(step[0])
            then(nc.vector.tensor_scalar(fa[:, :], fx[:, :], -1.0, None, ALU.mult))
            assert step[0] == M["steps"]["F"]
            low(V + 2)
            scw = col("sc_w")
            dve.wait_ge(dve_out.sem, dve_out.at(layer, 4))
            for tap in range(TAPS_SHORT + 1):
                for j in range(2):
                    if tap == 0:
                        then(nc.vector.tensor_scalar(scc[:, j, :], p_pad[:, j, 0:TA], scw[:, j * 3:j * 3 + 1], None, ALU.mult))
                        continue
                    after(step[0] - 1)
                    if tap < TAPS_SHORT:
                        then(nc.vector.scalar_tensor_tensor(
                            out=scc[:, j, :], in0=p_pad[:, j, tap:tap + TA], scalar=scw[:, j * 3 + tap:j * 3 + tap + 1],
                            in1=scc[:, j, :], op0=ALU.mult, op1=ALU.add))
                        continue
                    dve.wait_ge(act_out.sem, act_out.at(layer, 5 + j))
                    then(nc.vector.tensor_tensor(y[:, 6 + j, :], scc[:, j, :], scb[:, j, :], ALU.mult))
            assert step[0] == M["steps"]["short"]
            low(V + 3)
            dve.wait_ge(ln_act.sem, ln_act.at(layer, 4))
            ln_g = col("ln_g")
            for j in range(2):
                then(nc.vector.scalar_tensor_tensor(out=acc[:, j, :], in0=acc[:, j, :], scalar=ln_g[:, j:j + 1],
                                                    in1=gate[:, 0, :], op0=ALU.mult, op1=ALU.mult))
            assert step[0] == M["steps"]["normed"] == dve_step.per_layer


def head_norm_stage(nc, S, layer, M):
    ps, y, sq = S["psum"], M["y"], S["scratch"]
    u_hi, u_lo = M["u"]
    g = M["col"]("head_g")
    hn_sq, hn_pe, hn_ln, hn_root, hn_dve, hn_high = (
        S[x] for x in ("hn_sq", "hn_pe", "hn_ln", "hn_root", "hn_dve", "hn_high"))
    with nc.Block() as block:
        @block.tensor
        def _(pe):
            for k in range(KD):
                pe.wait_ge(hn_sq.sem, hn_sq.at(layer, k + 1))
                if k >= 4:
                    pe.wait_ge(hn_ln.sem, hn_ln.at(layer, k - 3))
                for c, (c0, cn) in enumerate(chunks(TA)):
                    mm = nc.tensor.matmul(ps[:, 2 * (k % 4) + c, 0:cn], S["mean64"][:, :], sq[:, k, c0:c0 + cn],
                                          start=True, stop=True)
                mm.then_inc(hn_pe.sem, 1)

        @block.scalar
        def _(act):
            for k in range(KD):
                nc.scalar.activation(sq[:, k, :], y[:, k, :], ACT.Square).then_inc(hn_sq.sem, 1)
            for k in range(KD):
                act.wait_ge(hn_pe.sem, hn_pe.at(layer, k + 1))
                nc.scalar.activation(split(sq[:, k, :], TA), banks(ps, 2 * (k % 4), TA), ACT.Ln,
                                     bias=S["eps6"][:, 0:1]).then_inc(hn_ln.sem, 1)
            for k in range(KD + 2):
                if k < KD:
                    act.wait_ge(hn_ln.sem, hn_ln.at(layer, k + 1))
                    nc.scalar.activation(sq[:, k, :], sq[:, k, :], ACT.Exp, scale=-0.5).then_inc(hn_root.sem, 1)
                if k >= 2:
                    act.wait_ge(hn_dve.sem, hn_dve.at(layer, k - 1))
                    nc.scalar.activation(u_hi[:, k - 2, :], y[:, k - 2, :], ACT.Copy).then_inc(hn_high.sem, 1)

        @block.vector
        def _(dve):
            for k in range(KD + 2):
                if k < KD:
                    dve.wait_ge(hn_root.sem, hn_root.at(layer, k + 1))
                    nc.vector.scalar_tensor_tensor(out=y[:, k, :], in0=y[:, k, :], scalar=g[:, k:k + 1],
                                                   in1=sq[:, k, :], op0=ALU.mult,
                                                   op1=ALU.mult).then_inc(hn_dve.sem, 1)
                if k >= 2:
                    dve.wait_ge(hn_high.sem, hn_high.at(layer, k - 1))
                    nc.vector.tensor_tensor(u_lo[:, k - 2, :], y[:, k - 2, :], u_hi[:, k - 2, :].bitcast(F32),
                                            ALU.subtract)


def up_stage_a(nc, S, W, layer, A, M, hid):
    ps, mm_done, w_lo = S["psum"], W["mm_done"], W["w_lo"]
    u_hi, u_lo = M["u"]
    free, convolved, activated, gated = S["psum_free"], S["ff_conv"], S["ff_act"], S["ff_gated"]
    multiplied, high_out = S["ff_mult"], S["ff_high"]
    z_pad, cv = M["z_pad"], M["cv"]
    ffw = M["col"]("ff_w")
    base, mm_base, part_base, free_base = 16, 49, 31, 8 + 4
    rounds, LOT = FF_PAIRS // 2, KD * UNIT
    with nc.Block() as block:
        @block.sync
        def _(sp):
            ring_feed(sp, W, layer, base, w_lo, lambda j: j * 2 + (part_base + 2),
                      (FF_PAIRS, lambda j: A["wup"][layer, j]), lambda j: A["wdown"][layer, j])

        @block.tensor
        def _(pe):
            with pe.Fori(0, rounds) as it:
                for j in range(4):
                    pe.wait_ge(free.sem, free.at(layer, it * 4 + (free_base + j + 1)))
                    pe.wait_ge(w_lo.sem, w_lo.at(layer, it * 4 + (part_base + j + 1)))
                    for k in range(KD):
                        cols = slice(k * UNIT, (k + 1) * UNIT)
                        mm = product(nc, [ps[:, 2 * j + c, 0:cn] for c, (_, cn) in enumerate(chunks(TA))],
                                     (W["hi"][:, j % 2, cols], W["lo"][:, j % 2, cols]),
                                     [(u_hi[:, k, c0:c0 + cn], u_lo[:, k, c0:c0 + cn]) for c0, cn in chunks(TA)],
                                     k == 0, k == KD - 1)
                    mm.then_inc(mm_done.sem, 1)

        @block.scalar
        def _(act):
            def high(it, j):
                weight_high(nc, act, W, layer, j % 2, (j // 2) % 2, (j % 2) * LOT, LOT,
                            slot_full(W, layer, base, it + j // 4), it * 4 + (mm_base + j - 1))

            def step(it, last):
                for j in range(4):
                    if not last or j < 2:
                        high(it, j + 2)
                    act.wait_ge(mm_done.sem, mm_done.at(layer, it * 4 + (mm_base + j + 1)))
                    act.wait_ge(convolved.sem, convolved.at(layer, it * 4 + (j + 1)))
                    nc.scalar.activation(split(z_pad[:, j, TAPS_SHORT - 1:TAPS_SHORT - 1 + TA], TA),
                                         banks(ps, 2 * j, TA), ACT.Copy).then_inc(free.sem, 1)
                    if j % 2 == 1:
                        act.wait_ge(convolved.sem, convolved.at(layer, it * 4 + (4 + j)))
                        nc.scalar.activation(cv[:, j - 1, :], cv[:, j - 1, :], ACT.Silu).then_inc(activated.sem, 1)
                        act.wait_ge(multiplied.sem, multiplied.at(layer, it * 2 + (j // 2 + 1)))
                        nc.scalar.activation(hid[0][:, it * 2 + j // 2, :], cv[:, j, :], ACT.Copy).then_inc(high_out.sem, 1)

            act.sem_inc(free.sem, 4)
            act.sem_inc(convolved.sem, 4)
            high(0, 0)
            high(0, 1)
            in_rounds(act, rounds, step)

        @block.vector
        def _(dve):
            def low(it, j):
                weight_low(nc, dve, W, layer, j % 2, (j // 2) % 2, (j % 2) * LOT, LOT, it * 4 + (part_base + j + 1))

            def step(it, last):
                for j in range(4):
                    if not last or j < 2:
                        low(it, j + 2)
                    dve.wait_ge(free.sem, free.at(layer, it * 4 + (free_base + 4 + j + 1)))
                    if j % 2 == 0:
                        dve.wait_ge(gated.sem, gated.at(layer, it * 2 + (j // 2 + 1)))
                    m = it * 2 + j // 2
                    wcol = [ffw[:, bass.ds(m * 6 + (3 * (j % 2) + tap), 1)] for tap in range(TAPS_SHORT)]
                    nc.vector.tensor_scalar(cv[:, j, :], z_pad[:, j, 0:TA], wcol[0], None,
                                            ALU.mult).then_inc(S["ff_tap"].sem, 1)
                    for tap in (1, 2):
                        dve.wait_ge(S["ff_tap"].sem, S["ff_tap"].at(layer, it * 8 + (2 * j + tap)))
                        nc.vector.scalar_tensor_tensor(
                            out=cv[:, j, :], in0=z_pad[:, j, tap:tap + TA], scalar=wcol[tap], in1=cv[:, j, :],
                            op0=ALU.mult, op1=ALU.add).then_inc(S["ff_tap"].sem if tap == 1 else convolved.sem, 1)
                    if j % 2 == 1:
                        dve.wait_ge(activated.sem, activated.at(layer, m + 1))
                        dve.wait_ge(convolved.sem, convolved.at(layer, it * 4 + (4 + j + 1)))
                        nc.vector.tensor_tensor(cv[:, j, :], cv[:, j - 1, :], cv[:, j, :],
                                                ALU.mult).then_inc(multiplied.sem, 1)
                        dve.wait_ge(high_out.sem, high_out.at(layer, m + 1))
                        nc.vector.tensor_tensor(hid[1][:, m, :], cv[:, j, :], hid[0][:, m, :].bitcast(F32),
                                                ALU.subtract).then_inc(gated.sem, 1)

            dve.sem_inc(gated.sem, 2)
            low(0, 0)
            low(0, 1)
            in_rounds(dve, rounds, step)


def first_stack(nc, G, A, h):
    with ExitStack() as ctx:
        sb = Scope(nc, ctx).sb

        def sem(name):
            return ctx.enter_context(nc.semaphore(name))

        def signal(name, per_layer, step=1):
            return Signal(sem(name), per_layer, step)

        cols = sb("cols_a", [P, N_COLS_A])
        strip = sb("mask_strip_a", [P, TA + META])
        pick = sb("pick_head", [2 * HEADS_A, HEADS_A])
        rstd = sb("rstd_a", [P, TA])

        def part(where, at, *shape):
            n = int(np.prod(shape))
            ap = where[:, at:at + n]
            return ap if len(shape) == 1 else ap.rearrange("p (a b) -> p a b", a=shape[0])

        def col(name):
            return cols[:, COLS_A[name][0]:COLS_A[name][1]]

        M = {"col": col, "steps": STEPS_A}
        ring = {"tiles": G["ring"], "full": [sem(f"slot{s}_full_a") for s in range(2)],
                "mm_done": signal("mm_done_a", MM_A), "per_layer": SLOTS_A,
                "w_hi": signal("w_hi_a", LOTS_A), "w_lo": signal("w_lo_a", LOTS_A)}
        per = HEADS_A * len(Q_TILES_A)
        S = dict(G["consts"])
        S.update(
            psum=G["psum"], rstd=rstd, split_norm={0: 0, 2: 1},
            squared=signal("squared_a", 4 * KD), summed=signal("summed_a", 4), rooted=signal("rooted_a", 4),
            rstd_ready=signal("rstd_ready_a", 4), scaled=signal("scaled_a", 4 * KD), rounded=signal("rounded_a", 2 * KD),
            act_out=signal("act_out", 24), dve_out=signal("dve_out", 5),
            dve_step=signal("dve_step", STEPS_A["normed"]), f_step=signal("f_step", 3),
            ln_pe=signal("ln_pe", 4), ln_act=signal("ln_act", 6), f_rows=signal("f_rows", 1, 16),
            cols_in=signal("cols_in_a", 1, 16),
            scores=signal("scores_a", per), shifted=signal("shifted_a", per), inverted=signal("inverted_a", per), probs=signal("probs_a", per),
            turned=signal("turned_a", per), turned_out=signal("turned_out_a", per), mixed=signal("mixed_a", per),
            stored=signal("stored_a", per), staged=signal("staged_a", HEADS_A // 2),
            y_turned=signal("y_turned_a", 4), y_out=signal("y_out_a", 4),
            psum_free=signal("psum_free_a", (8 + 4) + (44 + 4) + (8 + 2)),
            ff_conv=signal("ff_conv", 4 + 2 * FF_PAIRS), ff_act=signal("ff_act", FF_PAIRS),
            ff_mult=signal("ff_mult", FF_PAIRS), ff_high=signal("ff_high", FF_PAIRS),
            ff_gated=signal("ff_gated", 2 + FF_PAIRS), ff_tap=signal("ff_tap", 4 * FF_PAIRS))
        for name in ("hn_sq", "hn_pe", "hn_ln", "hn_root", "hn_dve", "hn_high"):
            S[name] = signal(name, KD)
        consts_in = sem("consts_in_a")

        with nc.Block() as block:
            @block.sync
            def _(sp):
                sp.dma_start(strip[:, :], A["mask_a"]).then_inc(consts_in, 16)
                sp.dma_start(pick[:, :], A["pick_head"]).then_inc(consts_in, 16)
                sp.wait_ge(consts_in, 32)

        def last_key(un):
            q0, qn = Q_TILES_A[un["i"]]
            return q0 + qn, Q_TILES_A[:un["i"] + 1]

        units = [{"head": head, "i": i} for head in range(4) for i in range(len(Q_TILES_A))]

        def weight_parts(scope, name, units=KD):
            hi, lo = scope.parts(name, 2, units * UNIT)
            return {**ring, "hi": hi, "lo": lo}

        def mixer(layer, scope):
            arena = scope.sb("arena_a", [P, 8 * TA + 2 * 2560 + 1116 + 1060 + 8 * TA])
            y = M["y"] = scope.sb("y_a", [P, KD, TA])
            f_left, f_right = scope.sb("f_left", [2 * HEADS_A, TA]), scope.sb("f_right", [2 * HEADS_A, TA])
            M["qk"], M["v"] = part(arena, 0, 8, TA), part(arena, 8 * TA, 5, 512)
            M["y_tm"] = part(arena, 8 * TA + 2560, 5, 512)
            at = 8 * TA + 5120
            M["a_pad"] = part(arena, at, 2, TA + TAPS_LONG - 1)
            M["p_pad"] = part(arena, at + 1116, 2, TA + TAPS_SHORT - 1)
            for n, name in enumerate(("acc", "gate", "scc", "scb")):
                M[name] = part(arena, at + 1116 + 1060 + n * 2 * TA, 2, TA)
            M["f_left"], M["f_sum"] = f_left, f_right[0:HEADS_A, :]
            S["scratch"] = part(arena, 0, KD, TA)

            with nc.Block() as block:
                @block.sync
                def _(sp):
                    sp.dma_start(cols[:, :], A["cols_a"][layer]).then_inc(S["cols_in"].sem, 16)
                    first_slots(sp, ring, lambda j: A["win"][layer, j])
                    sp.wait_ge(S["cols_in"].sem, S["cols_in"].at(layer, 1))
                    pass_waits(sp, S)

                @block.tensor
                def _(pe):
                    pe.sem_inc(ring["mm_done"].sem, 2)

                @block.vector
                def _(dve):
                    nc.vector.memset(M["a_pad"][:, :, 0:TAPS_LONG - 1], 0.0)
                    nc.vector.memset(M["p_pad"][:, :, 0:TAPS_SHORT - 1], 0.0)
                    nc.vector.memset(f_left[:, :], 1.0)
                    nc.vector.memset(f_right[:, :], 1.0)

            with ExitStack() as inner:
                local = Scope(nc, inner)
                M["u"] = local.parts("u_in_a", KD, TA)
                M["fa"] = local.sb("log_f", [HEADS_A, TA])
                norm_stage(nc, S, layer, 0, TA, h, col("mix_pre"), M["u"])
                in_stage_a(nc, S, weight_parts(local, "w_in"), layer, A, M)

            with ExitStack() as inner:
                stage = Scope(nc, inner).sb("stage_a", [P, 5 * TA + 1280])
                qa, ka = (Scope(nc, inner).sb(n, [DH + 2 * HEADS_A, 4, TA]) for n in ("q_and_f", "k_and_f"))
                v_meta = Scope(nc, inner).sb("v_meta", [META, 2, P])
                S.update(N=part(stage, 0, 2, TA), P=part(stage, 2 * TA, 3, TA), PT=part(stage, 5 * TA, 2, 640))

                with nc.Block() as block:
                    @block.vector
                    def _(dve):
                        for n in range(4):
                            nc.vector.tensor_copy(ka[DH:DH + 2 * HEADS_A, n, :], f_right[:, :])

                def stage_pair(it, n):
                    nc.vector.tensor_copy(v_meta[:, n, :], M["v"][0:META, 0, bass.ds(it * (4 * DH) + n * P, P)])
                    for hh in range(2):
                        rows, m = slice(DH * hh, DH * (hh + 1)), 2 * n + hh
                        nc.vector.tensor_scalar(qa[0:DH, m, :], M["qk"][rows, it * 4 + 2 * n, :], -DH ** -0.5, None, ALU.mult)
                        nc.vector.tensor_copy(ka[0:DH, m, :], M["qk"][rows, it * 4 + (2 * n + 1), :])
                        last = nc.vector.tensor_scalar(qa[DH:DH + 2 * HEADS_A, m, :], f_left[:, :],
                                                       pick[:, bass.ds(it * 4 + m, 1)], None, ALU.mult)
                    return last

                def invert(dve, it, unit, u_, qn, factor, total):
                    nc.vector.reciprocal(factor, total).then_inc(S["inverted"].sem, 1)

                def finish(dve, it, unit, u_, q0, qn, product, factor):
                    dst = M["y_tm"][0:qn, unit["i"], bass.ds(it * (4 * DH) + unit["head"] * DH, DH)]
                    return nc.vector.tensor_scalar(dst, product, factor, None, ALU.mult)

                softmax_stage(nc, S, layer, {
                    "base": 0, "rounds": HEADS_A // 4, "units": units, "T": TA, "stages": [0, len(units) // 2],
                    "q_tiles": Q_TILES_A, "keys": last_key, "stage": stage_pair, "finish": finish, "invert": invert,
                    "q": lambda un, q0, qn: qa[:, un["head"], q0:q0 + qn],
                    "k": lambda un, a, b: ka[:, un["head"], a:b],
                    "v": lambda it, un, j, sn: v_meta[:, un["head"] // 2, DH * (un["head"] % 2):DH * (un["head"] % 2 + 1)]
                         if j == 0 else M["v"][0:sn, j, bass.ds(it * (4 * DH) + DH * un["head"], DH)],
                    "more": lambda it, un, q0, qn: [],
                    "bias": lambda un, qn, n: strip[0:qn, TA:TA + n] if un["i"] == 0 else strip[0:qn, TA - n:TA],
                })
                turn_heads_stage(nc, S, layer, M["y_tm"], y, 4, Q_TILES_A)

            with ExitStack() as inner:
                local = Scope(nc, inner)
                M["u"] = local.parts("u_out_a", KD, TA)
                head_norm_stage(nc, S, layer, M)
                linear_stage(nc, S, weight_parts(local, "w_out"), layer, TA, lambda j: A["wout"][layer, j], 4, M["u"],
                             12, 41, 23, 0, lambda j: A["wup"][layer, j], out=y)
            norm_stage(nc, S, layer, 1, TA, y, col("mix_post"), y, residual=h)

        def glu(layer, scope):
            with ExitStack() as up_scope:
                hid = scope.parts("hid_a", FF_PAIRS, TA)
                local = Scope(nc, up_scope)
                M["u"] = local.parts("u_up_a", KD, TA)
                with ExitStack() as inner:
                    S["scratch"] = Scope(nc, inner).sb("squares_up_a", [P, KD, TA])
                    norm_stage(nc, S, layer, 2, TA, h, col("ffn_pre"), M["u"])
                M["z_pad"] = local.sb("z_pad", [P, 4, TA + TAPS_SHORT - 1])
                M["cv"] = local.sb("convolved", [P, 4, TA])
                with nc.Block() as block:
                    @block.vector
                    def _(dve):
                        nc.vector.memset(M["z_pad"][:, :, 0:TAPS_SHORT - 1], 0.0)
                up_stage_a(nc, S, weight_parts(local, "w_up_a"), layer, A, M, hid)
            y = scope.sb("y_down_a", [P, KD, TA])
            with ExitStack() as inner:
                linear_stage(nc, S, weight_parts(Scope(nc, inner), "w_down_a", 11), layer, TA,
                             lambda j: A["wdown"][layer, j], 16, hid, 38, 93, 75, 12 + 48, None,
                             units=FF_PAIRS // 2, tile_parts=2, out=y)
            S["scratch"] = scope.sb("squares_down_a", [P, KD, TA])
            norm_stage(nc, S, layer, 3, TA, y, col("ffn_post"), y, residual=h)

        with nc.Fori(0, DEPTH) as layer:
            with ExitStack() as inner:
                mixer(layer, Scope(nc, inner))
            with ExitStack() as inner:
                glu(layer, Scope(nc, inner))


MM_B = 2 + 16 + 32 + 4 + 8 + 64
LOTS_B = 16 + 8 + 8 + 64
OUT_TOKENS = TB
LAST_DIST = TB - 1
ROW_LEN = 640
T_SB, T_MB, T_DF, T_NSQ, T_CMP, T_KSW = 0, 4, 8, 12, 14, 15
V_SB, V_MB, V_DF, V_SLC, V_WIN, V_G = 0, 256, 512, 768, 832, 896
Y_SB, Y_MB, Y_NS, Y_DF = 0, 256, 512, 768
COLS_B = {}
_at = 0
for _name, _n in (("attn_g", KD), ("mlp_g", KD), ("pos", 2 * 16), ("w2k", 2 * P), ("w2v", 2 * DH),
                  ("lambda", 4 * 32), ("neg_lambda_init", 1), ("one_less_init", 1), ("subln", DH)):
    COLS_B[_name] = (_at, _at + _n)
    _at += _n
N_COLS_B = _at
UNITS_B = 96


def bias_setup(nc, S, A, M):
    ps = S["psum"]
    loaded, multiplied, copied, row_out, strips_in = (M[x] for x in ("loaded", "multiplied", "copied", "row_out", "strips_in"))
    table, rev, fwd, rows = M["table"], M["rev"], M["fwd"], M["rows"]
    scratch = M["bias_rows"]
    with nc.Block() as block:
        @block.sync
        def _(sp):
            sp.dma_start(table[0:N_BUCKETS, :], A["rel_bias"]).then_inc(loaded, 16)
            sp.dma_start(rev[:, :], A["onehot_rev"]).then_inc(loaded, 16)
            sp.dma_start(fwd[:, :], A["onehot_fwd"]).then_inc(loaded, 16)
            for name in ("tri", "neg_ones", "mask01", "mask_add", "cover", "blocks", "imp_scale", "imp_add",
                         "tri8", "valid", "reverse"):
                sp.dma_start(M[name][:, :], A[name]).then_inc(loaded, 16)
            sp.wait_ge(copied, 1)
            sp.dma_start(scratch, rows[:, :]).then_inc(row_out, 16)
            sp.wait_ge(row_out, 16)
            for hd in range(3 * HEADS_B):
                src = bass.AP(scratch.tensor, hd * ROW_LEN, [[1, P], [1, TB]])
                sp.dma_start(M["strips"][:, hd, :], src).then_inc(strips_in, 16)
            sp.wait_ge(strips_in, 16 * 3 * HEADS_B)
            sp.wait_ge(loaded, 16 * 14)

        @block.vector
        def _(dve):
            nc.vector.memset(table[N_BUCKETS:N_BUCKETS + 1, :], 1.0).then_inc(M["one_row"], 1)

        @block.tensor
        def _(pe):
            pe.wait_ge(loaded, 16 * 14)
            pe.wait_ge(M["one_row"], 1)
            for c in range(2):
                mm = nc.tensor.matmul(ps[0:3 * HEADS_B, c, 0:ROW_LEN // 2], table[:, :],
                                      rev[:, c * (ROW_LEN // 2):(c + 1) * (ROW_LEN // 2)], start=True, stop=True)
            mm.then_inc(multiplied, 1)
            for i in range(4):
                for c in range(N_CMP):
                    f0 = LAST_DIST + P * i - CMP_STRIDE * c - (CMP_LEN - 1)
                    at = (i * N_CMP + c) * HEADS_B
                    mm = nc.tensor.matmul(ps[:, 2, at:at + HEADS_B], fwd[:, f0:f0 + P],
                                          table[:, HEADS_B:2 * HEADS_B], start=True, stop=True)
            mm.then_inc(multiplied, 1)

        @block.scalar
        def _(act):
            act.wait_ge(multiplied, 1)
            nc.scalar.activation(rows[:, :].rearrange("p (c n) -> p c n", c=2),
                                 ps[0:3 * HEADS_B, 0:2, 0:ROW_LEN // 2], ACT.Copy).then_inc(copied, 1)
            act.wait_ge(multiplied, 2)
            for hd in range(HEADS_B):
                src = ps[:, 2, 0:4 * N_CMP * HEADS_B].rearrange("p (i c h) -> p i c h", i=4, h=HEADS_B)[:, :, :, hd]
                nc.scalar.activation(M["cbias"][:, hd, :, :], src, ACT.Copy)

    turned, placed = M["strip_turned"], M["strip_placed"]
    with nc.Block() as block:
        @block.tensor
        def _(pe):
            for hd in range(3 * HEADS_B):
                if hd >= 8:
                    pe.wait_ge(placed, hd - 7)
                nc.tensor.matmul(ps[:, hd % 8, 0:TB], M["reverse"][:, :], M["strips"][:, hd, :],
                                 start=True, stop=True).then_inc(turned, 1)

        @block.scalar
        def _(act):
            for hd in range(3 * HEADS_B):
                act.wait_ge(turned, hd + 1)
                nc.scalar.activation(M["strips"][:, hd, :], ps[:, hd % 8, 0:TB], ACT.Copy).then_inc(placed, 1)


def token_major_stage(nc, S, W, layer, A, M):
    ps, mm_done, w_lo, free = S["psum"], W["mm_done"], W["w_lo"], S["tm_free"]
    u_hi, u_lo = M["u"]
    base, mm_base, part_base, n = 8, 18, 16, 4 * 256
    with nc.Block() as block:
        @block.sync
        def _(sp):
            ring_feed(sp, W, layer, base, w_lo, lambda j: j * 2 + (part_base + 2),
                      (4, lambda j: A["wv_b"][layer, j]), lambda j: A["wcmp"][layer, j])

        @block.tensor
        def _(pe):
            with pe.Fori(0, 2) as it:
                for s in range(2):
                    for half in range(2):
                        pe.wait_ge(w_lo.sem, w_lo.at(layer, it * 4 + (part_base + 2 * s + half + 1)))
                        for i in range(4):
                            if half == 0:
                                pe.wait_ge(free.sem, free.at(layer, it * 8 + (4 * s + i + 1)))
                            for k in range(4):
                                kk, cols = 4 * half + k, slice(k * 256, (k + 1) * 256)
                                mm = product(nc, [ps[:, 4 * s + i, 0:256]],
                                             (u_hi[:, kk, P * i:P * (i + 1)], u_lo[:, kk, P * i:P * (i + 1)]),
                                             [(W["hi"][:, half, cols], W["lo"][:, half, cols])],
                                             kk == 0, kk == KD - 1)
                            mm.then_inc(mm_done.sem, 1)

        @block.scalar
        def _(act):
            def high(it, j):
                weight_high(nc, act, W, layer, j % 2, (j // 2) % 2, (j % 2) * n, n,
                            slot_full(W, layer, base, it + j // 4), it * 16 + (mm_base + 4 * (j - 1)))

            def step(it, last):
                for j in range(4):
                    s, half = j // 2, j % 2
                    if half == 1:
                        for i in range(4):
                            act.wait_ge(mm_done.sem, mm_done.at(layer, it * 16 + (mm_base + 4 * j + i + 1)))
                            nc.scalar.activation(M["v_tm"][:, i, bass.ds(it * 512 + 256 * s, 256)],
                                                 ps[:, 4 * s + i, 0:256], ACT.Copy).then_inc(free.sem, 1)
                    if not last or j < 2:
                        high(it, j + 2)

            act.sem_inc(free.sem, 8)
            high(0, 0)
            high(0, 1)
            in_rounds(act, 2, step)

        @block.vector
        def _(dve):
            def low(it, j):
                weight_low(nc, dve, W, layer, j % 2, (j // 2) % 2, (j % 2) * n, n, it * 4 + (part_base + j + 1))

            low(0, 0)
            low(0, 1)
            for j in range(2, 8):
                low(0, j)


def stick_stage(nc, S, ring, layer, A, M):
    ps, w, mm_done, fm, col = S["psum"], ring["tiles"], ring["mm_done"], M["fm"], M["col"]
    qs, ks = M["qs"], M["ks"]
    z_in, softplus, logit, fenced, weight, mixed, stored, staged = (
        S[x] for x in ("sb_z", "sb_softplus", "sb_logit", "sb_fenced", "sb_weight", "sb_mixed", "sb_stored", "sb_staged"))
    ln, sb_ln = M["sb_log"], S["sb_ln"]
    sp_, aw = M["sb_sp"], M["sb_w"]
    units = [(hh, st) for hh in range(2) for st in (3, 2, 1, 0)]
    U = len(units)
    blocks_in, hidden, projected, lam_step = S["blocks_in"], S["hidden"], S["projected"], S["lam_step"]
    base, mm_base = 12, 50
    xb, hg = M["xb"], M["hg"]
    HIDDEN_BANKS = (6, 7, 0, 1)

    def at(sig, it, n, per=1):
        return sig.at(layer, it * (U * per) + n)

    with nc.Block() as block:
        @block.sync
        def _(sp):
            ring_feed(sp, ring, layer, base, mm_done, lambda j: j + (mm_base + 1),
                      (4, lambda j: A["wcmp"][layer, j]), lambda j: A["wout_b"][layer, j])

        @block.tensor
        def _(pe):
            def compress(kv):
                pe.wait_ge(blocks_in.sem, blocks_in.at(layer, kv + 1))
                for s in range(2):
                    pe.wait_ge(ring["full"][s], slot_full(ring, layer, base, kv))
                    for l8 in range(8):
                        for m in range(2):
                            cols = slice((2 * l8 + m) * UNIT, (2 * l8 + m + 1) * UNIT)
                            mm = nc.tensor.matmul(ps[:, HIDDEN_BANKS[2 * kv + m], 0:N_CMP], w[:, s, cols],
                                                  xb[:, kv, 8 * s + l8, :], start=(s == 0 and l8 == 0),
                                                  stop=(s == 1 and l8 == 7))
                    mm.then_inc(mm_done.sem, 1)

            def z_term(out, u, start, stop):
                hh, st = units[u]
                rows = slice(64 * hh, 64 * hh + 64)
                return nc.tensor.matmul(out, ks[rows, P * st:P * (st + 1)], qs[rows, P * st:TB], start=start, stop=stop)

            def logits(it, u):
                hh, st = units[u]
                n = TB - P * st
                pe.wait_ge(softplus.sem, at(softplus, it, 2 * (u + 1), 2))
                if u >= 2:
                    pe.wait_ge(weight.sem, at(weight, it, u - 1))
                b = 2 + u % 2
                z_term(ps[:, b, 0:n], u, True, False)
                for jt in range(st + 1, 4):
                    nc.tensor.matmul(ps[:, b, P * (jt - st):n], M["neg_ones"][:, :], sp_[:, hh, jt, 0:TB - P * jt],
                                     start=False, stop=False, skip_group_check=True)
                mm = nc.tensor.matmul(ps[:, b, 0:n], M["tri"][:, :], sp_[:, hh, st, 0:n], start=False, stop=True)
                mm.then_inc(logit.sem, 1)

            def mix(it, hh):
                pe.wait_ge(weight.sem, at(weight, it, 4 * (hh + 1)))
                for tt in range(4):
                    for st in range(tt + 1):
                        mm = nc.tensor.matmul(ps[:, 4 + hh, DH * tt:DH * (tt + 1)],
                                              aw[:, hh, st, P * (tt - st):P * (tt - st + 1)],
                                              M["v_tm"][:, st, bass.ds(it * P + (V_SB + DH * hh), DH)],
                                              start=(st == 0), stop=(st == tt))
                mm.then_inc(mixed.sem, 1)

            compress(0)
            with pe.Fori(0, 2) as it:
                pe.wait_ge(staged.sem, staged.at(layer, it + 1))
                for u in range(U + 2):
                    if u < U:
                        hh, st = units[u]
                        z_term(ps[:, u % 2, 0:TB - P * st], u, True, True).then_inc(z_in.sem, 1)
                    if 1 <= u <= U:
                        logits(it, u - 1)
                    if u >= 2 and (u - 2) % 4 == 3:
                        mix(it, (u - 2) // 4)
                pe.wait_ge(stored.sem, stored.at(layer, it * 2 + 2))
            compress(1)
            w2k, w2v = col("w2k"), col("w2v")
            pe.wait_ge(hidden.sem, hidden.at(layer, 4))
            for m in range(2):
                nc.tensor.matmul(ps[:, 4, 0:N_CMP], w2k[:, P * m:P * (m + 1)], hg[:, m, :], start=(m == 0), stop=(m == 1))
            for m in range(2):
                mm = nc.tensor.matmul(ps[0:N_CMP, 5, 0:DH], hg[:, 2 + m, :], w2v[:, DH * m:DH * (m + 1)],
                                      start=(m == 0), stop=(m == 1))
            mm.then_inc(projected.sem, 1)

        @block.scalar
        def _(act):
            def log_term(it, u):
                n = TB - P * units[u][1]
                buf = ln[:, u % 2, 0:n]
                act.wait_ge(z_in.sem, at(z_in, it, u + 1))
                if u >= 2:
                    act.wait_ge(softplus.sem, at(softplus, it, 2 * (u - 1), 2))
                nc.scalar.activation(buf, ps[:, u % 2, 0:n], ACT.Abs).then_inc(sb_ln.sem, 1)
                act.wait_ge(sb_ln.sem, at(sb_ln, it, 3 * u + 1, 3))
                nc.scalar.activation(buf, buf, ACT.Exp, scale=-1.0).then_inc(sb_ln.sem, 1)
                act.wait_ge(sb_ln.sem, at(sb_ln, it, 3 * u + 2, 3))
                nc.scalar.activation(buf, buf, ACT.Ln, bias=1.0).then_inc(sb_ln.sem, 1)

            def weights(it, u):
                hh, st = units[u]
                n = TB - P * st
                act.wait_ge(fenced.sem, at(fenced, it, u + 1))
                nc.scalar.activation(aw[:, hh, st, 0:n], ps[:, 2 + u % 2, 0:n], ACT.Exp).then_inc(weight.sem, 1)

            load_ln_and_exp(nc, act)
            act.wait_ge(lam_step.sem, lam_step.at(layer, 1))
            nc.scalar.activation(M["lam"][:, 0:2], M["lam"][:, 0:2], ACT.Exp).then_inc(lam_step.sem, 1)
            with act.Fori(0, 2) as it:
                for u in range(U + 1):
                    if u < U:
                        log_term(it, u)
                    if u >= 1:
                        weights(it, u - 1)
            nc.scalar.activation(M["gates"][:, :, :], M["v_tm"][:, :, V_G:V_G + 12], ACT.Sigmoid).then_inc(lam_step.sem, 1)
            for n in range(4):
                act.wait_ge(mm_done.sem, mm_done.at(layer, mm_base + 2 * (n // 2) + 2))
                nc.scalar.activation(hg[:, n, :], ps[:, HIDDEN_BANKS[n], 0:N_CMP], ACT.Gelu_apprx_tanh).then_inc(hidden.sem, 1)
            act.wait_ge(projected.sem, projected.at(layer, 1))
            nc.scalar.activation(M["k_cmp"][:, :], ps[:, 4, 0:N_CMP], ACT.Copy)
            nc.scalar.activation(M["v_cmp"][0:N_CMP, :], ps[0:N_CMP, 5, 0:DH], ACT.Copy)

        @block.vector
        def _(dve):
            lam, pr, lv = M["lam"], M["lam_products"], col("lambda")
            for n in range(2):
                last = nc.vector.tensor_tensor_reduce(pr[:, 32 * n:32 * n + 32], lv[:, 64 * n:64 * n + 32],
                                                      lv[:, 64 * n + 32:64 * n + 64], 1.0, 0.0, ALU.mult, ALU.add,
                                                      lam[:, n:n + 1])
            last.then_inc(lam_step.sem, 1)
            pos = col("pos").rearrange("p (t r) -> p t r", t=2)
            tokens = fm[:, T_CMP, :].rearrange("p (c r t) -> p t r c", r=8, t=2)
            for kv in range(2):
                rows = slice(64 * kv, 64 * kv + 64)
                for t in range(2):
                    for half in range(2):
                        last = nc.vector.tensor_tensor(
                            xb[64 * t:64 * t + 64, kv, 8 * half:8 * half + 8, :],
                            tokens[rows, t, :, half:half + N_CMP],
                            pos[rows, t, 8 * half:8 * half + 8].unsqueeze(2).to_broadcast([64, 8, N_CMP]), ALU.add)
                last.then_inc(blocks_in.sem, 1)
            with dve.Fori(0, 2) as it:
                nc.vector.tensor_scalar(qs, fm[:, it * 2 + T_SB, :], DH ** -0.5, None, ALU.mult)
                nc.vector.tensor_copy(ks, fm[:, it * 2 + (T_SB + 1), :]).then_inc(staged.sem, 1)
                for u in range(U + 1):
                    if u < U:
                        hh, st = units[u]
                        n = TB - P * st
                        dve.wait_ge(sb_ln.sem, at(sb_ln, it, 3 * (u + 1), 3))
                        nc.vector.scalar_tensor_tensor(out=sp_[:, hh, st, 0:n], in0=ps[:, u % 2, 0:n], scalar=0.0,
                                                       in1=ln[:, u % 2, 0:n], op0=ALU.max,
                                                       op1=ALU.add).then_inc(softplus.sem, 1)
                        dve.wait_ge(softplus.sem, at(softplus, it, 2 * u + 1, 2))
                        nc.vector.tensor_tensor(sp_[:, hh, st, 0:P], sp_[:, hh, st, 0:P], M["mask01"][:, :],
                                                ALU.mult).then_inc(softplus.sem, 1)
                    if u >= 1:
                        dve.wait_ge(logit.sem, at(logit, it, u))
                        diag = ps[:, 2 + (u - 1) % 2, 0:P]
                        nc.vector.tensor_tensor(diag, diag, M["mask_add"][:, :], ALU.add).then_inc(fenced.sem, 1)
                for hh in range(2):
                    dve.wait_ge(mixed.sem, mixed.at(layer, it * 2 + (hh + 1)))
                    dst = M["y_tm"][:, :, bass.ds(it * P + (Y_SB + DH * hh), DH)]
                    nc.vector.tensor_copy(dst, ps[:, 4 + hh, 0:4 * DH].rearrange("p (t d) -> p t d", t=4)) \
                        .then_inc(stored.sem, 1)
            for t in (T_MB, T_MB + 2, T_NSQ, T_NSQ + 1):
                nc.vector.tensor_scalar(fm[:, t, :], fm[:, t, :], -DH ** -0.5, None, ALU.mult)
            for t in (T_DF, T_DF + 2):
                nc.vector.tensor_scalar(fm[:, t, :], fm[:, t, :], -(DH // 2) ** -0.5, None, ALU.mult)
            for n, dst in enumerate((M["k_slc"], M["k_win"])):
                for half in range(2):
                    nc.vector.tensor_copy(dst[64 * half:64 * half + 64, :], fm[64 * n:64 * n + 64, T_KSW, :])
            nc.vector.memset(M["pc_sum"][:, :, :], 0.0)
            nc.vector.tensor_scalar(M["subln"][:, :], col("subln"), col("one_less_init"), None, ALU.mult)
            dve.wait_ge(lam_step.sem, lam_step.at(layer, 2))
            nc.vector.scalar_tensor_tensor(out=M["neg_lam"][:, :], in0=lam[:, 1:2], scalar=lam[:, 0:1],
                                           in1=col("neg_lambda_init"), op0=ALU.subtract, op1=ALU.add)
            dve.wait_ge(lam_step.sem, lam_step.at(layer, 3))
            nc.vector.tensor_scalar(M["gates"][:, 0, 0:HEADS_B], M["gates"][:, 0, 0:HEADS_B], M["valid"][:, 0:1],
                                    None, ALU.mult)


def select_stage(nc, S, layer, M):
    ps, ident = S["psum"], S["ident"]
    pe_s, act_s, dve_s = S["sel_pe"], S["sel_act"], S["sel_dve"]
    pc, pcT, imp = M["pc_sum"], M["pc_turned"], M["imp"]
    gt, eq, rank = M["gt"], M["eq"], M["rank"]
    with nc.Block() as block:
        @block.tensor
        def _(pe):
            for i in range(4):
                mm = nc.tensor.transpose(ps[0:N_CMP, 0, P * i:P * (i + 1)], pc[:, i, :], ident[:, :])
            mm.then_inc(pe_s.sem, 1)
            pe.wait_ge(act_s.sem, act_s.at(layer, 1))
            for i in range(4):
                mm = nc.tensor.matmul(ps[:, 1, N_SLC * i:N_SLC * (i + 1)], pcT[0:N_CMP, P * i:P * (i + 1)],
                                      M["cover"][:, :], start=True, stop=True)
            mm.then_inc(pe_s.sem, 1)
            pe.wait_ge(dve_s.sem, dve_s.at(layer, 7))
            for i in range(4):
                mm = nc.tensor.transpose(ps[0:N_SLC, 2, P * i:P * (i + 1)], rank[:, i, :], ident[:, :])
            mm.then_inc(pe_s.sem, 1)

        @block.scalar
        def _(act):
            act.wait_ge(pe_s.sem, pe_s.at(layer, 1))
            nc.scalar.activation(pcT[0:N_CMP, :], ps[0:N_CMP, 0, :], ACT.Copy).then_inc(act_s.sem, 1)
            act.wait_ge(pe_s.sem, pe_s.at(layer, 3))
            nc.scalar.activation(M["not_sel"][:, :], ps[0:N_SLC, 2, :], ACT.Copy)

        @block.vector
        def _(dve):
            done = [0]

            def then(ins):
                ins.then_inc(dve_s.sem, 1)
                done[0] += 1
                dve.wait_ge(dve_s.sem, dve_s.at(layer, done[0]))

            flat = imp[:, :, :].rearrange("p i j -> p (i j)")
            wide = [P, 4, N_SLC, N_SLC]
            other = imp[:, :, :].unsqueeze(2).to_broadcast(wide)
            own = imp[:, :, :].unsqueeze(3).to_broadcast(wide)
            dve.wait_ge(pe_s.sem, pe_s.at(layer, 2))
            then(nc.vector.tensor_tensor(flat, ps[:, 1, 0:4 * N_SLC], M["imp_scale"][:, :], ALU.mult))
            then(nc.vector.tensor_tensor(flat, flat, M["imp_add"][:, :], ALU.add))
            nc.vector.tensor_tensor(gt[:, :, :, :], other, own, ALU.is_gt)
            then(nc.vector.tensor_tensor(eq[:, :, :, :], other, own, ALU.is_equal))
            tri8 = M["tri8"][:, :].rearrange("p (j k) -> p j k", j=N_SLC).unsqueeze(1).to_broadcast(wide)
            then(nc.vector.tensor_tensor(eq[:, :, :, :], eq[:, :, :, :], tri8, ALU.mult))
            then(nc.vector.tensor_tensor(gt[:, :, :, :], gt[:, :, :, :], eq[:, :, :, :], ALU.add))
            then(nc.vector.tensor_reduce(rank[:, :, :], gt[:, :, :, :], AX_X, ALU.add))
            then(nc.vector.tensor_scalar(rank[:, :, :], rank[:, :, :], float(SLC_TOP), None, ALU.is_ge))
            pass_waits(dve, S)


def diff_norm_stage(nc, S, layer, M):
    dn_dve, dn_act = S["dn_dve"], S["dn_act"]
    sq, ms = M["dn_sq"], M["dn_ms"]
    yv = M["y_tm"][:, :, Y_DF:Y_DF + 256].rearrange("p i (h d) -> p i h d", h=HEADS_B)
    shape = [P, 4, HEADS_B, DH]
    with nc.Block() as block:
        @block.vector
        def _(dve):
            nc.vector.tensor_tensor(sq[:, :, :, :], yv, yv, ALU.mult).then_inc(dn_dve.sem, 1)
            dve.wait_ge(dn_dve.sem, dn_dve.at(layer, 1))
            nc.vector.tensor_reduce(ms[:, :, :], sq[:, :, :, :], AX_X, ALU.add).then_inc(dn_dve.sem, 1)
            dve.wait_ge(dn_act.sem, dn_act.at(layer, 2))
            nc.vector.tensor_tensor(sq[:, :, :, :], yv, ms[:, :, :].unsqueeze(3).to_broadcast(shape),
                                    ALU.mult).then_inc(dn_dve.sem, 1)
            dve.wait_ge(dn_dve.sem, dn_dve.at(layer, 3))
            gain = M["subln"][:, :].unsqueeze(1).to_broadcast([P, 16, DH])
            nc.vector.tensor_tensor(sq[:, :, :, :].rearrange("p i h d -> p (i h) d"),
                                    sq[:, :, :, :].rearrange("p i h d -> p (i h) d"), gain,
                                    ALU.mult).then_inc(dn_dve.sem, 1)
            dve.wait_ge(dn_dve.sem, dn_dve.at(layer, 4))
            nc.vector.tensor_copy(M["y_tm"][:, :, Y_DF:Y_DF + 256],
                                  sq[:, :, :, :].rearrange("p i h d -> p i (h d)"))

        @block.scalar
        def _(act):
            act.wait_ge(dn_dve.sem, dn_dve.at(layer, 2))
            nc.scalar.activation(ms[:, :, :], ms[:, :, :], ACT.Ln, scale=1.0 / DH,
                                 bias=S["eps6"][:, 0:1]).then_inc(dn_act.sem, 1)
            act.wait_ge(dn_act.sem, dn_act.at(layer, 1))
            nc.scalar.activation(ms[:, :, :], ms[:, :, :], ACT.Exp, scale=-0.5).then_inc(dn_act.sem, 1)


def second_stack(nc, G, A, h_all, out):
    h = h_all[:, :, META:TA]
    with ExitStack() as ctx:
        sb = Scope(nc, ctx).sb

        def sem(name):
            return ctx.enter_context(nc.semaphore(name))

        def signal(name, per_layer, step=1):
            return Signal(sem(name), per_layer, step)

        cols = sb("cols_b", [P, N_COLS_B])
        strips = sb("strips", [P, 3 * HEADS_B, TB])

        def part(where, at, *shape):
            ap = where[:, at:at + int(np.prod(shape))]
            return ap if len(shape) == 1 else ap.rearrange("p (a b) -> p a b", a=shape[0])

        def col(name):
            return cols[:, COLS_B[name][0]:COLS_B[name][1]]

        M = {"col": col, "strips": strips}
        for name, shape in (("k_cmp", [P, N_CMP]),
                            ("v_cmp", [N_CMP, DH]), ("gates", [P, 4, 12]), ("pc_sum", [P, 4, N_CMP]),
                            ("lam", [P, 2]), ("lam_products", [P, 64]), ("neg_lam", [P, 1]), ("subln", [P, DH]),
                            ("imp", [P, 4, N_SLC]), ("gt", [P, 4, N_SLC, N_SLC]),
                            ("eq", [P, 4, N_SLC, N_SLC]), ("rank", [P, 4, N_SLC]), ("not_sel", [N_SLC, TB]),
                            ("dn_ms", [P, 4, HEADS_B]), ("hg", [P, 4, N_CMP]), ("cbias", [P, HEADS_B, 4, N_CMP]),
                            ("tri", [P, P]), ("neg_ones", [P, P]), ("mask01", [P, P]), ("mask_add", [P, P]),
                            ("cover", [N_CMP, N_SLC]), ("blocks", [N_SLC, TB]), ("imp_scale", [P, 4 * N_SLC]),
                            ("imp_add", [P, 4 * N_SLC]), ("tri8", [P, N_SLC * N_SLC]), ("valid", [P, 4])):
            M[name] = sb(name, shape)
        M["bias_rows"] = nc.dram_tensor("bias_rows", (3 * HEADS_B, ROW_LEN), F32, kind="Internal").ap()
        for name in ("loaded", "multiplied", "copied", "row_out", "strips_in", "one_row", "strip_turned", "strip_placed"):
            M[name] = sem(name + "_b")

        ring = {"tiles": G["ring"], "full": [sem(f"slot{s}_full_b") for s in range(2)],
                "mm_done": signal("mm_done_b", MM_B), "per_layer": SLOTS_B,
                "w_hi": signal("w_hi_b", LOTS_B), "w_lo": signal("w_lo_b", LOTS_B)}
        S = dict(G["consts"])
        S.update(
            psum=G["psum"], rstd=sb("rstd_b", [P, TB]), split_norm={0: 0, 1: 1}, rounded=signal("rounded_b", 2 * KD),
            sq_done=signal("sq_done", 32), sq_high=signal("sq_high", 32), sq_out=signal("sq_out", 2 * (16 + 4)),
            squared=signal("squared_b", 2 * KD), summed=signal("summed_b", 2), rooted=signal("rooted_b", 2),
            rstd_ready=signal("rstd_ready_b", 2), scaled=signal("scaled_b", 2 * KD), cols_in=signal("cols_in_b", 1, 16),
            psum_free=signal("psum_free_b", (16 + 4) + (8 + 4) + 2 * (16 + 4) + 2 * (8 + 2)), tm_free=signal("tm_free", 16 + 8),
            blocks_in=signal("blocks_in", 2), hidden=signal("hidden", 4), projected=signal("projected", 1),
            lam_step=signal("lam_step", 3), inv_step=signal("inv_step", 2 * UNITS_B),
            y_turned=signal("y_turned_b", 8), y_high=signal("y_high_b", 8), y_out=signal("y_out_b", 8),
            sb_z=signal("sb_z", 16), sb_ln=signal("sb_ln", 48), sb_softplus=signal("sb_softplus", 32),
            sb_logit=signal("sb_logit", 16), sb_fenced=signal("sb_fenced", 16), sb_weight=signal("sb_weight", 16),
            sb_mixed=signal("sb_mixed", 4), sb_stored=signal("sb_stored", 4), sb_staged=signal("sb_staged", 2),
            sel_pe=signal("sel_pe", 3), sel_act=signal("sel_act", 1), sel_dve=signal("sel_dve", 7),
            dn_dve=signal("dn_dve", 4), dn_act=signal("dn_act", 2))
        for name in ("scores", "shifted", "probs", "turned", "turned_out", "mixed", "stored", "inverted"):
            S[name] = signal(name + "_b", UNITS_B)

        with ExitStack() as inner:
            local = Scope(nc, inner)
            M["table"], M["rev"] = local.sb("table", [N_BUCKETS + 1, 3 * HEADS_B]), local.sb("rev", [N_BUCKETS + 1, ROW_LEN])
            M["fwd"], M["reverse"] = local.sb("fwd", [N_BUCKETS + 1, 1024]), local.sb("reverse", [P, P])
            M["rows"] = local.sb("rows", [3 * HEADS_B, ROW_LEN])
            bias_setup(nc, S, A, M)

        def unit(name, head, i, q_tile, k, v, y0, k_width=DH, row=None, **more):
            row = DH * (head % 2) if row is None else row
            return {"name": name, "head": head, "i": i, "q": (slice(row, row + k_width), q_tile), "k": k,
                    "v": v, "y": y0 + DH * head, **more}

        heads = [(head, i) for head in range(HEADS_B) for i in range(4)]
        compressed = [unit("compressed", hd, i, T_NSQ + hd // 2, "k_cmp", None, Y_NS, gate=hd) for hd, i in heads]
        selected = [unit("selected", hd, i, T_NSQ + hd // 2, "k_slc", V_SLC, Y_NS, gate=HEADS_B + hd,
                         strip=HEADS_B + hd, onto=0) for hd, i in heads]
        window = [unit("window", hd, i, T_NSQ + hd // 2, "k_win", V_WIN, Y_NS, gate=2 * HEADS_B + hd,
                       strip=HEADS_B + hd, onto=2 * (4 * hd + i) + 1) for hd, i in heads]
        moba = [unit("moba", hd, i, T_MB + 2 * (hd // 2), T_MB + 2 * (hd // 2) + 1, V_MB + DH * hd, Y_MB, strip=hd)
                for hd, i in heads]
        differential = [unit("differential", hd, i, T_DF + 2 * (hd // 2), T_DF + 2 * (hd // 2) + 1, V_DF + DH * hd,
                             Y_DF, k_width=32, row=DH * (hd % 2) + 32 * c, strip=2 * HEADS_B + hd, half=c,
                             **({"onto": 48 + 16 + 2 * (4 * hd + i) + 1} if c else {}))
                        for hd, i in heads for c in range(2)]

        def softmax_pass(layer, base, units):
            fm, v_tm, y_tm = M["fm"], M["v_tm"], M["y_tm"]
            inv_step, inverted, stored = S["inv_step"], S["inverted"], S["stored"]

            def keys(un):
                return (N_CMP, [(0, N_CMP)]) if un["name"] == "compressed" else (P * (un["i"] + 1), Q_TILES_B[:un["i"] + 1])

            def k(un, a, b):
                rows = un["q"][0]
                return M[un["k"]][rows, a:b] if isinstance(un["k"], str) else fm[rows, un["k"], a:b]

            def v(it, un, j, sn):
                return M["v_cmp"][:, :] if un["v"] is None else v_tm[:, j, un["v"]:un["v"] + DH]

            def more(it, un, q0, qn):
                if un["name"] != "selected":
                    return []
                return [(M["not_sel"][:, q0:q0 + qn], lambda a, b: M["blocks"][:, a:b])]

            def bias(un, qn, n):
                return M["cbias"][:, un["head"], un["i"], :] if un["name"] == "compressed" \
                    else strips[:, un["strip"], TB - n:TB]

            def invert(dve, it, un, u, qn, factor, total):
                def after(n):
                    dve.wait_ge(inv_step.sem, inv_step.at(layer, 2 * (base + u) + n))

                nc.vector.tensor_scalar(factor, total, TINY, None, ALU.max).then_inc(inv_step.sem, 1)
                after(1)
                nc.vector.reciprocal(factor, factor).then_inc(inv_step.sem, 1)
                after(2)
                scale = M["valid"][:, un["i"]:un["i"] + 1] if un["name"] == "compressed" \
                    else M["gates"][:, un["i"], un["gate"]:un["gate"] + 1] if "gate" in un \
                    else M["neg_lam"][:, 0:1] if un.get("half") else S["ones"][:, 0:1]
                nc.vector.tensor_tensor(factor, factor, scale, ALU.mult).then_inc(inverted.sem, 1)
                if un["name"] == "compressed":
                    dve.wait_ge(inverted.sem, inverted.at(layer, base + u + 1))
                    acc = M["pc_sum"][:, un["i"], :]
                    nc.vector.scalar_tensor_tensor(out=acc, in0=S["P"][:, u % 4, 0:N_CMP], scalar=factor,
                                                   in1=acc, op0=ALU.mult, op1=ALU.add)

            def finish(dve, it, un, u, q0, qn, product, factor):
                dst = y_tm[:, un["i"], un["y"]:un["y"] + DH]
                if un["name"] == "compressed":
                    return nc.vector.tensor_scalar(dst, product, factor, M["gates"][:, un["i"], un["gate"]:un["gate"] + 1],
                                                   ALU.mult, ALU.mult)
                if "onto" not in un:
                    return nc.vector.tensor_scalar(dst, product, factor, None, ALU.mult)
                if un["onto"]:
                    dve.wait_ge(stored.sem, stored.at(layer, un["onto"]))
                return nc.vector.scalar_tensor_tensor(out=dst, in0=product, scalar=factor, in1=dst,
                                                      op0=ALU.mult, op1=ALU.add)

            softmax_stage(nc, S, layer, {
                "base": base, "rounds": 1, "units": units, "T": TB, "q_tiles": Q_TILES_B, "keys": keys, "stages": [],
                "finish": finish, "invert": invert, "q": lambda un, q0, qn: fm[un["q"][0], un["q"][1], q0:q0 + qn],
                "k": k, "v": v, "more": more, "bias": bias})

        def weight_parts(scope, name):
            hi, lo = scope.parts(name, 2, KD * UNIT)
            return {**ring, "hi": hi, "lo": lo}

        def mixer(layer, scope):
            M["fm"], v_tm, y_tm = scope.sb("fm", [P, 16, TB]), scope.sb("v_tm", [P, 4, 1024]), scope.sb("y_tm", [P, 4, 1024])
            M["v_tm"], M["y_tm"] = v_tm, y_tm

            with nc.Block() as block:
                @block.sync
                def _(sp):
                    sp.dma_start(cols[:, :], A["cols_b"][layer]).then_inc(S["cols_in"].sem, 16)
                    first_slots(sp, ring, lambda j: A["win_b"][layer, j])
                    sp.wait_ge(S["cols_in"].sem, S["cols_in"].at(layer, 1))
                    pass_waits(sp, S)

                @block.tensor
                def _(pe):
                    pe.sem_inc(ring["mm_done"].sem, 2)

            with ExitStack() as inner:
                local = Scope(nc, inner)
                M["u"] = local.parts("u_in_b", KD, TB)
                S["scratch"] = M["fm"]
                norm_stage(nc, S, layer, 0, TB, h, col("attn_g"), M["u"])
                W = weight_parts(local, "w_in_b")
                linear_stage(nc, S, W, layer, TB, lambda j: A["win_b"][layer, j], 8, M["u"], 0, 2, 0, 0,
                             lambda j: A["wv_b"][layer, j], out=M["fm"])
                token_major_stage(nc, S, W, layer, A, M)
            attention = ExitStack()
            local = Scope(nc, attention)
            stage = local.sb("stage_b", [P, 15 * TB])
            M["qs"], M["ks"] = part(stage, 0, TB), part(stage, TB, TB)
            S.update(N=part(stage, 0, 4, TB), P=part(stage, 4 * TB, 4, TB), PT=part(stage, 8 * TB, 2, TB))
            M.update({
                "sb_log": part(stage, 2 * TB, 2, TB),
                "sb_sp": stage[:, 4 * TB:12 * TB].rearrange("p (a b c) -> p a b c", a=2, b=4),
                "sb_w": local.sb("sb_weights", [P, 2, 4, TB]), "pc_turned": stage[0:N_CMP, 0:TB],
                "k_slc": part(stage, 11 * TB, TB), "k_win": part(stage, 12 * TB, TB),
                "dn_sq": stage[:, 13 * TB:15 * TB].rearrange("p (a b c) -> p a b c", a=4, b=HEADS_B)})
            with ExitStack() as inner:
                M["xb"] = Scope(nc, inner).sb("cmp_blocks", [P, 2, 16, N_CMP])
                stick_stage(nc, S, ring, layer, A, M)
            softmax_pass(layer, 0, [un for pair in zip(compressed, moba) for un in pair] + window)
            select_stage(nc, S, layer, M)
            softmax_pass(layer, 48, selected + differential)
            diff_norm_stage(nc, S, layer, M)
            attention.close()
            with ExitStack() as inner:
                local = Scope(nc, inner)
                y_hi, y_lo = local.parts("y_b", KD, TB)
                turn_heads_stage(nc, S, layer, y_tm, y_hi, 8, Q_TILES_B, y_lo)
                linear_stage(nc, S, weight_parts(local, "w_out_b"), layer, TB, lambda j: A["wout_b"][layer, j], 4,
                             (y_hi, y_lo), 16, 54, 24, 20, lambda j: A["wup_b"][layer, j], evacuate="add", out=h)

        def mlp(layer, scope):
            u = scope.parts("u_up_b", KD, TB)
            with ExitStack() as inner:
                S["scratch"] = Scope(nc, inner).sb("squares_b", [P, KD, TB])
                norm_stage(nc, S, layer, 1, TB, h, col("mlp_g"), u)
            hid, W = scope.parts("hid_b", 16, TB), weight_parts(scope, "w_mlp_b")
            relu = scope.sb("rectified", [P, 4, TB])
            for half in range(2):
                S["sq_base"], S["sq_base2"] = 20 * half, 16 * half
                linear_stage(nc, S, W, layer, TB, lambda j: A["wup_b"][layer, j + 8 * half], 8, u, 20 + 16 * half,
                             62 + 32 * half, 32 + 32 * half, 32 + 30 * half,
                             lambda j: A["wdown_b"][layer, j + 8 * half], evacuate="relu2", out=relu, out_parts=hid)
                linear_stage(nc, S, W, layer, TB, lambda j: A["wdown_b"][layer, j + 8 * half], 8, hid, 28 + 16 * half,
                             78 + 32 * half, 48 + 32 * half, 52 + 30 * half,
                             None if half else (lambda j: A["wup_b"][layer, j + 8]), tile_parts=2, evacuate="add", out=h)

        with nc.Fori(0, DEPTH) as layer:
            with ExitStack() as inner:
                mixer(layer, Scope(nc, inner))
            with ExitStack() as inner:
                mlp(layer, Scope(nc, inner))

        final_in, out_done = sem("final_in"), sem("out_done")
        with nc.Block() as block:
            @block.sync
            def _(sp):
                sp.dma_start(cols[:, 0:KD], A["final_g"]).then_inc(final_in, 16)
                sp.wait_ge(final_in, 16)
        result = sb("result", [P, KD, TB])
        S["scratch"] = sb("squares_final", [P, KD, TB])
        norm_stage(nc, S, DEPTH, 0, TB, h, cols[:, 0:KD], result, plain=True)
        with nc.Block() as block:
            @block.sync
            def _(sp):
                sp.dma_start(out, result[:, :, :]).then_inc(out_done, 16)
                sp.wait_ge(out_done, 16)


def constants_b():
    dist = np.arange(-LAST_DIST, TB)
    n = np.maximum(dist, 0)
    exact = N_BUCKETS // 2
    nf = np.maximum(n, 1).astype(np.float32)
    large = exact + (np.log(nf / np.float32(exact)) / np.float32(np.log(128 / exact))
                     * np.float32(N_BUCKETS - exact)).astype(np.int32)
    bucket = np.where(n < exact, n, np.minimum(large, N_BUCKETS - 1))
    fwd = np.zeros((N_BUCKETS + 1, 1024), np.float32)
    for x, (d, b) in enumerate(zip(dist, bucket)):
        fwd[b if d >= 0 else N_BUCKETS, x] = -1.0 if d >= 0 else NEG
    rev = np.zeros((N_BUCKETS + 1, ROW_LEN), np.float32)
    rev[:, 0:639] = fwd[:, 2 * LAST_DIST - np.arange(639)]
    p, c = np.arange(P)[:, None], np.arange(P)[None, :]
    out = {"onehot_fwd": fwd, "reverse": np.eye(P)[::-1], "onehot_rev": rev, "tri": np.where(p >= c, -1, 0), "neg_ones": np.full((P, P), -1),
           "mask01": np.where(c > p, 1, 0), "mask_add": np.where(c > p, 0, -NEG)}
    start, s0 = np.arange(N_CMP) * CMP_STRIDE, np.arange(N_SLC) * SLC_LEN
    lo = np.maximum(start[:, None], s0[None])
    hi = np.minimum(start[:, None] + CMP_LEN - 1, s0[None] + SLC_LEN - 1)
    out["cover"] = np.clip(hi - lo + 1, 0, None) / CMP_LEN
    out["blocks"] = np.kron(np.eye(N_SLC), np.full((1, SLC_LEN), NEG))
    own = (np.arange(TB) // SLC_LEN).reshape(4, P).T[:, :, None]
    j = np.arange(N_SLC)[None, None]
    out["imp_scale"] = (j < own).astype(np.float32).reshape(P, -1)
    out["imp_add"] = np.where(j == own, NEG, np.where(j < own, 0, -NEG)).reshape(P, -1)
    out["tri8"] = np.tile((np.arange(8)[None, :] < np.arange(8)[:, None]).reshape(1, -1), (P, 1))
    valid = np.ones((P, 4))
    valid[:CMP_LEN - 1, 0] = 0
    out["valid"] = valid
    return {k: np.ascontiguousarray(v.astype(np.float32)) for k, v in out.items()}


def pack_b(i):
    w = i["w_in_2"]
    sizes = [256] * 7 + [64] * 6 + [12] + [256] * 3
    at = np.cumsum([0] + sizes)
    (sbq, sbk, sbv, mbq, mbk, mbv, nsq, kc, vc, ks, vs, kw, vw, g, dfq, dfk, dfv) = (
        w[..., a:b] for a, b in zip(at[:-1], at[1:]))
    fm = np.concatenate([interleave(sbq, sbk), interleave(mbq, mbk), interleave(dfq, dfk), nsq, kc, vc, ks, kw], -1)
    pad = np.zeros(g.shape[:2] + (1024 - V_G - 12,), np.float32)
    tm = np.concatenate([sbv, mbv, dfv, vs, vw, g, pad], -1)

    def first_layer(w1):
        return w1.reshape(DEPTH, 2, 8, P, CMP_HID).transpose(0, 1, 3, 2, 4).reshape(DEPTH, 2, P, 8 * CMP_HID)

    def by_tile(v):
        n, k, m = v.shape
        return v.reshape(n, k // P, P, m).transpose(0, 2, 1, 3).reshape(n, P, -1)

    wdown = i["w_down_2"].reshape(DEPTH, 2, 16, P, KD, P).transpose(0, 1, 4, 3, 2, 5).reshape(DEPTH, 2 * KD, P, SLOT)
    pos = np.concatenate([i[n].reshape(DEPTH, 16, 2, DH).transpose(0, 3, 2, 1) for n in ("cmp_pos_k_2", "cmp_pos_v_2")], 1)
    rep = lambda v: np.broadcast_to(v.reshape(DEPTH, 1, -1), (DEPTH, P, v.reshape(DEPTH, -1).shape[1]))
    init = np.array([0.8 - 0.6 * np.exp(-0.3 * l) for l in range(DEPTH)], np.float64)
    w2k = i["cmp_k_w2_2"]
    cols = {"attn_g": feature_columns(i["norm_attn_2"]), "mlp_g": feature_columns(i["norm_mlp_2"]),
            "pos": pos.reshape(DEPTH, P, 32), "w2k": by_tile(np.concatenate([w2k, w2k], -1)),
            "w2v": by_tile(i["cmp_v_w2_2"]), "lambda": rep(i["diff_lambda_2"]),
            "neg_lambda_init": rep((-init).astype(np.float32)), "one_less_init": rep((1 - init).astype(np.float32)),
            "subln": rep(i["diff_subln_2"])}
    return {**constants_b(), "win_b": by_pairs(fm), "wv_b": by_columns(tm),
            "wcmp": np.concatenate([first_layer(i["cmp_k_w1_2"]), first_layer(i["cmp_v_w1_2"])], 1),
            "wout_b": by_pairs(i["w_out_2"]), "wup_b": by_pairs(i["w_up_2"]), "wdown_b": wdown,
            "rel_bias": i["rel_bias_2"], "final_g": np.ascontiguousarray(feature_columns(i["final_norm_2"][None])[0]),
            "cols_b": np.concatenate([cols[n] for n in COLS_B], -1)}


def constants():
    c = {"ident": np.eye(P), "mean_mat": np.full((P, P), 1 / D), "mean256": np.full((P, P), 1 / 256)}
    c["mean64"] = np.kron(np.eye(2), np.full((64, 64), 1 / 64))
    p, col = np.arange(P)[:, None], np.arange(P)[None, :]
    mask = np.zeros((P, TA + META))
    mask[:, TA - P:TA] = np.where(col > p, NEG, 0)
    mask[:, TA:] = np.where(np.arange(META)[None, :] > p, NEG, 0)
    c["mask_a"] = mask
    c["pick_head"] = np.tile(np.eye(HEADS_A), (2, 1))
    return {k: np.ascontiguousarray(v.astype(np.float32)) for k, v in c.items()}


def by_pairs(w):
    n, k, m = w.shape
    w = w.reshape(n, k // P, P, m // (2 * P), 2, P).transpose(0, 3, 2, 4, 1, 5)
    return np.ascontiguousarray(w).reshape(n, m // (2 * P), P, 2 * (k // P) * P)


def by_halves(w):
    n, k, m = w.shape
    w = w.reshape(n, 2, k // (2 * P), P, m // P, P).transpose(0, 4, 1, 3, 2, 5)
    return np.ascontiguousarray(w).reshape(n, 2 * m // P, P, (k // (2 * P)) * P)


def by_columns(w):
    n, k, m = w.shape
    w = w.reshape(n, k // P, P, m // 256, 256).transpose(0, 3, 2, 1, 4)
    return np.ascontiguousarray(w).reshape(n, m // 256, P, (k // P) * 256)


def feature_columns(v):
    return np.ascontiguousarray(v.reshape(v.shape[0], -1, P).transpose(0, 2, 1))


def tap_columns(w):
    n, taps, c = w.shape
    return np.ascontiguousarray(w.reshape(n, taps, c // P, P).transpose(0, 3, 2, 1)).reshape(n, P, -1)


def interleave(a, b):
    n, k, m = a.shape
    return np.stack([a.reshape(n, k, -1, P), b.reshape(n, k, -1, P)], 3).reshape(n, k, 2 * m)


def pack_a(i):
    w = i["w_in"]
    q, k, v = w[..., :512], w[..., 512:1024], w[..., 1024:1536]
    f, rest = w[..., 1536:1544], w[..., 1544:]
    val, gate, sb_, sc_, sx = (rest[..., 256 * n:256 * (n + 1)] for n in range(5))
    fpad = np.concatenate([f, np.zeros(f.shape[:2] + (248,), np.float32)], -1)
    branches = by_pairs(np.concatenate([gate, val, sc_, sx, sb_, fpad], -1))
    out = {"win": np.concatenate([branches, by_pairs(interleave(q, k)), by_columns(v)], 1),
           "wout": by_pairs(i["w_out"]),
           "wup": by_pairs(interleave(i["ffn_w_up"][..., :D_FF], i["ffn_w_up"][..., D_FF:])),
           "wdown": by_halves(i["ffn_w_down"])}
    bf = np.zeros((DEPTH, P, 1), np.float32)
    bf[:, :HEADS_A, 0] = i["b_forget"]
    pw = i["a_pw_w"].reshape(DEPTH, 2, P, 256).transpose(0, 2, 1, 3).reshape(DEPTH, P, 512)
    cols = {"mix_pre": feature_columns(i["mix_pre_g"]), "mix_post": feature_columns(i["mix_post_g"]),
            "ffn_pre": feature_columns(i["ffn_pre_g"]), "ffn_post": feature_columns(i["ffn_post_g"]),
            "head_g": feature_columns(i["head_g"]), "dw_b": feature_columns(i["a_dw_b"]),
            "ln_g": feature_columns(i["a_ln_g"]), "ln_b": feature_columns(i["a_ln_b"]),
            "dw_w": tap_columns(i["a_dw_w"]), "sc_w": tap_columns(i["sc_conv_w"]),
            "ff_w": tap_columns(interleave(i["ffn_conv_w"][..., :D_FF], i["ffn_conv_w"][..., D_FF:])),
            "b_forget": bf, "pw_w": pw}
    out["cols_a"] = np.concatenate([cols[n] for n in COLS_A], -1)
    x = np.concatenate([i["meta_tokens"][None], i["x"]], 1)[0]
    out["x"] = x.T.reshape(KD, P, TA).transpose(1, 0, 2)
    return out


def build(nc, A, out):
    with ExitStack() as ctx:
        def sb(name, shape):
            return ctx.enter_context(nc.sbuf_tensor(name, shape, F32))

        h = sb("h", [P, KD, TA])
        ring = sb("ring", [P, 2, SLOT])
        psum = ctx.enter_context(nc.psum_tensor("psum", [P, 8, 512], F32))
        consts = {n: sb(n, [P, P]) for n in ("ident", "mean_mat", "mean256", "mean64")}
        consts["ones"] = sb("ones", [P, TA])
        consts["eps5"], consts["eps6"] = sb("eps5", [P, 1]), sb("eps6", [P, 1])
        consts["neg_max"], consts["total"] = sb("neg_max", [P, 4]), sb("total", [P, 6])
        consts["factor"] = sb("factor", [P, 4])
        loaded = ctx.enter_context(nc.semaphore("loaded"))
        consts["passed"] = ctx.enter_context(nc.semaphore("passed"))
        G = {"ring": ring, "psum": psum, "consts": consts}
        names = ("ident", "mean_mat", "mean256", "mean64")
        with nc.Block() as block:
            @block.sync
            def _(sp):
                sp.dma_start(h[:, :, :], A["x"]).then_inc(loaded, 16)
                for n in names:
                    sp.dma_start(consts[n][:, :], A[n]).then_inc(loaded, 16)
                sp.wait_ge(loaded, 16 * (1 + len(names)))

            @block.vector
            def _(dve):
                nc.vector.memset(consts["ones"][:, :], 1.0)
                nc.vector.memset(consts["eps5"][:, :], 1e-5)
                nc.vector.memset(consts["eps6"][:, :], 1e-6)
        first_stack(nc, G, A, h)
        second_stack(nc, G, A, h, out)


def kernel(**inputs):
    import concourse.bacc as bacc
    from concourse.bass_utils import run_bass_kernel_spmd

    nc = bacc.Bacc("TRN2", target_bir_lowering=False, num_devices=1)
    inputs = {k: np.ascontiguousarray(v) for k, v in inputs.items()}
    arrays = {**constants(), **pack_a(inputs), **pack_b(inputs)}
    arrays = {f"in_{k}": np.ascontiguousarray(v) for k, v in arrays.items()}
    A = {k[3:]: nc.dram_tensor(k, v.shape, mybir.dt.from_np(v.dtype), kind="ExternalInput").ap()
         for k, v in arrays.items()}
    out = nc.dram_tensor("out", (P, KD, OUT_TOKENS), F32, kind="ExternalOutput").ap()
    build(nc, A, out)
    r = run_bass_kernel_spmd(nc, [arrays], core_ids=[0])
    got = r.results[0]["out"]
    return np.ascontiguousarray(got.transpose(2, 1, 0)).reshape(1, OUT_TOKENS, D)
```
